# Optimizing a Trainium2 kernel written in Bass

```python
import math
import jax
import jax.numpy as jnp
from jax import lax
import numpy as np

D_MODEL = 1024
BATCH = 1
SEQ = 512
DEPTH = 1
DEC_BATCH = 1
DEC_SEQ = 64
PAST_LEN = 512

CHUNK = 64
SB_HEAD_DIM = 64
SB_HEADS = D_MODEL // 128
SB_WIDTH = SB_HEADS * SB_HEAD_DIM
SB_QBLOCK = 128
LRU_WIDTH = D_MODEL // 2
LRU_BLOCKS = 8
LRU_BLOCK_DIM = LRU_WIDTH // LRU_BLOCKS
LRU_C = 8.0
CONV_W = 4
SSM_INNER = D_MODEL // 2
SSM_HEAD_DIM = 64
SSM_HEADS = SSM_INNER // SSM_HEAD_DIM
SSM_GROUPS = 2
SSM_HPG = SSM_HEADS // SSM_GROUPS
SSM_STATE = 128
SSM_CONV_DIM = SSM_INNER + 2 * SSM_GROUPS * SSM_STATE
MIX_WIDTH = SB_WIDTH + LRU_WIDTH + SSM_INNER
N_BRANCH = 3
IN_SPLITS = (SB_WIDTH, 2 * SB_WIDTH, 3 * SB_WIDTH,
             3 * SB_WIDTH + LRU_WIDTH, 3 * SB_WIDTH + 2 * LRU_WIDTH,
             3 * SB_WIDTH + 2 * LRU_WIDTH + SSM_INNER,
             3 * SB_WIDTH + 2 * LRU_WIDTH + SSM_INNER + SSM_CONV_DIM)
IN_PROJ_WIDTH = IN_SPLITS[-1] + SSM_HEADS
N_EXPERT_GROUPS = 4
EXPERTS_PER_GROUP = 8
N_EXPERTS = N_EXPERT_GROUPS * EXPERTS_PER_GROUP
TOP_K = 2
D_EXPERT = D_MODEL // 2
MOE_BLOCK = 128
EPS = 1e-6

kernel_name = 'hybrid_streaming_sb_rglru_ssd_hmoe'

def rmsnorm(x, g):
    x32 = x.astype(jnp.float32)
    y = x32 * lax.rsqrt(jnp.mean(x32 * x32, axis=-1, keepdims=True) + EPS)
    return (y * g.astype(jnp.float32)).astype(x.dtype)

def causal_conv(x, prev, w, b):
    T = x.shape[1]
    xp = jnp.concatenate([prev.astype(x.dtype), x], axis=1)
    y = sum(xp[:, k:k + T] * w[k] for k in range(CONV_W)) + b
    return y, xp[:, -(CONV_W - 1):]

def stick_breaking(q, k, v, q_pos, k_pos):
    z = jnp.einsum('bqhd,bkhd->bhqk', q, k, preferred_element_type=jnp.float32) * (SB_HEAD_DIM ** -0.5)
    mask = k_pos[None, :] < q_pos[:, None]
    log_beta = jax.nn.log_sigmoid(z)
    log_keep = jnp.where(mask, jax.nn.log_sigmoid(-z), 0.0)
    log_after = lax.cumsum(log_keep, axis=3, reverse=True) - log_keep
    w = jnp.where(mask, jnp.exp(log_beta + log_after), 0.0)
    o = jnp.einsum('bhqk,bkhd->bqhd', w, v.astype(jnp.float32))
    return o.astype(q.dtype)

def stick_breaking_prompt(q, k, v):
    B, S, H, Dh = q.shape
    k_pos = jnp.arange(S)

    def block(i):
        start = i * SB_QBLOCK
        qb = lax.dynamic_slice_in_dim(q, start, SB_QBLOCK, axis=1)
        return stick_breaking(qb, k, v, start + jnp.arange(SB_QBLOCK), k_pos)

    o = lax.map(block, jnp.arange(S // SB_QBLOCK))
    return jnp.moveaxis(o, 0, 1).reshape(B, S, H, Dh)

def linear_recurrence(a, b, h0):
    b = b.at[:, 0].add(a[:, 0] * h0)

    def combine(left, right):
        return left[0] * right[0], right[0] * left[1] + right[1]

    _, h = lax.associative_scan(combine, (a, b), axis=1)
    return h

def rglru_branch(x, gate, conv_prev, h0, conv_w, conv_b, w_a, b_a, w_x, b_x, lam):
    B, T, _ = x.shape
    xc, conv_new = causal_conv(x, conv_prev, conv_w, conv_b)
    xc32 = xc.astype(jnp.float32)
    xh = xc32.reshape(B, T, LRU_BLOCKS, LRU_BLOCK_DIM)
    r = jax.nn.sigmoid(jnp.einsum('bthi,hij->bthj', xh, w_a.astype(jnp.float32)).reshape(B, T, LRU_WIDTH) + b_a)
    i = jax.nn.sigmoid(jnp.einsum('bthi,hij->bthj', xh, w_x.astype(jnp.float32)).reshape(B, T, LRU_WIDTH) + b_x)
    log_a = LRU_C * r * jax.nn.log_sigmoid(lam.astype(jnp.float32))
    a = jnp.exp(log_a)
    mult = jnp.sqrt(-jnp.expm1(2.0 * log_a))
    h = linear_recurrence(a, mult * (i * xc32), h0.astype(jnp.float32))
    y = h * jax.nn.gelu(gate.astype(jnp.float32), approximate=True)
    return y.astype(x.dtype), conv_new, h[:, -1]

def ssd_scan(x, dA, Bm, Cm, h0, chunk):
    b, T = x.shape[:2]
    nc = T // chunk
    x = x.reshape(b, nc, chunk, SSM_GROUPS, SSM_HPG, SSM_HEAD_DIM)
    dA = dA.reshape(b, nc, chunk, SSM_GROUPS, SSM_HPG)
    Bm = Bm.reshape(b, nc, chunk, SSM_GROUPS, SSM_STATE)
    Cm = Cm.reshape(b, nc, chunk, SSM_GROUPS, SSM_STATE)
    a_cum = jnp.cumsum(dA, axis=2)
    causal = jnp.tril(jnp.ones((chunk, chunk), bool))[None, None, :, :, None, None]
    seg = a_cum[:, :, :, None] - a_cum[:, :, None, :]
    decay_ls = jnp.exp(jnp.where(causal, seg, -jnp.inf))
    cb = jnp.einsum('bclgn,bcsgn->bclsg', Cm, Bm)
    y_diag = jnp.einsum('bclsg,bclsge,bcsgep->bclgep', cb, decay_ls, x)
    decay_to_end = jnp.exp(a_cum[:, :, -1:] - a_cum)
    chunk_states = jnp.einsum('bclgn,bclge,bclgep->bcgepn', Bm, decay_to_end, x)
    chunk_decay = jnp.exp(a_cum[:, :, -1])

    def step(h, inp):
        d, s = inp
        return d[..., None, None] * h + s, h

    h_last, h_in = lax.scan(step, h0, (jnp.moveaxis(chunk_decay, 1, 0), jnp.moveaxis(chunk_states, 1, 0)))
    h_in = jnp.moveaxis(h_in, 0, 1)
    y_off = jnp.einsum('bclgn,bcgepn,bclge->bclgep', Cm, h_in, jnp.exp(a_cum))
    y = (y_diag + y_off).reshape(b, T, SSM_GROUPS, SSM_HPG, SSM_HEAD_DIM)
    return y, h_last

def ssd_branch(z, xbc, dt_raw, conv_prev, h0, conv_w, conv_b, dt_bias, a_log, d_skip, g_norm):
    B, T, _ = z.shape
    xbc_c, conv_new = causal_conv(xbc, conv_prev, conv_w, conv_b)
    xbc_c = jax.nn.silu(xbc_c.astype(jnp.float32))
    xs, Bm, Cm = jnp.split(xbc_c, [SSM_INNER, SSM_INNER + SSM_GROUPS * SSM_STATE], axis=-1)
    xs = xs.reshape(B, T, SSM_GROUPS, SSM_HPG, SSM_HEAD_DIM)
    Bm = Bm.reshape(B, T, SSM_GROUPS, SSM_STATE)
    Cm = Cm.reshape(B, T, SSM_GROUPS, SSM_STATE)
    dt = jax.nn.softplus(dt_raw.astype(jnp.float32) + dt_bias).reshape(B, T, SSM_GROUPS, SSM_HPG)
    A = -jnp.exp(a_log.astype(jnp.float32)).reshape(SSM_GROUPS, SSM_HPG)
    chunk = CHUNK if T % CHUNK == 0 else T
    h0 = h0.astype(jnp.float32).reshape(B, SSM_GROUPS, SSM_HPG, SSM_HEAD_DIM, SSM_STATE)
    y, h_last = ssd_scan(xs * dt[..., None], dt * A, Bm, Cm, h0, chunk)
    y = y + d_skip.astype(jnp.float32).reshape(SSM_GROUPS, SSM_HPG, 1) * xs
    y = y.reshape(B, T, SSM_GROUPS, SSM_HPG * SSM_HEAD_DIM) * jax.nn.silu(
        z.astype(jnp.float32).reshape(B, T, SSM_GROUPS, SSM_HPG * SSM_HEAD_DIM))
    y = y * lax.rsqrt(jnp.mean(y * y, axis=-1, keepdims=True) + EPS) * g_norm.astype(jnp.float32).reshape(SSM_GROUPS, -1)
    return (y.reshape(B, T, SSM_INNER).astype(z.dtype), conv_new,
            h_last.reshape(B, SSM_HEADS, SSM_HEAD_DIM, SSM_STATE))

def hier_moe(u, w_rg, b_rg, w_re, b_re, w_eg, w_eu, w_ed):
    lead = u.shape[:-1]
    uf = u.reshape(-1, D_MODEL)
    T = uf.shape[0]
    g_logits = (uf @ w_rg + b_rg).astype(jnp.float32)
    p_group = jax.nn.softmax(g_logits, axis=-1)
    g_sel = jnp.argmax(g_logits, axis=-1)
    e_logits = (uf @ w_re + b_re).astype(jnp.float32).reshape(T, N_EXPERT_GROUPS, EXPERTS_PER_GROUP)
    e_in = jnp.take_along_axis(e_logits, g_sel[:, None, None], axis=1)[:, 0]
    top_v, top_i = lax.top_k(e_in, TOP_K)
    gate = jax.nn.softmax(top_v, axis=-1) * jnp.take_along_axis(p_group, g_sel[:, None], axis=1)
    e_flat = (g_sel[:, None] * EXPERTS_PER_GROUP + top_i).reshape(-1)
    w_flat = gate.reshape(-1)
    tok_flat = jnp.repeat(jnp.arange(T), TOP_K)
    order = jnp.argsort(e_flat)
    e_s, tok_s, w_s = e_flat[order], tok_flat[order], w_flat[order]
    counts = jnp.bincount(e_flat, length=N_EXPERTS)
    starts = jnp.cumsum(counts) - counts
    padded = ((counts + MOE_BLOCK - 1) // MOE_BLOCK) * MOE_BLOCK
    pad_ends = jnp.cumsum(padded)
    pad_starts = pad_ends - padded
    n_assign = T * TOP_K
    dest = pad_starts[e_s] + (jnp.arange(n_assign) - starts[e_s])
    n_blocks = -(-n_assign // MOE_BLOCK) + N_EXPERTS
    cap = n_blocks * MOE_BLOCK
    x_buf = jnp.zeros((cap, D_MODEL), uf.dtype).at[dest].set(uf[tok_s])
    w_buf = jnp.zeros((cap,), jnp.float32).at[dest].set(w_s)
    t_buf = jnp.zeros((cap,), jnp.int32).at[dest].set(tok_s.astype(jnp.int32))
    blk_expert = jnp.minimum(jnp.searchsorted(pad_ends, jnp.arange(n_blocks) * MOE_BLOCK, side='right'),
                             N_EXPERTS - 1)

    def run_block(args):
        xb, e = args
        return (jax.nn.silu(xb @ w_eg[e]) * (xb @ w_eu[e])) @ w_ed[e]

    y_buf = lax.map(run_block, (x_buf.reshape(n_blocks, MOE_BLOCK, D_MODEL), blk_expert)).reshape(cap, D_MODEL)
    out = jnp.zeros((T, D_MODEL), jnp.float32).at[t_buf].add(y_buf.astype(jnp.float32) * w_buf[:, None])
    return out.reshape(*lead, D_MODEL).astype(u.dtype)

def token_mixers(u, lp, past):
    B, T, _ = u.shape
    proj = u @ lp['w_in']
    q, k, v, xb, gb, zc, xbc, dtr = jnp.split(proj, IN_SPLITS, axis=-1)
    head_shape = (B, T, SB_HEADS, SB_HEAD_DIM)
    q, k, v = q.reshape(head_shape), k.reshape(head_shape), v.reshape(head_shape)
    if past is None:
        o_a = stick_breaking_prompt(q, k, v)
        lru_conv0 = jnp.zeros((B, CONV_W - 1, LRU_WIDTH), u.dtype)
        lru_h0 = jnp.zeros((B, LRU_WIDTH), jnp.float32)
        ssm_conv0 = jnp.zeros((B, CONV_W - 1, SSM_CONV_DIM), u.dtype)
        ssm_h0 = jnp.zeros((B, SSM_HEADS, SSM_HEAD_DIM, SSM_STATE), jnp.float32)
    else:
        k_past, v_past, lru_conv0, lru_h0, ssm_conv0, ssm_h0 = past
        P = k_past.shape[1]
        k_all = jnp.concatenate([k_past.astype(k.dtype), k], axis=1)
        v_all = jnp.concatenate([v_past.astype(v.dtype), v], axis=1)
        o_a = stick_breaking(q, k_all, v_all, P + jnp.arange(T), jnp.arange(P + T))
    o_a = o_a.reshape(B, T, SB_WIDTH)
    o_b, lru_conv1, lru_h1 = rglru_branch(xb, gb, lru_conv0, lru_h0, lp['lru_conv_w'], lp['lru_conv_b'],
                                          lp['lru_w_a'], lp['lru_b_a'], lp['lru_w_x'], lp['lru_b_x'],
                                          lp['lru_lambda'])
    o_c, ssm_conv1, ssm_h1 = ssd_branch(zc, xbc, dtr, ssm_conv0, ssm_h0, lp['ssm_conv_w'], lp['ssm_conv_b'],
                                        lp['ssm_dt_bias'], lp['ssm_a_log'], lp['ssm_d'], lp['ssm_norm_g'])
    gates = jax.nn.sigmoid(u @ lp['w_gate'] + lp['b_gate']).reshape(B, T, N_BRANCH, D_MODEL)
    wbo = lp['w_branch_out']
    merged = (gates[:, :, 0] * (o_a @ wbo[:SB_WIDTH])
              + gates[:, :, 1] * (o_b @ wbo[SB_WIDTH:SB_WIDTH + LRU_WIDTH])
              + gates[:, :, 2] * (o_c @ wbo[SB_WIDTH + LRU_WIDTH:]))
    return merged @ lp['w_out'], (k, v, lru_conv1, lru_h1, ssm_conv1, ssm_h1)

def run_trunk(x, layer_params, g_final, past):
    h = x
    per_layer = []
    for l in range(DEPTH):
        lp = {name: arr[l] for name, arr in layer_params.items()}
        layer_past = None if past is None else tuple(p[l] for p in past)
        mix, st = token_mixers(rmsnorm(h, lp['g_mix']), lp, layer_past)
        h = h + mix
        h = h + hier_moe(rmsnorm(h, lp['g_ffn']), lp['w_router_group'], lp['b_router_group'],
                         lp['w_router_expert'], lp['b_router_expert'],
                         lp['w_expert_gate'], lp['w_expert_up'], lp['w_expert_down'])
        per_layer.append(st)
    new_states = tuple(jnp.stack([s[i] for s in per_layer], axis=0) for i in range(6))
    return rmsnorm(h, g_final), new_states

def setup_inputs(seed: int = 0) -> dict:
    key = jax.random.key(seed)
    keys = iter(jax.random.split(key, 48))

    def nrm(shape, scale):
        return jax.random.normal(next(keys), shape, jnp.float32) * scale

    L = DEPTH
    x_prompt = nrm((BATCH, SEQ, D_MODEL), 1.0)
    x_sample = nrm((DEC_BATCH, DEC_SEQ, D_MODEL), 1.0)
    cache_sb_k = nrm((L, DEC_BATCH, PAST_LEN, SB_HEADS, SB_HEAD_DIM), 1.0)
    cache_sb_v = nrm((L, DEC_BATCH, PAST_LEN, SB_HEADS, SB_HEAD_DIM), 1.0)
    state_lru_conv = nrm((L, DEC_BATCH, CONV_W - 1, LRU_WIDTH), 1.0)
    state_lru_h = nrm((L, DEC_BATCH, LRU_WIDTH), 0.5)
    state_ssm_conv = nrm((L, DEC_BATCH, CONV_W - 1, SSM_CONV_DIM), 1.0)
    state_ssm_h = nrm((L, DEC_BATCH, SSM_HEADS, SSM_HEAD_DIM, SSM_STATE), 0.1)
    g_mix = 1.0 + nrm((L, D_MODEL), 0.02)
    w_in = nrm((L, D_MODEL, IN_PROJ_WIDTH), D_MODEL ** -0.5)
    w_gate = nrm((L, D_MODEL, N_BRANCH * D_MODEL), D_MODEL ** -0.5)
    b_gate = nrm((L, N_BRANCH * D_MODEL), 0.02)
    w_branch_out = nrm((L, MIX_WIDTH, D_MODEL), (MIX_WIDTH // N_BRANCH) ** -0.5)
    w_out = nrm((L, D_MODEL, D_MODEL), D_MODEL ** -0.5)
    lru_conv_w = nrm((L, CONV_W, LRU_WIDTH), CONV_W ** -0.5)
    lru_conv_b = nrm((L, LRU_WIDTH), 0.02)
    lru_w_a = nrm((L, LRU_BLOCKS, LRU_BLOCK_DIM, LRU_BLOCK_DIM), LRU_BLOCK_DIM ** -0.5)
    lru_b_a = nrm((L, LRU_WIDTH), 0.02)
    lru_w_x = nrm((L, LRU_BLOCKS, LRU_BLOCK_DIM, LRU_BLOCK_DIM), LRU_BLOCK_DIM ** -0.5)
    lru_b_x = nrm((L, LRU_WIDTH), 0.02)
    a0 = jax.random.uniform(next(keys), (L, LRU_WIDTH), jnp.float32, minval=0.9, maxval=0.999)
    lru_lambda = jnp.log(a0) - jnp.log1p(-a0)
    ssm_conv_w = nrm((L, CONV_W, SSM_CONV_DIM), CONV_W ** -0.5)
    ssm_conv_b = nrm((L, SSM_CONV_DIM), 0.02)
    dt0 = jnp.exp(jax.random.uniform(next(keys), (L, SSM_HEADS), jnp.float32,
                                     minval=math.log(1e-3), maxval=math.log(1e-1)))
    ssm_dt_bias = dt0 + jnp.log(-jnp.expm1(-dt0))
    ssm_a_log = jnp.log(jax.random.uniform(next(keys), (L, SSM_HEADS), jnp.float32, minval=1.0, maxval=16.0))
    ssm_d = 1.0 + nrm((L, SSM_HEADS), 0.1)
    ssm_norm_g = 1.0 + nrm((L, SSM_INNER), 0.02)
    g_ffn = 1.0 + nrm((L, D_MODEL), 0.02)
    w_router_group = nrm((L, D_MODEL, N_EXPERT_GROUPS), D_MODEL ** -0.5)
    b_router_group = nrm((L, N_EXPERT_GROUPS), 0.01)
    w_router_expert = nrm((L, D_MODEL, N_EXPERTS), D_MODEL ** -0.5)
    b_router_expert = nrm((L, N_EXPERTS), 0.01)
    w_expert_gate = nrm((L, N_EXPERTS, D_MODEL, D_EXPERT), D_MODEL ** -0.5)
    w_expert_up = nrm((L, N_EXPERTS, D_MODEL, D_EXPERT), D_MODEL ** -0.5)
    w_expert_down = nrm((L, N_EXPERTS, D_EXPERT, D_MODEL), D_EXPERT ** -0.5)
    g_final = 1.0 + nrm((D_MODEL,), 0.02)
    return {'x_prompt': x_prompt, 'x_sample': x_sample,
            'cache_sb_k': cache_sb_k, 'cache_sb_v': cache_sb_v,
            'state_lru_conv': state_lru_conv, 'state_lru_h': state_lru_h,
            'state_ssm_conv': state_ssm_conv, 'state_ssm_h': state_ssm_h,
            'g_mix': g_mix, 'w_in': w_in, 'w_gate': w_gate, 'b_gate': b_gate,
            'w_branch_out': w_branch_out, 'w_out': w_out,
            'lru_conv_w': lru_conv_w, 'lru_conv_b': lru_conv_b, 'lru_w_a': lru_w_a, 'lru_b_a': lru_b_a,
            'lru_w_x': lru_w_x, 'lru_b_x': lru_b_x, 'lru_lambda': lru_lambda,
            'ssm_conv_w': ssm_conv_w, 'ssm_conv_b': ssm_conv_b, 'ssm_dt_bias': ssm_dt_bias,
            'ssm_a_log': ssm_a_log, 'ssm_d': ssm_d, 'ssm_norm_g': ssm_norm_g,
            'g_ffn': g_ffn, 'w_router_group': w_router_group, 'b_router_group': b_router_group,
            'w_router_expert': w_router_expert, 'b_router_expert': b_router_expert,
            'w_expert_gate': w_expert_gate, 'w_expert_up': w_expert_up, 'w_expert_down': w_expert_down,
            'g_final': g_final}

def reference(x_prompt, x_sample, cache_sb_k, cache_sb_v, state_lru_conv, state_lru_h, state_ssm_conv,
              state_ssm_h, g_mix, w_in, w_gate, b_gate, w_branch_out, w_out, lru_conv_w, lru_conv_b,
              lru_w_a, lru_b_a, lru_w_x, lru_b_x, lru_lambda, ssm_conv_w, ssm_conv_b, ssm_dt_bias,
              ssm_a_log, ssm_d, ssm_norm_g, g_ffn, w_router_group, b_router_group, w_router_expert,
              b_router_expert, w_expert_gate, w_expert_up, w_expert_down, g_final):
    layer_params = {'g_mix': g_mix, 'w_in': w_in, 'w_gate': w_gate, 'b_gate': b_gate,
                    'w_branch_out': w_branch_out, 'w_out': w_out,
                    'lru_conv_w': lru_conv_w, 'lru_conv_b': lru_conv_b, 'lru_w_a': lru_w_a, 'lru_b_a': lru_b_a,
                    'lru_w_x': lru_w_x, 'lru_b_x': lru_b_x, 'lru_lambda': lru_lambda,
                    'ssm_conv_w': ssm_conv_w, 'ssm_conv_b': ssm_conv_b, 'ssm_dt_bias': ssm_dt_bias,
                    'ssm_a_log': ssm_a_log, 'ssm_d': ssm_d, 'ssm_norm_g': ssm_norm_g,
                    'g_ffn': g_ffn, 'w_router_group': w_router_group, 'b_router_group': b_router_group,
                    'w_router_expert': w_router_expert, 'b_router_expert': b_router_expert,
                    'w_expert_gate': w_expert_gate, 'w_expert_up': w_expert_up, 'w_expert_down': w_expert_down}
    y_prompt, (kp, vp, lcp, lhp, scp, shp) = run_trunk(x_prompt, layer_params, g_final, None)
    y_sample, (ks, vs, lcs, lhs, scs, shs) = run_trunk(
        x_sample, layer_params, g_final,
        (cache_sb_k, cache_sb_v, state_lru_conv, state_lru_h, state_ssm_conv, state_ssm_h))
    return (y_prompt, y_sample, kp, vp, lcp, lhp, scp, shp, ks, vs, lcs, lhs, scs, shs)


_drawn_inputs = setup_inputs


def setup_inputs(seed=0):
    import zlib

    import numpy as np

    out = dict(_drawn_inputs(seed))
    spreads = {}
    factors = {'cache_sb_k': 3.729,
     'b_gate': 2.887,
     'lru_b_a': 8.0,
     'lru_b_x': 6.125,
     'ssm_norm_g': 2.745,
     'b_router_group': 3.46,
     'b_router_expert': 12.326,
     'g_final': 8.641,
     'g_ffn': 2.958}
    for name, (base, spread) in spreads.items():
        noise = np.random.default_rng([zlib.crc32(name.encode()), seed]).standard_normal(out[name].shape)
        drawn = base * np.exp(spread * noise) if base else spread * noise
        out[name] = jnp.asarray(drawn.astype(out[name].dtype))
    for name, factor in factors.items():
        out[name] = (out[name] * factor).astype(out[name].dtype)
    return out
```

```python
from contextlib import ExitStack

import concourse.bass as bass
from concourse import mybir

F32 = mybir.dt.float32
I32 = mybir.dt.int32
U32 = mybir.dt.uint32
ALU = mybir.AluOpType
ACT = mybir.ActivationFunctionType
AXX = mybir.AxisListType.X

P = 128
D = 1024
SEQ = 512
DEC = 64
PAST = 512
T = SEQ + DEC
HALF = T // 2
KD = D // P
TT = [(t * P, P) for t in range(SEQ // P)] + [(SEQ, DEC)]
NT = len(TT)
HEADS = 8
HD = 64
PAIRS = HEADS // 2
KB = SEQ // P
W = 512
WT = W // P
STATE = 128
GROUPS = 2
XBC = W + 2 * GROUPS * STATE
XT = XBC // P
CW = 4
GAP = CW - 1
TW = SEQ + GAP + DEC + 1
SAMP = SEQ + GAP
XP = TW + GAP
EPS = 1e-6
NEG = -1.0e30
BIG = 3.0e38
GELU_C = 0.7978845608028654
GELU_A = 0.044715

NG = 4
EPG = 8
NE = NG * EPG
DE = D // 2
BLK = 64
NA = T * 2
OVB = NA // (BLK + 1) + 1
OVB += OVB % 2
EPAIRS = NE // 2
OPAIRS = OVB // 2
NPC = EPAIRS + OPAIRS

PAR_ROWS = [("g_mix", 8), ("b_gate", 24), ("lru_conv_w", 16), ("lru_conv_b", 4), ("ssm_conv_w", 32),
            ("ssm_conv_b", 8), ("lru_b_a", 4), ("lru_b_x", 4), ("lru_lambda", 4), ("ssm_norm_g", 4),
            ("state_lru_h", 4)]
PAR = {}
_n = 0
for _name, _k in PAR_ROWS:
    PAR[_name] = _n
    _n += _k
NPAR = _n
NST = 36
TAILS = 80
SMALL = 960
ROUND = 12582912.0

UNITS = ([("in", 0 * 256 + 256 * i) for i in range(6)]
         + [("in", 3072 + 256 * i) for i in range(4)]
         + [("in", 1536 + 256 * i) for i in range(4)]
         + [("in", 2560 + 256 * i) for i in range(2)])
for _b in range(3):
    UNITS += [("gate", _b * D), ("branch", _b, 0), ("gate", _b * D + 256),
              ("gate", _b * D + 512), ("branch", _b, 1), ("gate", _b * D + 768)]
UNITS += [("out", 256 * i) for i in range(4)]
NSLOT = 4

ITEMS = []
for _c in range(WT):
    ITEMS += [("q", _c, h, _c // 2, _c % 2) for h in range(2)]
for _c in range(WT):
    ITEMS += [("k", _c, h, 2 + _c // 2, _c % 2) for h in range(2)]
for _u in range(2):
    ITEMS += [("v", _u, t, 4 + _u, 0) for t in range(NT)]
ITEMS += [("dt", 0, h, None, 0) for h in range(2)]
MIX0 = len(ITEMS)
for _c in range(XT):
    ITEMS += [("x", _c, h, 6 + _c // 2, _c % 2) for h in range(2)]
for _c in range(WT):
    ITEMS += [("r", _c, h, 10 + _c // 2, _c % 2) for h in range(2)]
for _c in range(WT):
    ITEMS += [("gb", _c, h, 12 + _c // 2, _c % 2) for h in range(2)]
for _u in range(2):
    ITEMS += [("z", _u, t, 14 + _u, 0) for t in range(NT)]
MIX1 = len(ITEMS)
for _b in range(3):
    for _c in range(KD):
        for _h in range(2):
            _base = 16 + 6 * _b
            _g = _base + [0, 2, 3, 5][_c // 2]
            ITEMS += [("g", _c, _h, _g, _c % 2, _b), ("b", _c, _h, _base + [1, 4][_c // 4], _c % 4, _b)]
OUT0 = len(ITEMS)
for _t in range(NT):
    ITEMS += [("o", _t, q, 34 + q, 0) for q in range(4)]
DVE_KINDS = ("k", "b", "o")
IDX = {}
for _i, _it in enumerate(ITEMS):
    IDX[(_it[0],) + _it[1:3] + _it[5:]] = _i
LAST_OF = {}
for _i, _it in enumerate(ITEMS):
    LAST_OF[_it[3]] = _i
DRAINED = []
_cnt = [0, 0]
for _it in ITEMS:
    _e = 1 if _it[0] in DVE_KINDS else 0
    _cnt[_e] += 1
    DRAINED.append((_e, _cnt[_e]))

ATT = [("p", hp, kb) for hp in range(PAIRS) for kb in reversed(range(KB))]
ATT += [("d", 0, kb) for kb in reversed(range(PAST // P + 1))]
NATT = len(ATT)


def att_at(u):
    return (3 * u) // 2


JOBS = {}


def job(item, *what):
    JOBS.setdefault(item, []).append(what)


_v0 = IDX[("v", 0, 0)]
for _i in range(4):
    job(_v0 + 1 + _i, "past_keys", _i)
for _i in range(NT):
    job(_v0 + 5 + _i, "keys_out", _i)
job(MIX0, "dt_turn", 0)
for _s in range(MIX1 - MIX0):
    for _u in range(NATT):
        if att_at(_u) + 3 == _s:
            job(MIX0 + _s, "att_values", _u)
    for _u in range(NATT):
        if att_at(_u) + 2 == _s:
            job(MIX0 + _s, "att_after", _u)
    for _u in range(NATT):
        if att_at(_u) == _s:
            job(MIX0 + _s, "att_scores", _u)
for _c in range(XT):
    job(IDX[("x", _c, 1)] + 1, "conv", _c)
for _c in range(WT):
    job(IDX[("r", _c, 1)] + 1, "conv", XT + _c)
for _u in range(NATT):
    job(MIX0 + att_at(_u), "att_soft", _u)


def mix3(s):
    return MIX1 + 2 * s


job(mix3(1), "state_in", 0)
for _i in range(XT):
    job(mix3(_i // 4), "silu", _i)
for _t in range(NT):
    job(mix3(2 + _t // 2), "ssm_turn", _t)
for _c in range(WT):
    job(mix3(4 + 2 * _c), "lru", _c)
for _c in range(NT):
    job(mix3(11 + 4 * _c), "ssd_decay", _c)
    job(mix3(13 + 4 * _c), "ssd_mix", _c)
    job(mix3(15 + 4 * _c), "ssd_turn", _c)
job(mix3(13), "tails_turn", 0)
job(mix3(26), "state_out", 0)
job(mix3(30), "state_out", 1)
for _t in range(NT):
    job(OUT0 + 4 * (_t + 1), "ffn_norm", _t)
    job(OUT0 + 4 * (_t + 1) + 2, "ffn_turn", _t)
NITEM = len(ITEMS)
for _i, _j in [(k, v) for k, v in JOBS.items() if k > NITEM]:
    JOBS.setdefault(NITEM, []).extend(_j)
    del JOBS[_i]


def trunk_and_experts(nc, a, o):
    ctx = ExitStack()
    with ctx:
        def sb(name, shape, dt=F32):
            return ctx.enter_context(nc.sbuf_tensor(name, shape, dt))

        def ps(name, shape):
            return ctx.enter_context(nc.psum_tensor(name, shape, F32))

        def sem(name):
            return ctx.enter_context(nc.semaphore(name))

        arena = sb("arena", [P, 52608])
        cut = [0]

        def take(n):
            cut[0] += n
            assert cut[0] <= 52608, cut[0]
            return cut[0] - n

        def at(off, *dims):
            n = 1
            for d in dims:
                n *= d
            v = arena[:, off:off + n]
            if len(dims) == 2:
                v = v.rearrange("p (a b) -> p a b", a=dims[0])
            if len(dims) == 3:
                v = v.rearrange("p (a b c) -> p a b c", a=dims[0], b=dims[1])
            return v

        ident, u_incl, u_strict, neg_l, neg_ones, ones, att_mask, ssd_mask = (
            at(take(P), P) for _ in range(8))
        cpar = at(take(NPAR), NPAR)
        cst = at(take(NST), NST)
        rowc = at(take(60), 60)
        tails = at(take(TAILS), TAILS)
        small = take(SMALL)
        w_dt = at(take(KD * 8), KD, 8)
        h_off = take(NT * D)
        h = at(h_off, NT, D)
        merged_off = take(KD * T)
        merged = at(merged_off, KD, T)
        ring_off = take(NSLOT * 2048)
        ring8 = [at(ring_off + 2048 * s, KD, 256) for s in range(NSLOT)]
        ring4 = [at(ring_off + 2048 * s, WT, 512) for s in range(NSLOT)]
        front = cut[0]
        uT = at(take(KD * T), KD, T)
        q2_off = take(2 * PAIRS * T)
        q2 = at(q2_off, 2, PAIRS, T)
        oAT = at(q2_off, PAIRS, T)
        oBT = at(q2_off + PAIRS * T, PAIRS, T)
        xconv_off = take(XT * TW)
        xconv = at(xconv_off, XT, TW)
        oCT = at(xconv_off, WT, T)
        xc = at(take(WT * TW), WT, TW)
        gb = at(take(WT * TW), WT, TW)
        z2 = at(take(NT * W), NT, W)
        tmp = cut[0]
        kT = at(take(PAIRS * T), PAIRS, T)
        kpT = at(take(PAIRS * PAST), PAIRS, PAST)
        att_a = [at(take(1024), 2, 512) for _ in range(2)]
        att_b = [at(take(1024), 2, 512) for _ in range(2)]
        att_s = at(take(1024), 2, 512)
        xp_off = [take(584) for _ in range(2)]
        xp = [at(x, 584) for x in xp_off]
        v_sb = at(merged_off, NT, W)
        vp_sb = at(merged_off + NT * W, KB, W)
        kp_raw = at(xconv_off, KB, W)
        st_a = at(xconv_off + 2048, P)
        st_b = at(xconv_off + 2048 + P, P)
        junk = at(xconv_off + 2048 + 2 * P, D)
        ko = [at(h_off + 512 * i, W) for i in range(2)]
        dtT = at(h_off + 1024, T)
        cut[0] = tmp
        xs_tok = at(take(NT * W), NT, W)
        b_tok = at(take(NT * 256), NT, 256)
        xdt = at(take(W), HEADS, HD)
        xdd = at(take(W), HEADS, HD)
        y_off_sb = at(take(W), W)
        y_sb = at(take(W), W)
        lt = [at(take(TW), TW) for _ in range(5)]
        gsb = [at(take(HALF), HALF) for _ in range(2)]
        gtmp = [at(take(HALF), HALF) for _ in range(2)]
        lru_w = at(take(8 * P), 2, WT, P)
        e_off = h_off
        th = [at(e_off + TW * i, TW) for i in range(2)]
        e_flat = e_off
        m_flat = e_off + 1024
        td_flat = e_off + 2048
        hT = at(e_off + 3072, W)
        hS = at(e_off + 3584, W)
        ss_in = at(e_off + 4096, WT, P)
        tz = at(e_off + 4608, W)
        h_out = at(td_flat, WT, P)
        tail_row = lt[3][:, 0:P]

        wexp_off = front
        w_g = at(wexp_off, 2 * KD, DE)
        w_u = at(wexp_off + 8192, 2 * KD, DE)
        w_d = at(wexp_off + 16384, 2 * (DE // P), D)
        cut[0] = front + 24576
        u2 = [at(take(D), D) for _ in range(2)]
        u2T = [at(take(D), KD, P) for _ in range(2)]
        g_ffn = at(take(D), D)
        w_r = at(take(KD * 36), KD, 36)
        lg = at(take(NT * 36), NT, 36)
        v_top = [at(take(NT), NT) for _ in range(2)]
        rank_full = at(take(NT * NE), NT, NE)
        e_masked = at(take(NT * NE), NT, NE)
        e_cand = at(take(NT * NE), NT, NE)
        e_hot = [at(take(NT * NE), NT, NE) for _ in range(2)]
        hot_sum = at(take(NT * NE), NT, NE)
        g_cand = at(take(NT * NG), NT, NG)
        g_hot = at(take(NT * NG), NT, NG)
        g_max, g_key, e_key, p_sel = (at(take(NT), NT) for _ in range(4))
        for_exp = at(take(NT * NG + NT), NT * NG + NT)
        tile_base = at(take((NT + 1) * NE), NT + 1, NE)
        n_over, over_incl, over_start = (at(take(NE), NE) for _ in range(3))
        rank, first, expert, blk_no, place, col, side, is_over, div = (at(take(2 * NT), 2, NT) for _ in range(9))
        eid = at(take(OVB), OVB)
        cut[0] = merged_off
        xg = at(take(D), D)
        xT = at(take(D), KD, P)
        hidT = at(take(DE), DE // P, P)
        gate_t = at(take(DE), DE)
        gate_a = at(take(DE), DE)
        hid = at(take(DE), DE)
        y_out_sb = at(take(D), D)
        y_back = [[at(take(D), D) for _ in range(2)] for _ in range(2)]
        g_fin = at(take(D), D)
        over_cmp = at(take(OVB * NE), OVB, NE)
        assert cut[0] <= front

        cs = [small]

        def tiny(*dims):
            n = 1
            for d in dims:
                n *= d
            cs[0] += n
            assert cs[0] <= small + SMALL
            return at(cs[0] - n, *dims)

        ssq = tiny(8)
        rstd = tiny(8)
        sp_x, sp_e, sp_u, sp_l, sp_m, sp_p = (tiny(44) for _ in range(6))
        dt_sb = sp_x[:, 0:40].rearrange("p (t h) -> p t h", t=NT)
        a_exp = tiny(8)
        dA = tiny(NT, 8)
        ls4 = tiny(WT)
        ls4n = tiny(WT)
        acs = tiny(8)
        ea = tiny(8)
        cd = tiny(8)
        ssy = tiny(2)
        rsy = tiny(2)
        ss2 = tiny(8)
        rs2 = tiny(8)

        w_sel = tiny(2, NT)
        ss3 = tiny(8)
        rs3 = tiny(8)
        rev = tiny(NE)
        iota_f = tiny(NE)
        tok_id = tiny(NT).bitcast(I32)
        iota_i = tiny(NE).bitcast(I32)
        no_token = tiny(NPC).bitcast(I32)
        tab = tiny(NPC).bitcast(I32)
        idx_now = tiny(1).bitcast(I32)
        tab_row = tiny(2 * NT).bitcast(I32)
        y_row = tiny(2 * NT).bitcast(I32)
        over_total = tiny(1).bitcast(I32)
        over_expert = tiny(OVB).bitcast(I32)
        assert cs[0] <= small + SMALL

        pj = ps("pj", [P, 2, 512])
        za = ps("za", [P, 2, 512])
        zb = ps("zb", [P, 2, 512])
        zz = [za, zb]
        oa = ps("oa", [P, 512])
        ms = ps("ms", [P, 512])

        u2d = nc.dram_tensor("u2d", (T, D), F32, kind="Internal").ap()
        tabd = nc.dram_tensor("tabd", (P * NPC, 1), I32, kind="Internal").ap()
        yd = nc.dram_tensor("yd", ((NE + OVB) * BLK, D), F32, kind="Internal").ap()

        names = """consts par_in bc_in kp_in vp_in wdt_in par_up par_half ssq_r var_r std_r xn_r
            pe_par xt_ps ut_r pj_full pj_act pj_dve kp_ps kp_r ko_ps ko_r dt_ps dt_raw
            sp_na sp_eo sp_uo sp_lo dt_r z_r nab_r ln_e l_r sp_r zw_r s_sum w_r_ o_r o_out q_zero masked
            conv_c silu_t silu_r turn_ps turn_r lruw_in lruw_z lru_ps lru_tr lru_ac lru_g2 lru_g3 lru_gt
            lru_ib lru_a2 lru_m2 lru_mu lru_h ob_r ssin_in hs_ps hs_r
            td_r dec_ps acs_r d_r ea_r em_r e_r m_r xdt_r xdd_r tz_r mix_ps hcd_r h_r y0_r y1_r y2_r yg_r
            ssy_r vy_r sy_r yn_r yt_ps oc_r so_ps so_r so_out v_out tl_out tl_ps tl_r gm_r
            x2_in gains_in wr_in u2_a u2_r u2t_ps u2t_r lg_ps lg_r
            ids_r tab_moved yd_zero tab_out fexp_in fexp_r hots_r rank_ps rows_r over_r
            idx_r idx_seen xg_in xt2_ps xt2_a xt2_d wg_in wu_in wd_in gate_done up_done gate_th gate_mul hid_r hidt_ps hidt_r
            down_a down_b y_a y_b y_out experts_done hy_r fin_r fin_out
            dve_c pool_c""".split()
        S = {n: sem(n) for n in names}
        x_in = [sem(f"x_in{t}") for t in range(NT)]
        back_in = [sem(f"back_in{s}") for s in range(2)]
        ko_out = [sem(f"ko_out{s}") for s in range(2)]
        u2_out = [sem(f"u2_out{s}") for s in range(2)]
        unit_in = [sem(f"unit_in{s}") for s in range(NSLOT)]

        def drained(n):
            e, v = DRAINED[n]
            return S["pj_act"] if e == 0 else S["pj_dve"], v

        def wait_drained(eng, n):
            s, v = drained(n)
            eng.wait_ge(s, v)

        def rows(ap, lo, n):
            return ap.rearrange("l (r p) -> (l r) p", p=P)[lo:lo + n, :]

        def att_view(buf, u):
            kind, hp, kb = ATT[u]
            if kind == "p":
                return buf[:, :, 0:SEQ - kb * P]
            return buf[0:P if kb < KB else DEC, 0, :]

        def tw_cols(t):
            o0, n = TT[t]
            lo = o0 if t < NT - 1 else SAMP
            return lo, n

        block = ctx.enter_context(nc.Block())

        @block.sync
        def _(sp):
            for t, (o0, n) in enumerate(TT):
                src = a["x_prompt"][0, o0:o0 + n, :] if t < NT - 1 else a["x_sample"][0]
                sp.dma_start(h[0:n, t, :], src).then_inc(x_in[t], 16)
                if t == 0:
                    sp.dma_start(w_dt, a["w_in"][0, :, 4096:4104].rearrange("(k p) n -> p k n", p=P)
                                 ).then_inc(S["wdt_in"], 16)
            for u, unit in enumerate(UNITS):
                if u == 2:
                    sp.dma_start(kp_raw, a["cache_sb_k"][0, 0].rearrange("(b p) h d -> p b (h d)", p=P)
                                 ).then_inc(S["kp_in"], 16)
                if u == 4:
                    sp.dma_start(vp_sb, a["cache_sb_v"][0, 0].rearrange("(b p) h d -> p b (h d)", p=P)
                                 ).then_inc(S["vp_in"], 16)
                if u == 34:
                    sp.wait_ge(S["oc_r"], NT)
                    sp.wait_ge(S["so_out"], 32)
                    for t, (o0, n) in enumerate(TT):
                        src = a["x_prompt"][0, o0:o0 + n, :] if t < NT - 1 else a["x_sample"][0]
                        sp.dma_start(h[0:n, t, :], src).then_inc(S["x2_in"], 16)
                if u >= NSLOT:
                    sp.wait_ge(S["pj_full"], LAST_OF[u - NSLOT] + 1)
                if unit[0] == "branch":
                    src = a["w_branch_out"][0, unit[1] * W:(unit[1] + 1) * W, 512 * unit[2]:512 * unit[2] + 512]
                    dst = ring4[u % NSLOT]
                else:
                    w = a[{"in": "w_in", "gate": "w_gate", "out": "w_out"}[unit[0]]]
                    src = w[0, :, unit[1]:unit[1] + 256]
                    dst = ring8[u % NSLOT]
                sp.dma_start(dst, src.rearrange("(k p) n -> p k n", p=P)).then_inc(unit_in[u % NSLOT], 16)
            def load_experts(i, first, second):
                for j, w in enumerate((first, second)):
                    if j == 0 and i is not None:
                        sp.wait_ge(S["gate_done"], i)
                    sp.dma_start(w_g[:, KD * j:KD * (j + 1), :], expert_w("w_expert_gate", w)).then_inc(S["wg_in"], 16)
                for j, w in enumerate((first, second)):
                    if j == 0 and i is not None:
                        sp.wait_ge(S["up_done"], i)
                    sp.dma_start(w_u[:, KD * j:KD * (j + 1), :], expert_w("w_expert_up", w)).then_inc(S["wu_in"], 16)
                for j, w in enumerate((first, second)):
                    if j == 0 and i is not None:
                        sp.wait_ge(S["down_b"], i)
                    sp.dma_start(w_d[:, DE // P * j:DE // P * (j + 1), :], expert_w("w_expert_down", w)
                                 ).then_inc(S["wd_in"], 16)

            def expert_w(name, e):
                rows_e = D if name != "w_expert_down" else DE
                v = a[name][0].rearrange("e (k p) f -> p (e k) f", p=P)
                k = rows_e // P
                return v[:, bass.ds(e * k, k), :]

            def store_y(i):
                sp.wait_ge(S["y_a"], i + 1)
                sp.wait_ge(S["y_b"], i + 1)
                sp.dma_start(yd[bass.ds(i * P, P), :], y_out_sb).then_inc(S["y_out"], 16)

            sp.wait_ge(S["gm_r"], 4 * KD)
            load_experts(None, 0, EPAIRS)
            with sp.Fori(0, EPAIRS - 1) as i:
                load_experts(i + 1, i + 1, i + 1 + EPAIRS)
                store_y(i)
            store_y(EPAIRS - 1)
            sp.wait_ge(S["y_out"], 16 * EPAIRS)
            sp.wait_ge(S["over_r"], 1)
            total = sp.value_load(over_total[0:1, 0:1], min_val=0, max_val=OVB)
            for j in range(OPAIRS):
                with sp.If(total > j):
                    ids = [sp.value_load(over_expert[0:1, c:c + 1], min_val=0, max_val=NE - 1)
                           for c in (j, j + OPAIRS)]
                    load_experts(EPAIRS + j, *ids)
                    store_y(EPAIRS + j)
                    sp.wait_ge(S["y_out"], 16 * (EPAIRS + j + 1))
            sp.sem_inc(S["experts_done"], 1)
            sp.wait_ge(S["fin_out"], 16 * NT)
            for name, n in (("v_out", 2), ("tl_out", 6), ("so_out", 2)):
                sp.wait_ge(S[name], 16 * n)
            for s in range(2):
                sp.wait_ge(ko_out[s], 16 * ((NT + 1 - s) // 2))
                sp.wait_ge(u2_out[s], 16 * ((NT + 1 - s) // 2))

        @block.tensor
        def _(pe):
            def par_turn():
                pe.wait_ge(S["consts"], 8)
                pe.wait_ge(S["par_in"], 16 * (len(PAR_ROWS) + 2))
                pe.transpose(ms[:, 0:NPAR], st_a[0:NPAR, :], ident[0:NPAR, 0:NPAR])
                pe.transpose(oa[:, 0:NST], st_b[0:NST, :], ident[0:NST, 0:NST]).then_inc(S["pe_par"], 1)

            def x_turn(t):
                n = TT[t][1]
                z = zz[t % 2]
                pe.wait_ge(S["xn_r"], t + 1)
                if t >= 2:
                    pe.wait_ge(S["ut_r"], t - 1)
                for k in range(KD):
                    m = pe.transpose(z[:, k // 4, (k % 4) * P:(k % 4) * P + n], h[0:n, t, k * P:(k + 1) * P],
                                     ident[0:n, 0:n])
                m.then_inc(S["xt_ps"], 1)

            def item(n):
                it = ITEMS[n]
                kind, c, hh, u, ct = it[:5]
                if n >= 2:
                    wait_drained(pe, n - 2)
                if u is not None:
                    pe.wait_ge(unit_in[u % NSLOT], 16 * (u // NSLOT + 1))
                cols = slice(hh * HALF, (hh + 1) * HALF)
                bank = pj[:, n % 2, :]
                if kind == "b":
                    br = it[5]
                    if hh == 0 and c == 0:
                        pe.wait_ge(*[(S["o_out"], PAIRS + 1), (S["ob_r"], WT), (S["oc_r"], NT)][br])
                    src = [oAT, oBT, oCT][br]
                    for k in range(WT):
                        m = pe.matmul(bank[:, 0:HALF], ring4[u % NSLOT][:, k, ct * P:(ct + 1) * P],
                                      src[:, k, cols], start=k == 0, stop=k == WT - 1)
                elif kind in "vzo":
                    t, part = (c, hh) if kind == "o" else (hh, c)
                    o0, rows_n = TT[t]
                    if kind == "o" and n == OUT0:
                        pe.wait_ge(S["gm_r"], 32)
                    src = merged if kind == "o" else uT
                    for k in range(KD):
                        m = pe.matmul(bank[0:rows_n, 0:256], src[:, k, o0:o0 + rows_n], ring8[u % NSLOT][:, k, :],
                                      start=k == 0, stop=k == KD - 1)
                elif kind == "dt":
                    if hh == 0:
                        pe.wait_ge(S["wdt_in"], 16)
                    for k in range(KD):
                        m = pe.matmul(bank[0:8, 0:HALF], w_dt[:, k, :], uT[:, k, cols],
                                      start=k == 0, stop=k == KD - 1)
                else:
                    for k in range(KD):
                        m = pe.matmul(bank[:, 0:HALF], ring8[u % NSLOT][:, k, ct * P:(ct + 1) * P],
                                      uT[:, k, cols], start=k == 0, stop=k == KD - 1)
                m.then_inc(S["pj_full"], 1)

            def past_keys(i):
                if i == 0:
                    pe.wait_ge(S["kp_in"], 16)
                    pe.wait_ge(S["ut_r"], NT)
                z = zz[i // 2]
                for b in range(KB):
                    m = pe.transpose(z[:, i % 2, b * P:(b + 1) * P], kp_raw[:, b, i * P:(i + 1) * P], ident)
                m.then_inc(S["kp_ps"], 1)

            def keys_out(t):
                o0, n = TT[t]
                z = [oa, ms][t % 2]
                if t == 0:
                    pe.wait_ge(S["par_up"], 2)
                    wait_drained(pe, IDX[("k", WT - 1, 1)])
                if t >= 2:
                    pe.wait_ge(S["ko_r"], t - 1)
                for c in range(WT):
                    m = pe.transpose(z[0:n, c * P:(c + 1) * P], kT[:, c, o0:o0 + n], ident)
                m.then_inc(S["ko_ps"], 1)

            def dt_turn(_):
                wait_drained(pe, IDX[("dt", 0, 1)])
                pe.wait_ge(S["ko_r"], NT)
                for t, (o0, n) in enumerate(TT):
                    m = pe.transpose(ms[0:n, t * 8:t * 8 + 8], dtT[0:8, o0:o0 + n], ident[0:8, 0:8])
                m.then_inc(S["dt_ps"], 1)

            def att_scores(u):
                kind, hp, kb = ATT[u]
                z = zz[u % 2]
                if u == 0:
                    wait_drained(pe, IDX[("q", WT - 1, 1)])
                    wait_drained(pe, IDX[("k", WT - 1, 1)])
                    pe.wait_ge(S["q_zero"], 1)
                    pe.wait_ge(S["kp_r"], 4)
                if u >= 2:
                    pe.wait_ge(S["w_r_"], u - 1)
                if kind == "p":
                    q0 = kb * P
                    for e in range(2):
                        m = pe.matmul(z[:, e, 0:SEQ - q0], kT[:, hp, q0:q0 + P], q2[:, e, hp, q0:SEQ],
                                      start=True, stop=False, skip_group_check=True)
                else:
                    n = P if kb < KB else DEC
                    for c in range(PAIRS):
                        key = kpT[:, c, kb * P:(kb + 1) * P] if kb < KB else kT[:, c, SEQ:T]
                        m = pe.matmul(z[0:n, 0, c * P:(c + 1) * P], key, q2[:, :, c, SEQ:T],
                                      start=c == 0, stop=False, skip_group_check=True)
                m.then_inc(S["z_r"], 1)

            def att_after(u):
                kind, hp, kb = ATT[u]
                z = zz[u % 2]
                pe.wait_ge(S["sp_r"], u + 1)
                first = kb == (KB - 1 if kind == "p" else KB)
                if not first or kind == "d":
                    pe.wait_ge(S["s_sum"], u)
                b = att_b[u % 2]
                sums = att_s
                if kind == "p":
                    n = SEQ - kb * P
                    for e in range(2):
                        if not first:
                            pe.matmul(z[:, e, P:n], neg_ones, sums[:, e, 0:n - P],
                                      start=False, stop=False, skip_group_check=True)
                        m = pe.matmul(z[:, e, 0:n], neg_l, b[:, e, 0:n],
                                      start=False, stop=True, skip_group_check=True)
                else:
                    n = P if kb < KB else DEC
                    if not first:
                        pe.matmul(z[:, 0, :], neg_ones, sums[:, 0, :], start=False, stop=False,
                                  skip_group_check=True)
                    m = pe.matmul(z[0:n, 0, :], neg_l[0:n, 0:n], b[0:n, 0, :], start=False, stop=True,
                                  skip_group_check=True)
                m.then_inc(S["zw_r"], 1)

            def att_values(u):
                kind, hp, kb = ATT[u]
                w = att_a[u % 2]
                if u == 0:
                    wait_drained(pe, IDX[("v", 1, NT - 1)])
                    pe.wait_ge(S["vp_in"], 16)
                    pe.wait_ge(S["ko_r"], NT)
                pe.wait_ge(S["w_r_"], u + 1)
                if kind == "p":
                    q0 = kb * P
                    if kb == KB - 1 and hp > 0:
                        pe.wait_ge(S["o_out"], hp)
                    for e in range(2):
                        c0 = (2 * hp + e) * HD
                        m = pe.matmul(oa[e * HD:(e + 1) * HD, q0:SEQ], v_sb[:, kb, c0:c0 + HD],
                                      w[:, e, 0:SEQ - q0], start=kb == KB - 1, stop=kb == 0,
                                      skip_group_check=True)
                else:
                    if kb == KB:
                        pe.wait_ge(S["o_out"], PAIRS)
                    n = P if kb < KB else DEC
                    for c in range(PAIRS):
                        for e in range(2):
                            c0 = (2 * c + e) * HD
                            v = vp_sb[:, kb, c0:c0 + HD] if kb < KB else v_sb[0:n, kb, c0:c0 + HD]
                            w0 = c * P + e * HD
                            m = pe.matmul(oa[e * HD:(e + 1) * HD, c * HD:(c + 1) * HD], v,
                                          w[0:n, 0, w0:w0 + HD], start=kb == KB and c == 0, stop=kb == 0,
                                          skip_group_check=True)
                m.then_inc(S["o_r"], 1)

            def state_in(_):
                pe.wait_ge(S["ssin_in"], 16)
                pe.wait_ge(S["dt_raw"], 1)
                for j in range(WT):
                    m = pe.transpose(ms[:, j * P:(j + 1) * P], ss_in[:, j, :], ident)
                m.then_inc(S["hs_ps"], 1)

            def ssm_turn(t):
                lo, n = tw_cols(t)
                if t == 0:
                    pe.wait_ge(S["silu_r"], XT)
                    pe.wait_ge(S["hs_r"], 1)
                    pe.wait_ge(S["o_out"], PAIRS + 1)
                else:
                    pe.wait_ge(S["turn_r"], 2 * t)
                for j in range(6):
                    z = ms if j < WT else oa
                    m = pe.transpose(z[0:n, (j % WT) * P:(j % WT + 1) * P], xconv[:, j, lo:lo + n], ident)
                m.then_inc(S["turn_ps"], 1)

            def lru(c):
                if c == 0:
                    pe.wait_ge(S["lruw_in"], 16 * 2 * HEADS)
                    pe.wait_ge(S["conv_c"], XT + WT)
                else:
                    pe.wait_ge(S["lru_tr"], 2 * c)
                for g in range(2):
                    for hh in range(2):
                        m = pe.matmul(zz[g][:, hh, 0:TW // 2], lru_w[:, g, c, :],
                                      xc[:, c, hh * (TW // 2):(hh + 1) * (TW // 2)], start=True, stop=True)
                m.then_inc(S["lru_ps"], 1)

            def ssd_decay(c):
                o0, n = TT[c]
                pe.wait_ge(S["td_r"], c + 1)
                if c == 0:
                    pe.wait_ge(S["lru_tr"], 2 * WT)
                else:
                    pe.wait_ge(S["m_r"], c)
                    pe.wait_ge(S["ea_r"], c)
                td = at(td_flat, HEADS, n)
                if n == P:
                    for b in range(2):
                        pe.matmul(za[:, b, :], ones[0:n, :], td[0:n, b * 4:(b + 1) * 4, :], start=True, stop=True)
                else:
                    pe.matmul(za[:, 0, :], ones[0:n, :], td[0:n, :, :], start=True, stop=True)
                pe.matmul(zb[0:n, 0, 256:264], u_incl[0:n, 0:n], dA[0:n, c, :], start=True, stop=True)
                lo, _ = tw_cols(c)
                for g in range(GROUPS):
                    m = pe.matmul(zb[0:n, 0, g * n:(g + 1) * n], xconv[:, 4 + g, lo:lo + n],
                                  xconv[:, 6 + g, lo:lo + n], start=True, stop=True)
                m.then_inc(S["dec_ps"], 1)

            def ssd_mix(c):
                o0, n = TT[c]
                lo, _ = tw_cols(c)
                pe.wait_ge(S["m_r"], c + 1)
                pe.wait_ge(S["xdd_r"], c + 1)
                if c == 0:
                    pe.wait_ge(S["turn_r"], 2 * NT)
                else:
                    pe.wait_ge(S["h_r"], c)
                    pe.wait_ge(S["oc_r"], c)
                    if c == NT - 1:
                        pe.wait_ge(S["so_r"], 1)
                m_sb = at(m_flat, HEADS, n)
                for hd in range(HEADS):
                    pe.matmul(zb[0:n, 1, hd * HD:(hd + 1) * HD], m_sb[0:n, hd, :], xdt[0:n, hd, :],
                              start=True, stop=True)
                if c > 0:
                    state = hT if c < NT - 1 else hS
                    for g in range(GROUPS):
                        pe.matmul(oa[0:n, g * 256:(g + 1) * 256], xconv[:, 6 + g, lo:lo + n],
                                  state[:, g * 256:(g + 1) * 256], start=True, stop=True)
                for g in range(GROUPS):
                    m = pe.matmul(ms[:, g * 256:(g + 1) * 256], b_tok[0:n, c, g * P:(g + 1) * P],
                                  xdd[0:n, 4 * g:4 * g + 4, :], start=True, stop=True)
                m.then_inc(S["mix_ps"], 1)

            def ssd_turn(c):
                o0, n = TT[c]
                pe.wait_ge(S["yn_r"], c + 1)
                if c == 0:
                    pe.wait_ge(S["tl_r"], 1)
                for j in range(WT):
                    m = pe.transpose(oa[:, j * P:j * P + n], y_sb[0:n, j * P:(j + 1) * P], ident[0:n, 0:n])
                m.then_inc(S["yt_ps"], 1)

            def tails_turn(_):
                pe.wait_ge(S["lru_h"], 2 * WT)
                pe.wait_ge(S["turn_r"], 2 * NT)
                pe.transpose(oa[0:TAILS, 0:P], tails, ident).then_inc(S["tl_ps"], 1)

            def state_out(i):
                pe.wait_ge(S["h_r"], NT - 1 + i)
                state = [hT, hS][i]
                for j in range(WT):
                    m = pe.transpose(ms[:, j * P:(j + 1) * P], state[:, j * P:(j + 1) * P], ident)
                m.then_inc(S["so_ps"], 1)

            def ffn_turn(t):
                o0, n = TT[t]
                z = zz[t % 2]
                pe.wait_ge(S["u2_r"], t + 1)
                if t >= 2:
                    pe.wait_ge(S["u2t_r"], t - 1)
                for k in range(KD):
                    m = pe.transpose(z[:, k // 4, (k % 4) * P:(k % 4) * P + n], u2[t % 2][0:n, k * P:(k + 1) * P],
                                     ident[0:n, 0:n])
                m.then_inc(S["u2t_ps"], 1)
                if t == 0:
                    pe.wait_ge(S["wr_in"], 32)
                    pe.wait_ge(S["so_r"], 2)
                pe.wait_ge(S["u2t_r"], t + 1)
                for k in range(KD):
                    m = pe.matmul(ms[0:n, t * 36:(t + 1) * 36], u2T[t % 2][:, k, 0:n], w_r[:, k, :],
                                  start=k == 0, stop=k == KD - 1)
                m.then_inc(S["lg_ps"], 1)

            def expert_pair(i, before=True):
                pe.wait_ge(S["xg_in"], (i + 1) * 16)
                if before:
                    pe.wait_ge(S["hidt_r"], i)
                for k in range(KD):
                    z = oa if k < KD // 2 else ms
                    m = pe.transpose(z[:, (k % 4) * P:(k % 4 + 1) * P], xg[:, k * P:(k + 1) * P], ident)
                m.then_inc(S["xt2_ps"], 1)
                pe.wait_ge(S["xt2_a"], i + 1)
                pe.wait_ge(S["xt2_d"], i + 1)
                for b, (w, loaded, done) in enumerate(((w_g, "wg_in", "gate_done"), (w_u, "wu_in", "up_done"))):
                    pe.wait_ge(S[loaded], (i + 1) * 32)
                    for k in range(KD):
                        for j in range(2):
                            m = pe.matmul(za[j * BLK:(j + 1) * BLK, b, :], xT[:, k, j * BLK:(j + 1) * BLK],
                                          w[:, j * KD + k, :], start=k == 0, stop=k == KD - 1)
                    m.then_inc(S[done], 1)
                pe.wait_ge(S["hid_r"], i + 1)
                for k in range(DE // P):
                    m = pe.transpose(oa[:, k * P:(k + 1) * P], hid[:, k * P:(k + 1) * P], ident)
                m.then_inc(S["hidt_ps"], 1)
                pe.wait_ge(S["hidt_r"], i + 1)
                pe.wait_ge(S["wd_in"], (i + 1) * 32)
                for q, (done, free) in enumerate((("down_a", "y_a"), ("down_b", "y_b"))):
                    if before:
                        pe.wait_ge(S[free], i)
                    for k in range(DE // P):
                        for j in range(2):
                            m = pe.matmul(zb[j * BLK:(j + 1) * BLK, q, :], hidT[:, k, j * BLK:(j + 1) * BLK],
                                          w_d[:, j * (DE // P) + k, q * 512:(q + 1) * 512],
                                          start=k == 0, stop=k == DE // P - 1)
                    m.then_inc(S[done], 1)

            def ranks():
                pe.wait_ge(S["hots_r"], 1)
                pe.matmul(ms[:, 0:NT * NE], u_strict, hot_sum, start=True, stop=True)
                pe.matmul(ms[:, NT * NE:2 * NT * NE], ones, hot_sum, start=True, stop=True
                          ).then_inc(S["rank_ps"], 1)

            steps = {f.__name__: f for f in (past_keys, keys_out, dt_turn, att_scores, att_after, att_values,
                                             state_in, ssm_turn, lru, ssd_decay, ssd_mix, ssd_turn, tails_turn,
                                             state_out, ffn_turn)}
            par_turn()
            for t in range(NT):
                x_turn(t)
            pe.wait_ge(S["ut_r"], NT)
            for n in range(NITEM + 1):
                for name, i in JOBS.get(n, []):
                    if name in steps:
                        steps[name](i)
                if n < NITEM:
                    item(n)
            ranks()
            expert_pair(0, before=False)
            with pe.Fori(1, EPAIRS) as i:
                expert_pair(i)
            pe.wait_ge(S["over_r"], 1)
            total = pe.value_load(over_total[0:1, 0:1], min_val=0, max_val=OVB)
            for j in range(OPAIRS):
                with pe.If(total > j):
                    expert_pair(EPAIRS + j)

        @block.scalar
        def _(act):
            lo = 0
            for name, k in PAR_ROWS:
                src = a[name][0]
                if len(src.shape) == 1:
                    src = src.rearrange("(r p) -> r p", p=P)
                elif len(src.shape) == 2:
                    src = src.rearrange("k (r p) -> (k r) p", p=P)
                act.dma_start(st_a[lo:lo + k, :], src).then_inc(S["par_in"], 16)
                lo += k
            act.dma_start(st_b[0:12, :], a["state_lru_conv"][0, 0].rearrange("k (r p) -> (k r) p", p=P)
                          ).then_inc(S["par_in"], 16)
            act.dma_start(st_b[12:36, :], a["state_ssm_conv"][0, 0].rearrange("k (r p) -> (k r) p", p=P)
                          ).then_inc(S["par_in"], 16)
            for lo, n, name in ((0, 8, "ssm_dt_bias"), (8, 8, "ssm_a_log"), (16, 8, "ssm_d"),
                                (24, 4, "b_router_group"), (28, 32, "b_router_expert")):
                act.dma_start(rowc[:, lo:lo + n], a[name][0:1, :].partition_broadcast(P)
                              ).then_inc(S["bc_in"], 16)

            def x_norm(t):
                n = TT[t][1]
                act.wait_ge(x_in[t], 16)
                act.activation(junk[0:n, :], h[0:n, t, :], ACT.Square, accum_out=ssq[0:n, t:t + 1]
                               ).then_inc(S["ssq_r"], 1)
                act.wait_ge(S["var_r"], t + 1)
                act.activation(rstd[0:n, t:t + 1], ssq[0:n, t:t + 1], ACT.Sqrt).then_inc(S["std_r"], 1)

            def par_up():
                act.wait_ge(S["pe_par"], 1)
                act.activation(cpar, ms[:, 0:NPAR], ACT.Copy).then_inc(S["par_up"], 1)
                act.activation(cst, oa[:, 0:NST], ACT.Copy).then_inc(S["par_up"], 1)

            def item(n):
                it = ITEMS[n]
                kind, c, hh = it[:3]
                if kind in DVE_KINDS:
                    return
                act.wait_ge(S["pj_full"], n + 1)
                bank = pj[:, n % 2, :]
                lo = hh * HALF
                if kind == "q":
                    if n == 0:
                        act.wait_ge(S["q_zero"], 1)
                    act.activation(q2[0:HD, 0, c, lo:lo + HALF], bank[0:HD, 0:HALF], ACT.Copy, scale=HD ** -0.5)
                    m = act.activation(q2[HD:P, 1, c, lo:lo + HALF], bank[HD:P, 0:HALF], ACT.Copy,
                                       scale=HD ** -0.5)
                elif kind in "vz":
                    t, r = hh, TT[hh][1]
                    dst = v_sb if kind == "v" else z2
                    m = act.activation(dst[0:r, t, 256 * c:256 * (c + 1)], bank[0:r, 0:256], ACT.Copy,
                                       scale=1.0 if kind == "v" else 0.5)
                elif kind == "dt":
                    if hh == 0:
                        act.wait_ge(S["xt_ps"], NT)
                    m = act.activation(dtT[0:8, lo:lo + HALF], bank[0:8, 0:HALF], ACT.Copy)
                elif kind in ("x", "r"):
                    j = c + (XT if kind == "r" else 0)
                    dst = xp[j % 2]
                    if j < 2 and hh == 0:
                        act.wait_ge(S["masked"], 1)
                    if j >= 2 and hh == 0:
                        act.wait_ge(S["conv_c"], j - 1)
                    if hh == 0:
                        m = act.activation(dst[:, GAP:GAP + HALF], bank[:, 0:HALF], ACT.Copy)
                    else:
                        act.activation(dst[:, GAP + HALF:GAP + SEQ], bank[:, 0:SEQ - HALF], ACT.Copy)
                        m = act.activation(dst[:, SAMP + GAP:SAMP + GAP + DEC], bank[:, SEQ - HALF:HALF], ACT.Copy)
                elif kind == "gb":
                    if hh == 0:
                        m = act.activation(gb[:, c, 0:HALF], bank[:, 0:HALF], ACT.Copy)
                    else:
                        act.activation(gb[:, c, HALF:SEQ], bank[:, 0:SEQ - HALF], ACT.Copy)
                        m = act.activation(gb[:, c, SAMP:SAMP + DEC], bank[:, SEQ - HALF:HALF], ACT.Copy)
                elif kind == "g":
                    br = it[5]
                    k = (n - MIX1) // 2
                    if k == 0:
                        act.wait_ge(S["conv_c"], XT + WT)
                        act.wait_ge(S["s_sum"], NATT)
                    if k >= 2:
                        wait_drained(act, n - 3)
                    j = PAR["b_gate"] + br * KD + c
                    m = act.activation(gsb[k % 2], bank[:, 0:HALF], ACT.Tanh, scale=0.5, bias=cpar[:, j:j + 1])
                m.then_inc(S["pj_act"], 1)
                if n == IDX[("v", 1, NT - 1)]:
                    act.wait_ge(*drained(n))
                    act.dma_start(o["v_p"][0, 0].rearrange("(t p) h d -> p t (h d)", p=P),
                                  v_sb[:, 0:NT - 1, :]).then_inc(S["v_out"], 16)
                    act.dma_start(o["v_s"][0, 0].rearrange("s h d -> s (h d)"),
                                  v_sb[0:DEC, NT - 1, :]).then_inc(S["v_out"], 16)

            def keys_out(t):
                o0, n = TT[t]
                act.wait_ge(S["ko_ps"], t + 1)
                if t == 0:
                    act.wait_ge(S["xt_ps"], NT)
                if t >= 2:
                    act.wait_ge(ko_out[t % 2], 16 * (t // 2))
                act.activation(ko[t % 2][0:n, :], [oa, ms][t % 2][0:n, :], ACT.Copy).then_inc(S["ko_r"], 1)
                act.wait_ge(S["ko_r"], t + 1)
                dst = o["k_p"][0, 0, o0:o0 + n] if t < NT - 1 else o["k_s"][0, 0]
                act.dma_start(dst.rearrange("s h d -> s (h d)"), ko[t % 2][0:n, :]).then_inc(ko_out[t % 2], 16)

            def dt_turn(_):
                act.wait_ge(S["sp_na"], 1)
                act.activation(sp_e, sp_e, ACT.Exp).then_inc(S["sp_eo"], 1)
                act.activation(a_exp, rowc[:, 8:16], ACT.Exp).then_inc(S["sp_eo"], 1)
                act.wait_ge(S["sp_uo"], 1)
                act.activation(sp_l, sp_u, ACT.Ln).then_inc(S["sp_lo"], 1)

            def att_scores(u):
                b = att_view(att_a[u % 2], u)
                act.wait_ge(S["nab_r"], u + 1)
                act.activation(b, b, ACT.Exp).then_inc(S["ln_e"], 1)
                act.wait_ge(S["ln_e"], u + 1)
                act.activation(b, b, ACT.Ln, bias=1.0).then_inc(S["l_r"], 1)

            def att_after(u):
                act.wait_ge(S["zw_r"], u + 1)
                act.activation(att_view(att_a[u % 2], u), att_view(zz[u % 2], u), ACT.Exp).then_inc(S["w_r_"], 1)

            def att_values(u):
                kind, hp, kb = ATT[u]
                if kb == 0:
                    act.wait_ge(S["o_r"], u + 1)
                    if kind == "p":
                        act.activation(oAT[:, hp, 0:SEQ], oa[:, :], ACT.Copy).then_inc(S["o_out"], 1)
                    else:
                        act.activation(oAT[:, :, SEQ:T], oa[:, 0:PAIRS * HD].rearrange("p (c q) -> p c q", c=PAIRS),
                                       ACT.Copy).then_inc(S["o_out"], 1)

            def silu(i):
                if i == 0:
                    act.wait_ge(ko_out[0], 16 * 3)
                    act.wait_ge(ko_out[1], 16 * 2)
                    act.wait_ge(S["dt_r"], 1)
                if i >= 2:
                    act.wait_ge(S["silu_r"], i - 1)
                act.wait_ge(S["conv_c"], i + 1)
                act.activation(th[i % 2], xconv[:, i, :], ACT.Tanh).then_inc(S["silu_t"], 1)

            def state_in(_):
                act.wait_ge(S["hs_ps"], 1)
                act.activation(hS, ms[:, :], ACT.Copy).then_inc(S["hs_r"], 1)

            def ssm_turn(t):
                n = TT[t][1]
                act.wait_ge(S["turn_ps"], t + 1)
                act.activation(b_tok[0:n, t, :], oa[0:n, 0:256], ACT.Copy).then_inc(S["turn_r"], 1)

            def both(z):
                return z[:, :, 0:TW // 2]

            def lru(c):
                r, i, la, m, gl = [x.rearrange("p (a b) -> p a b", a=2) for x in lt]
                act.wait_ge(S["lru_ps"], c + 1)
                if c > 0:
                    act.wait_ge(S["ob_r"], c)
                ba = PAR["lru_b_a"] + c
                bx = PAR["lru_b_x"] + c
                act.activation(r, both(za), ACT.Tanh, scale=0.5, bias=cpar[:, ba:ba + 1]).then_inc(S["lru_tr"], 1)
                act.activation(i, both(zb), ACT.Tanh, scale=0.5, bias=cpar[:, bx:bx + 1]).then_inc(S["lru_tr"], 1)
                act.wait_ge(S["lru_tr"], 2 * c + 2)
                act.activation(la, r, ACT.Exp, scale=ls4[:, c:c + 1], bias=ls4[:, c:c + 1]
                               ).then_inc(S["lru_ac"], 1)
                act.activation(r, r, ACT.Tanh, scale=ls4n[:, c:c + 1], bias=ls4n[:, c:c + 1]
                               ).then_inc(S["lru_ac"], 1)
                act.wait_ge(S["lru_g3"], c + 1)
                act.activation(gl, gl, ACT.Tanh, scale=GELU_C).then_inc(S["lru_gt"], 1)
                act.wait_ge(S["lru_m2"], c + 1)
                act.activation(r, m, ACT.Sqrt).then_inc(S["lru_mu"], 1)

            def ssd_decay(c):
                n = TT[c][1]
                act.wait_ge(S["acs_r"], c + 1)
                act.activation(ea[0:n, :], acs[0:n, :], ACT.Exp)
                act.wait_ge(S["d_r"], c + 1)
                if c > 1:
                    act.wait_ge(S["hcd_r"], c - 1)
                last = za[:, :, :].rearrange("p a (b l) -> p (a b) l", l=P)[:, :, P - 1] if n == P else \
                    za[:, 0, :].rearrange("p (b l) -> p b l", l=n)[:, :, n - 1]
                act.activation(cd, last, ACT.Exp).then_inc(S["ea_r"], 1)
                act.wait_ge(S["em_r"], c + 1)
                e = at(e_flat, HEADS, n)[0:n]
                act.activation(e, e, ACT.Exp).then_inc(S["e_r"], 1)
                if c > 0:
                    act.wait_ge(S["yg_r"], c)
                act.activation(tz[0:n, :], z2[0:n, c, :], ACT.Tanh).then_inc(S["tz_r"], 1)

            def ssd_mix(c):
                n = TT[c][1]
                act.wait_ge(S["yg_r"], c + 1)
                for g in range(GROUPS):
                    m = act.activation(y_off_sb[0:n, g * 256:(g + 1) * 256], y_sb[0:n, g * 256:(g + 1) * 256],
                                       ACT.Square, accum_out=ssy[0:n, g:g + 1])
                m.then_inc(S["ssy_r"], 1)
                act.wait_ge(S["vy_r"], c + 1)
                act.activation(rsy[0:n, :], ssy[0:n, :], ACT.Sqrt).then_inc(S["sy_r"], 1)

            def tails_turn(_):
                act.wait_ge(S["tl_ps"], 1)
                act.wait_ge(S["ob_r"], WT)
                act.activation(tail_row[0:TAILS, :], oa[0:TAILS, 0:P], ACT.Copy).then_inc(S["tl_r"], 1)
                act.wait_ge(S["tl_r"], 1)
                for q, tag in enumerate("ps"):
                    r0 = q * 36
                    act.dma_start(o["lru_conv_" + tag][0, 0].rearrange("k (r p) -> (k r) p", p=P),
                                  tail_row[r0:r0 + 12, :]).then_inc(S["tl_out"], 16)
                    act.dma_start(o["ssm_conv_" + tag][0, 0].rearrange("k (r p) -> (k r) p", p=P),
                                  tail_row[r0 + 12:r0 + 36, :]).then_inc(S["tl_out"], 16)
                    act.dma_start(o["lru_h_" + tag][0, 0].rearrange("(r p) -> r p", p=P),
                                  tail_row[72 + 4 * q:76 + 4 * q, :]).then_inc(S["tl_out"], 16)

            def state_out(i):
                act.wait_ge(S["so_ps"], i + 1)
                act.wait_ge(S["dec_ps"], NT - 1 + i)
                if i == 1:
                    act.wait_ge(S["so_out"], 16)
                act.activation(h_out, ms[:, :].rearrange("p (j n) -> p j n", j=WT), ACT.Copy).then_inc(S["so_r"], 1)
                act.wait_ge(S["so_r"], i + 1)
                act.dma_start(o["ssm_h_" + "ps"[i]][0, 0].rearrange("(j q) p n -> (q p) j n", q=2), h_out
                              ).then_inc(S["so_out"], 16)

            def ffn_norm(t):
                n = TT[t][1]
                wait_drained(act, IDX[("o", t, 3)])
                if t >= 2:
                    act.wait_ge(S["u2t_ps"], t - 1)
                    act.wait_ge(u2_out[t % 2], 16 * (t // 2))
                act.activation(u2[t % 2][0:n, :], h[0:n, t, :], ACT.Square, accum_out=ss2[0:n, t:t + 1]
                               ).then_inc(S["ssq_r"], 1)
                act.wait_ge(S["var_r"], NT + t + 1)
                act.activation(rs2[0:n, t:t + 1], ss2[0:n, t:t + 1], ACT.Sqrt).then_inc(S["std_r"], 1)

            def ffn_turn(t):
                o0, n = TT[t]
                act.wait_ge(S["u2_r"], t + 1)
                act.dma_start(u2d[o0:o0 + n, :], u2[t % 2][0:n, :]).then_inc(u2_out[t % 2], 16)
                act.wait_ge(S["u2t_ps"], t + 1)
                if t >= 2:
                    act.wait_ge(S["lg_ps"], t - 1)
                act.activation(u2T[t % 2][:, :, 0:n], zz[t % 2][:, :, :].rearrange("p a (b l) -> p (a b) l", l=P)
                               [:, :, 0:n], ACT.Copy).then_inc(S["u2t_r"], 1)

            def routing():
                act.wait_ge(S["fexp_in"], 1)
                act.activation(for_exp, for_exp, ACT.Exp).then_inc(S["fexp_r"], 1)

            def expert_pair(i, before=True):
                act.wait_ge(S["xt2_ps"], i + 1)
                act.activation(xT[:, 0:KD // 2, :], oa[:, :].rearrange("p (k l) -> p k l", k=4), ACT.Copy
                               ).then_inc(S["xt2_a"], 1)
                act.wait_ge(S["gate_done"], i + 1)
                act.activation(gate_t, za[:, 0, :], ACT.Tanh, scale=0.5).then_inc(S["gate_th"], 1)
                act.wait_ge(S["down_a"], i + 1)
                if before:
                    act.wait_ge(S["y_out"], i * 16)
                act.activation(y_out_sb[:, 0:512], zb[:, 0, :], ACT.Copy).then_inc(S["y_a"], 1)

            def final(t):
                o0, n = TT[t]
                act.wait_ge(S["hy_r"], t + 1)
                act.activation(y_back[t % 2][0][0:n, :], h[0:n, t, :], ACT.Square, accum_out=ss3[0:n, t:t + 1]
                               ).then_inc(S["ssq_r"], 1)
                act.wait_ge(S["var_r"], 2 * NT + t + 1)
                act.activation(rs3[0:n, t:t + 1], ss3[0:n, t:t + 1], ACT.Sqrt).then_inc(S["std_r"], 1)
                act.wait_ge(S["fin_r"], t + 1)
                dst = o["y_p"][0, o0:o0 + n, :] if t < NT - 1 else o["y_s"][0]
                act.dma_start(dst, h[0:n, t, :]).then_inc(S["fin_out"], 16)

            steps = {f.__name__: f for f in (keys_out, dt_turn, att_scores, att_after, att_values, silu, state_in,
                                             ssm_turn, lru, ssd_decay, ssd_mix, tails_turn, state_out,
                                             ffn_norm, ffn_turn)}
            par_up_at = 2
            for t in range(NT):
                x_norm(t)
                if t == par_up_at:
                    par_up()
            for n in range(NITEM + 1):
                for name, i in JOBS.get(n, []):
                    if name in steps:
                        steps[name](i)
                if n < NITEM:
                    item(n)
            routing()
            expert_pair(0, before=False)
            with act.Fori(1, EPAIRS) as i:
                expert_pair(i)
            act.wait_ge(S["over_r"], 1)
            total = act.value_load(over_total[0:1, 0:1], min_val=0, max_val=OVB)
            for j in range(OPAIRS):
                with act.If(total > j):
                    expert_pair(EPAIRS + j)
            for t in range(NT):
                final(t)

        def bc(v, *shape):
            return v.to_broadcast(list(shape))

        @block.vector
        def _(dve):
            links = [0]

            def link(ins):
                links[0] += 1
                ins.then_inc(S["dve_c"], 1)
                dve.wait_ge(S["dve_c"], links[0])

            def x_norm(t):
                n = TT[t][1]
                dve.wait_ge(S["ssq_r"], t + 1)
                dve.tensor_scalar(ssq[0:n, t:t + 1], ssq[0:n, t:t + 1], 1.0 / D, EPS, ALU.mult, ALU.add
                                  ).then_inc(S["var_r"], 1)
                dve.wait_ge(S["std_r"], t + 1)
                link(dve.reciprocal(rstd[0:n, t:t + 1], rstd[0:n, t:t + 1]))
                dve.tensor_scalar(h[0:n, t, :], h[0:n, t, :], rstd[0:n, t:t + 1], None, ALU.mult
                                  ).then_inc(S["xn_r"], 1)

            def x_turn(t):
                o0, n = TT[t]
                z = zz[t % 2]
                dve.wait_ge(S["xt_ps"], t + 1)
                for b in range(2):
                    g = PAR["g_mix"] + 4 * b
                    m = dve.tensor_tensor(uT[:, 4 * b:4 * b + 4, o0:o0 + n],
                                          z[:, b, :].rearrange("p (k l) -> p k l", k=4)[:, :, 0:n],
                                          bc(cpar[:, g:g + 4].unsqueeze(2), P, 4, n), ALU.mult)
                m.then_inc(S["ut_r"], 1)

            def par_half():
                dve.wait_ge(S["par_up"], 2)
                for name, k in (("b_gate", 24), ("ssm_conv_w", 40), ("lru_b_a", 8)):
                    v = cpar[:, PAR[name]:PAR[name] + k]
                    m = dve.tensor_scalar(v, v, 0.5, None, ALU.mult)
                lam = cpar[:, PAR["lru_lambda"]:PAR["lru_lambda"] + 4]
                dve.tensor_scalar(sp_x[:, 40:44], lam, -1.0, None, ALU.mult).then_inc(S["par_half"], 1)

            def item(n):
                it = ITEMS[n]
                kind, c, hh = it[:3]
                if kind not in DVE_KINDS:
                    return
                dve.wait_ge(S["pj_full"], n + 1)
                bank = pj[:, n % 2, :]
                lo = hh * HALF
                if kind == "k":
                    m = dve.tensor_copy(kT[:, c, lo:lo + HALF], bank[:, 0:HALF])
                elif kind == "b":
                    br = it[5]
                    k = (n - MIX1) // 2
                    wait_drained(dve, n - 1)
                    dst = merged[:, c, lo:lo + HALF] if br == 0 else gtmp[k % 2]
                    if k == 0:
                        dve.wait_ge(S["v_out"], 32)
                    if br > 0:
                        kk = k - 2 * KD
                        if kk >= 2:
                            dve.wait_ge(S["gm_r"], kk - 1)
                    m = dve.scalar_tensor_tensor(out=dst, in0=gsb[k % 2], scalar=1.0, in1=bank[:, 0:HALF],
                                                 op0=ALU.add, op1=ALU.mult)
                elif kind == "o":
                    t, q = c, hh
                    r = TT[t][1]
                    if n == OUT0:
                        dve.wait_ge(S["x2_in"], 16 * NT)
                    v = h[0:r, t, 256 * q:256 * (q + 1)]
                    m = dve.scalar_tensor_tensor(out=v, in0=bank[0:r, 0:256], scalar=0.5, in1=v,
                                                 op0=ALU.mult, op1=ALU.add)
                m.then_inc(S["pj_dve"], 1)

            def past_keys(i):
                dve.wait_ge(S["kp_ps"], i + 1)
                dve.tensor_copy(kpT[:, i, :], zz[i // 2][:, i % 2, :]).then_inc(S["kp_r"], 1)

            def dt_turn(_):
                dve.wait_ge(S["dt_ps"], 1)
                dve.wait_ge(S["bc_in"], 16 * 5)
                link(dve.memset(sp_x[:, 0:40], 0.0))
                link(dve.tensor_tensor(dt_sb[:, 0:4, :], ms[:, 0:32].rearrange("p (t e) -> p t e", t=4),
                                       bc(rowc[:, 0:8].unsqueeze(1), P, 4, 8), ALU.add))
                dve.tensor_tensor(dt_sb[0:DEC, 4, :], ms[0:DEC, 32:40], rowc[0:DEC, 0:8], ALU.add
                                  ).then_inc(S["dt_raw"], 1)
                dve.wait_ge(S["dt_raw"], 1)
                link(dve.tensor_scalar(sp_p, sp_x, 0.0, None, ALU.max))
                dve.scalar_tensor_tensor(out=sp_e, in0=sp_p, scalar=-2.0, in1=sp_x, op0=ALU.mult, op1=ALU.add
                                         ).then_inc(S["sp_na"], 1)
                dve.wait_ge(S["sp_eo"], 2)
                dve.tensor_scalar(sp_u, sp_e, 1.0, None, ALU.add).then_inc(S["sp_uo"], 1)
                dve.wait_ge(S["sp_uo"], 1)
                dve.wait_ge(S["sp_lo"], 1)
                link(dve.tensor_scalar(sp_u, sp_u, -1.0, None, ALU.add))
                link(dve.tensor_scalar(sp_m, sp_u, 0.0, None, ALU.is_equal))
                link(dve.tensor_tensor(sp_l, sp_l, sp_m, ALU.add))
                link(dve.tensor_tensor(sp_u, sp_u, sp_m, ALU.add))
                link(dve.reciprocal(sp_u, sp_u))
                link(dve.tensor_tensor(sp_l, sp_l, sp_e, ALU.mult))
                link(dve.tensor_tensor(sp_l, sp_l, sp_u, ALU.mult))
                link(dve.tensor_tensor(sp_x, sp_l, sp_p, ALU.add))
                dve.tensor_scalar(ls4, sp_x[:, 40:44], -4.0, None, ALU.mult)
                dve.tensor_scalar(ls4n, sp_x[:, 40:44], 4.0, None, ALU.mult)
                dve.scalar_tensor_tensor(out=dA, in0=dt_sb, scalar=-1.0, in1=bc(a_exp.unsqueeze(1), P, NT, 8),
                                         op0=ALU.mult, op1=ALU.mult).then_inc(S["dt_r"], 1)

            def att_scores(u):
                kind, hp, kb = ATT[u]
                z = zz[u % 2]
                dve.wait_ge(S["z_r"], u + 1)
                if kind == "p":
                    dve.tensor_tensor(z[:, :, 0:P], z[:, :, 0:P], bc(att_mask.unsqueeze(1), P, 2, P), ALU.add
                                      ).then_inc(S["masked"], 1)
                    dve.wait_ge(S["masked"], u + 2)
                elif kb == KB:
                    v = z[0:DEC, 0, :].rearrange("p (c q) -> p c q", c=HEADS)
                    dve.tensor_tensor(v, v, bc(att_mask[0:DEC, 0:DEC].unsqueeze(1), DEC, HEADS, DEC), ALU.add
                                      ).then_inc(S["masked"], 1)
                    dve.wait_ge(S["masked"], u + 2)
                if u >= 2:
                    dve.wait_ge(S["o_r"], u - 1)
                    dve.wait_ge(S["s_sum"], u - 1)
                link(dve.tensor_scalar(att_view(att_b[u % 2], u), att_view(z, u), 0.0, None, ALU.max))
                dve.scalar_tensor_tensor(out=att_view(att_a[u % 2], u), in0=att_view(att_b[u % 2], u),
                                         scalar=-2.0, in1=att_view(z, u), op0=ALU.mult, op1=ALU.add
                                         ).then_inc(S["nab_r"], 1)

            def conv(j):
                src = xp[j % 2]
                ssm = j < XT
                c = j if ssm else j - XT
                kind = "x" if ssm else "r"
                nt = XT if ssm else WT
                base = 12 if ssm else 0
                wait_drained(dve, IDX[(kind, c, 1)])
                link(dve.tensor_copy(src[:, SAMP:SAMP + GAP],
                                     cst[:, base:base + GAP * nt].rearrange("p (k c) -> p k c", k=GAP)[:, :, c]))
                for q, lo in enumerate((SEQ, SAMP + DEC)):
                    v = tails[:, q * 36 + base:q * 36 + base + GAP * nt].rearrange("p (k c) -> p k c", k=GAP)
                    dve.tensor_copy(v[:, :, c], src[:, lo:lo + GAP])
                dst = (xconv if ssm else xc)[:, c, :]
                w0 = PAR["ssm_conv_w" if ssm else "lru_conv_w"] + c
                b0 = PAR["ssm_conv_b" if ssm else "lru_conv_b"] + c
                if j == 0:
                    dve.wait_ge(S["kp_ps"], 4)
                link(dve.tensor_scalar(dst, src[:, 0:TW], cpar[:, w0:w0 + 1], cpar[:, b0:b0 + 1],
                                       ALU.mult, ALU.add))
                for k in range(1, CW):
                    w = w0 + k * nt
                    m = dve.scalar_tensor_tensor(out=dst, in0=src[:, k:k + TW], scalar=cpar[:, w:w + 1], in1=dst,
                                                 op0=ALU.mult, op1=ALU.add)
                    if k < CW - 1:
                        link(m)
                m.then_inc(S["conv_c"], 1)

            def silu(i):
                dve.wait_ge(S["silu_t"], i + 1)
                dve.scalar_tensor_tensor(out=xconv[:, i, :], in0=th[i % 2], scalar=1.0, in1=xconv[:, i, :],
                                         op0=ALU.add, op1=ALU.mult).then_inc(S["silu_r"], 1)

            def ssm_turn(t):
                n = TT[t][1]
                if t == 0:
                    dve.wait_ge(S["s_sum"], NATT)
                dve.wait_ge(S["turn_ps"], t + 1)
                dve.tensor_copy(xs_tok[0:n, t, :], ms[0:n, :]).then_inc(S["turn_r"], 1)

            def lru(c):
                r, i, la, m, gl = lt
                dve.wait_ge(S["lru_tr"], 2 * c + 2)
                dve.scalar_tensor_tensor(out=i, in0=i, scalar=1.0, in1=xc[:, c, :], op0=ALU.add, op1=ALU.mult
                                         ).then_inc(S["lru_ib"], 1)
                dve.wait_ge(S["lru_a2"], c + 1)
                dve.wait_ge(S["lru_ac"], 2 * c + 2)
                dve.scalar_tensor_tensor(out=m, in0=m, scalar=1.0, in1=r, op0=ALU.add, op1=ALU.mult
                                         ).then_inc(S["lru_m2"], 1)
                dve.wait_ge(S["lru_mu"], c + 1)
                link(dve.scalar_tensor_tensor(out=i, in0=r, scalar=0.5, in1=i, op0=ALU.mult, op1=ALU.mult))
                h0 = PAR["state_lru_h"] + c
                dve.tensor_tensor_scan(m[:, 0:SEQ], la[:, 0:SEQ], i[:, 0:SEQ], 0.0, ALU.mult, ALU.add)
                link(dve.tensor_tensor_scan(m[:, SAMP:SAMP + DEC], la[:, SAMP:SAMP + DEC], i[:, SAMP:SAMP + DEC],
                                            cpar[:, h0:h0 + 1], ALU.mult, ALU.add))
                for q, last in enumerate((SEQ - 1, SAMP + DEC - 1)):
                    col = 72 + 4 * q + c
                    dve.tensor_copy(tails[:, col:col + 1], m[:, last:last + 1]).then_inc(S["lru_h"], 1)
                dve.wait_ge(S["lru_gt"], c + 1)
                link(dve.scalar_tensor_tensor(out=gl, in0=gl, scalar=1.0, in1=gb[:, c, :],
                                              op0=ALU.add, op1=ALU.mult))
                dve.scalar_tensor_tensor(out=oBT[:, c, 0:SEQ], in0=gl[:, 0:SEQ], scalar=0.5, in1=m[:, 0:SEQ],
                                         op0=ALU.mult, op1=ALU.mult)
                dve.scalar_tensor_tensor(out=oBT[:, c, SEQ:T], in0=gl[:, SAMP:SAMP + DEC], scalar=0.5,
                                         in1=m[:, SAMP:SAMP + DEC], op0=ALU.mult, op1=ALU.mult
                                         ).then_inc(S["ob_r"], 1)

            def ssd_decay(c):
                n = TT[c][1]
                e = at(e_flat, HEADS, n)[0:n]
                mm = at(m_flat, HEADS, n)[0:n]
                dve.wait_ge(S["dec_ps"], c + 1)
                dve.tensor_copy(acs[0:n, :], zb[0:n, 0, 256:264]).then_inc(S["acs_r"], 1)
                dve.wait_ge(S["acs_r"], c + 1)
                if c > 0:
                    dve.wait_ge(S["xdd_r"], c)
                src = za[0:n, :, :].rearrange("p a (b l) -> p (a b) l", l=P) if n == P else \
                    za[0:n, 0, :].rearrange("p (b l) -> p b l", l=n)
                dve.tensor_tensor(e, src, bc(acs[0:n, :].unsqueeze(2), n, HEADS, n), ALU.subtract
                                  ).then_inc(S["d_r"], 1)
                dve.wait_ge(S["e_r"], c + 1)
                if c > 0:
                    dve.wait_ge(S["mix_ps"], c)
                for g in range(GROUPS):
                    k = dve.tensor_tensor(mm[:, 4 * g:4 * g + 4, :], e[:, 4 * g:4 * g + 4, :],
                                          bc(zb[0:n, 0, g * n:(g + 1) * n].unsqueeze(1), n, 4, n), ALU.mult)
                k.then_inc(S["m_r"], 1)

            def ssd_mix(c):
                n = TT[c][1]
                y3 = y_sb[0:n, :].rearrange("p (e d) -> p e d", e=HEADS)
                t3 = y_off_sb[0:n, :].rearrange("p (e d) -> p e d", e=HEADS)
                dve.wait_ge(S["mix_ps"], c + 1)
                dve.wait_ge(S["ea_r"], c + 1)
                state = hT if c < NT - 1 else hS
                if c > 0:
                    dve.wait_ge(S["yt_ps"], c)
                    link(dve.tensor_tensor(t3, oa[0:n, :].rearrange("p (e d) -> p e d", e=HEADS),
                                           bc(ea[0:n, :].unsqueeze(2), n, HEADS, HD), ALU.mult))
                    dve.tensor_tensor(y_sb[0:n, :], zb[0:n, 1, :], y_off_sb[0:n, :], ALU.add
                                      ).then_inc(S["y0_r"], 1)
                    dve.wait_ge(S["hcd_r"], c)
                    dve.tensor_tensor(state, ms[:, :], state, ALU.add).then_inc(S["h_r"], 1)
                else:
                    dve.tensor_copy(y_sb[0:n, :], zb[0:n, 1, :]).then_inc(S["y0_r"], 1)
                    dve.tensor_copy(state, ms[:, :]).then_inc(S["h_r"], 1)
                dve.wait_ge(S["tz_r"], c + 1)
                dve.scalar_tensor_tensor(out=tz[0:n, :], in0=tz[0:n, :], scalar=1.0, in1=z2[0:n, c, :],
                                         op0=ALU.add, op1=ALU.mult).then_inc(S["y1_r"], 1)
                dve.wait_ge(S["ssy_r"], c + 1)
                dve.tensor_scalar(ssy[0:n, :], ssy[0:n, :], 1.0 / 256, EPS, ALU.mult, ALU.add
                                  ).then_inc(S["vy_r"], 1)
                dve.wait_ge(S["sy_r"], c + 1)
                link(dve.reciprocal(rsy[0:n, :], rsy[0:n, :]))
                for g in range(GROUPS):
                    v = y_sb[0:n, g * 256:(g + 1) * 256]
                    k = dve.tensor_scalar(v, v, rsy[0:n, g:g + 1], None, ALU.mult)
                k.then_inc(S["yn_r"], 1)

            def ssd_turn(c):
                o0, n = TT[c]
                dve.wait_ge(S["yt_ps"], c + 1)
                g = PAR["ssm_norm_g"]
                dve.tensor_tensor(oCT[:, :, o0:o0 + n], oa[:, :].rearrange("p (j l) -> p j l", j=WT)[:, :, 0:n],
                                  bc(cpar[:, g:g + 4].unsqueeze(2), P, WT, n), ALU.mult).then_inc(S["oc_r"], 1)

            def ffn_norm(t):
                n = TT[t][1]
                dve.wait_ge(S["ssq_r"], NT + t + 1)
                dve.tensor_scalar(ss2[0:n, t:t + 1], ss2[0:n, t:t + 1], 1.0 / D, EPS, ALU.mult, ALU.add
                                  ).then_inc(S["var_r"], 1)
                dve.wait_ge(S["std_r"], NT + t + 1)
                link(dve.reciprocal(rs2[0:n, t:t + 1], rs2[0:n, t:t + 1]))
                dve.tensor_scalar(u2[t % 2][0:n, :], h[0:n, t, :], rs2[0:n, t:t + 1], None, ALU.mult
                                  ).then_inc(S["u2_a"], 1)

            def ffn_turn(t):
                n = TT[t][1]
                if t == 0:
                    link(dve.memset(lg, 0.0))
                dve.wait_ge(S["lg_ps"], t + 1)
                dve.tensor_tensor(lg[0:n, t, :], ms[0:n, t * 36:(t + 1) * 36], rowc[0:n, 24:60], ALU.add
                                  ).then_inc(S["lg_r"], 1)

            def per(v, k):
                return bc(v.unsqueeze(2), P, NT, k)

            def across(v, k=NT):
                return bc(v.unsqueeze(1), P, k, v.shape[-1])

            def one_hot(dst, values, top, cand, key, keys):
                k = values.shape[-1]
                link(dve.tensor_reduce(top, values, AXX, ALU.max))
                link(dve.tensor_tensor(cand, values, per(top, k), ALU.is_equal))
                link(dve.tensor_tensor(cand, cand, across(keys), ALU.mult))
                link(dve.tensor_reduce(key, cand, AXX, ALU.max))
                link(dve.tensor_tensor(dst, across(keys), per(key, k), ALU.is_equal))

            def floor_div(dst, src, d):
                link(dve.tensor_scalar(dst, src, 1.0 / d, 0.5 / d - 0.5, ALU.mult, ALU.add))
                link(dve.tensor_scalar(dst, dst, ROUND, None, ALU.add))
                link(dve.tensor_scalar(dst, dst, ROUND, None, ALU.subtract))

            def routing():
                g_lg, e_lg = lg[:, :, 0:NG], lg[:, :, NG:NG + NE]
                dve.wait_ge(S["lg_r"], NT)
                dve.wait_ge(S["ids_r"], 1)
                dve.tensor_copy(iota_f, iota_i)
                link(dve.tensor_scalar(rev, iota_i, -1.0, float(NE), ALU.mult, ALU.add))
                one_hot(g_hot, g_lg, g_max, g_cand, g_key, rev[:, 0:NG])
                link(dve.tensor_scalar(g_cand, g_hot, BIG, -BIG, ALU.mult, ALU.add))
                for t in range(NT):
                    m = dve.tensor_tensor(e_masked[:, t, :].rearrange("p (g e) -> p g e", g=NG),
                                          e_lg[:, t, :].rearrange("p (g e) -> p g e", g=NG),
                                          bc(g_cand[:, t, :].unsqueeze(2), P, NG, EPG), ALU.add)
                link(m)
                one_hot(e_hot[0], e_masked, v_top[0], e_cand, e_key, rev)
                link(dve.scalar_tensor_tensor(out=e_masked, in0=e_hot[0], scalar=-BIG, in1=e_masked,
                                              op0=ALU.mult, op1=ALU.add))
                one_hot(e_hot[1], e_masked, v_top[1], e_cand, e_key, rev)
                for s in range(2):
                    m = dve.memset(e_hot[s][DEC:P, NT - 1, :], 0.0)
                link(m)
                dve.tensor_tensor(hot_sum, e_hot[0], e_hot[1], ALU.add).then_inc(S["hots_r"], 1)
                dve.tensor_tensor(for_exp[:, 0:NT * NG].rearrange("p (t g) -> p t g", t=NT), g_lg, per(g_max, NG),
                                  ALU.subtract)
                dve.tensor_tensor(for_exp[:, NT * NG:], v_top[1], v_top[0], ALU.subtract).then_inc(S["fexp_in"], 1)
                dve.wait_ge(S["rank_ps"], 1)
                link(dve.memset(tile_base[:, 0, :], 0.0))
                for t in range(NT):
                    link(dve.tensor_tensor(tile_base[:, t + 1, :], tile_base[:, t, :],
                                           ms[:, (NT + t) * NE:(NT + t + 1) * NE], ALU.add))
                link(dve.tensor_tensor(rank_full, ms[:, 0:NT * NE].rearrange("p (t e) -> p t e", t=NT),
                                       tile_base[:, 0:NT, :], ALU.add))
                link(dve.tensor_scalar(n_over, tile_base[:, NT, :], -1.0, None, ALU.add))
                floor_div(n_over, n_over, BLK)
                link(dve.tensor_scalar(n_over, n_over, 0.0, None, ALU.max))
                link(dve.tensor_tensor_scan(over_incl, ones[:, 0:NE], n_over, 0.0, ALU.mult, ALU.add))
                link(dve.tensor_tensor(over_start, over_incl, n_over, ALU.subtract))
                for s in range(2):
                    for dst, v in ((rank, rank_full), (first, across(over_start)), (expert, across(iota_f))):
                        link(dve.tensor_tensor(e_cand, e_hot[s], v, ALU.mult))
                        link(dve.tensor_reduce(dst[:, s, :], e_cand, AXX, ALU.add))
                floor_div(div, rank, BLK)
                link(dve.scalar_tensor_tensor(out=place, in0=div, scalar=-float(BLK), in1=rank,
                                              op0=ALU.mult, op1=ALU.add))
                link(dve.tensor_scalar(is_over, div, 0.0, None, ALU.is_gt))
                link(dve.scalar_tensor_tensor(out=first, in0=first, scalar=-1.0, in1=div, op0=ALU.add, op1=ALU.add))
                link(dve.tensor_scalar(side, expert, float(EPAIRS), None, ALU.is_ge))
                link(dve.scalar_tensor_tensor(out=col, in0=side, scalar=-float(EPAIRS), in1=expert,
                                              op0=ALU.mult, op1=ALU.add))
                link(dve.tensor_scalar(div, first, float(OPAIRS), None, ALU.is_ge))
                link(dve.scalar_tensor_tensor(out=first, in0=div, scalar=-float(OPAIRS), in1=first,
                                              op0=ALU.mult, op1=ALU.add))
                link(dve.tensor_scalar(first, first, float(EPAIRS), None, ALU.add))
                for own, over in ((side, div), (col, first)):
                    link(dve.tensor_tensor(over, over, own, ALU.subtract))
                    link(dve.tensor_tensor(over, over, is_over, ALU.mult))
                    link(dve.tensor_tensor(own, own, over, ALU.add))
                link(dve.scalar_tensor_tensor(out=place, in0=side, scalar=float(BLK), in1=place,
                                              op0=ALU.mult, op1=ALU.add))
                flat = [v.rearrange("p s t -> p (s t)") for v in (place, col)]
                dve.scalar_tensor_tensor(out=tab_row, in0=flat[0], scalar=float(NPC), in1=flat[1],
                                         op0=ALU.mult, op1=ALU.add)
                dve.scalar_tensor_tensor(out=y_row, in0=flat[1], scalar=float(2 * BLK), in1=flat[0],
                                         op0=ALU.mult, op1=ALU.add).then_inc(S["rows_r"], 1)
                link(dve.tensor_tensor(over_cmp, bc(over_incl.unsqueeze(1), P, OVB, NE),
                                       bc(iota_f[:, 0:OVB].unsqueeze(2), P, OVB, NE), ALU.is_le))
                link(dve.tensor_reduce(eid, over_cmp, AXX, ALU.add))
                dve.tensor_scalar(over_expert, eid, float(NE - 1), None, ALU.min)
                dve.tensor_copy(over_total, over_incl[:, NE - 1:NE]).then_inc(S["over_r"], 1)
                dve.wait_ge(S["fexp_r"], 1)
                link(dve.tensor_reduce(p_sel, for_exp[:, 0:NT * NG].rearrange("p (t g) -> p t g", t=NT), AXX,
                                       ALU.add))
                link(dve.tensor_scalar(w_sel[:, 0, :], for_exp[:, NT * NG:], 1.0, None, ALU.add))
                link(dve.tensor_tensor(w_sel[:, 0, :], w_sel[:, 0, :], p_sel, ALU.mult))
                link(dve.reciprocal(w_sel[:, 0, :], w_sel[:, 0, :]))
                link(dve.tensor_tensor(w_sel[:, 1, :], w_sel[:, 0, :], for_exp[:, NT * NG:], ALU.mult))

            def expert_pair(i, before=True):
                dve.wait_ge(S["xt2_ps"], i + 1)
                dve.tensor_copy(xT[:, KD // 2:KD, :], ms[:, :].rearrange("p (k l) -> p k l", k=4)
                                ).then_inc(S["xt2_d"], 1)
                dve.wait_ge(S["gate_th"], i + 1)
                dve.scalar_tensor_tensor(out=gate_a, in0=gate_t, scalar=1.0, in1=za[:, 0, :],
                                         op0=ALU.add, op1=ALU.mult).then_inc(S["gate_mul"], 1)
                dve.wait_ge(S["gate_mul"], i + 1)
                dve.wait_ge(S["up_done"], i + 1)
                dve.scalar_tensor_tensor(out=hid, in0=gate_a, scalar=0.5, in1=za[:, 1, :],
                                         op0=ALU.mult, op1=ALU.mult).then_inc(S["hid_r"], 1)
                dve.wait_ge(S["hidt_ps"], i + 1)
                dve.tensor_copy(hidT, oa[:, :].rearrange("p (k l) -> p k l", k=4)).then_inc(S["hidt_r"], 1)
                dve.wait_ge(S["down_b"], i + 1)
                if before:
                    dve.wait_ge(S["y_out"], i * 16)
                dve.tensor_copy(y_out_sb[:, 512:D], zb[:, 1, :]).then_inc(S["y_b"], 1)

            def final(t):
                n = TT[t][1]
                hv = h[0:n, t, :]
                dve.wait_ge(back_in[t % 2], 32 * (t // 2 + 1))
                link(dve.scalar_tensor_tensor(out=hv, in0=y_back[t % 2][0][0:n, :], scalar=w_sel[0:n, 0, t:t + 1],
                                              in1=hv, op0=ALU.mult, op1=ALU.add))
                dve.scalar_tensor_tensor(out=hv, in0=y_back[t % 2][1][0:n, :], scalar=w_sel[0:n, 1, t:t + 1],
                                         in1=hv, op0=ALU.mult, op1=ALU.add).then_inc(S["hy_r"], 1)
                dve.wait_ge(S["ssq_r"], 2 * NT + t + 1)
                dve.tensor_scalar(ss3[0:n, t:t + 1], ss3[0:n, t:t + 1], 1.0 / D, EPS, ALU.mult, ALU.add
                                  ).then_inc(S["var_r"], 1)
                dve.wait_ge(S["std_r"], 2 * NT + t + 1)
                dve.wait_ge(S["gains_in"], 32)
                link(dve.reciprocal(rs3[0:n, t:t + 1], rs3[0:n, t:t + 1]))
                dve.scalar_tensor_tensor(out=hv, in0=hv, scalar=rs3[0:n, t:t + 1], in1=g_fin[0:n, :],
                                         op0=ALU.mult, op1=ALU.mult).then_inc(S["fin_r"], 1)

            steps = {f.__name__: f for f in (past_keys, dt_turn, att_scores, conv, silu, ssm_turn, lru,
                                             ssd_decay, ssd_mix, ssd_turn, ffn_norm, ffn_turn)}
            x_norm(0)
            x_norm(1)
            x_norm(2)
            par_half()
            x_turn(0)
            x_norm(3)
            x_turn(1)
            x_norm(4)
            for t in range(2, NT):
                x_turn(t)
            for n in range(NITEM + 1):
                for name, i in JOBS.get(n, []):
                    if name in steps:
                        steps[name](i)
                if n < NITEM:
                    item(n)
            routing()
            expert_pair(0, before=False)
            with dve.Fori(1, EPAIRS) as i:
                expert_pair(i)
            dve.wait_ge(S["over_r"], 1)
            total = dve.value_load(over_total[0:1, 0:1], min_val=0, max_val=OVB)
            for j in range(OPAIRS):
                with dve.If(total > j):
                    expert_pair(EPAIRS + j)
            for t in range(NT):
                final(t)

        @block.gpsimd
        def _(pool):
            pool.memset(ones, 1.0)
            pool.memset(neg_ones, -1.0)
            pool.memset(att_s, 0.0).then_inc(S["pool_c"], 1)
            pool.wait_ge(S["pool_c"], 1)
            zeros = att_s[:, 0, 0:P]

            def mask(dst, src, op, fill, step, ch):
                pool.affine_select(out=dst, in_=src, pattern=[[step, P]], compare_op=op, fill=fill, base=0,
                                   channel_multiplier=ch).then_inc(S["consts"], 1)

            mask(ident, zeros, ALU.not_equal, 1.0, -1, 1)
            mask(u_incl, ones, ALU.is_ge, 0.0, 1, -1)
            mask(u_strict, ones, ALU.is_gt, 0.0, 1, -1)
            mask(neg_l, neg_ones, ALU.is_ge, 0.0, -1, 1)
            mask(att_mask, zeros, ALU.is_gt, NEG, 1, -1)
            mask(ssd_mask, zeros, ALU.is_ge, NEG, 1, -1)
            pool.memset(xp[0], 0.0)
            pool.memset(xp[1], 0.0).then_inc(S["consts"], 1)
            pool.memset(gb[:, :, SEQ:TW], 0.0).then_inc(S["consts"], 1)
            pool.memset(q2, 0.0).then_inc(S["q_zero"], 1)
            pool.wait_ge(S["consts"], 8)
            pool.sem_inc(S["masked"], 1)
            pool.iota(iota_i, [[1, NE]], base=0, channel_multiplier=0)
            pool.iota(tok_id, [[P, NT]], base=0, channel_multiplier=1)
            pool.memset(no_token, 0).then_inc(S["ids_r"], 1)
            pool.dma_start(yd[NE * BLK:(NE + OVB) * BLK, :].rearrange("(c p) d -> p c d", p=P),
                           att_s[:, :, :].rearrange("p a b -> p (a b)").unsqueeze(1).to_broadcast([P, OPAIRS, D])
                           ).then_inc(S["yd_zero"], 16)
            pool.wait_ge(S["ids_r"], 1)
            pool.dma_start(tabd.rearrange("(p c) o -> p (c o)", p=P), no_token).then_inc(S["tab_moved"], 16)

            def att_soft(u):
                b, ln = att_view(att_b[u % 2], u), att_view(att_a[u % 2], u)
                pool.wait_ge(S["l_r"], u + 1)
                pool.tensor_tensor(b, b, ln, ALU.add).then_inc(S["sp_r"], 1)

            def att_after(u):
                kind, hp, kb = ATT[u]
                s, b = att_s, att_b[u % 2]
                pool.wait_ge(S["zw_r"], u + 1)
                if u == 0:
                    pool.wait_ge(S["yd_zero"], 16)
                if kind == "p":
                    n = SEQ - kb * P
                    if kb == KB - 1:
                        pool.tensor_copy(s[:, :, 0:n], b[:, :, 0:n]).then_inc(S["s_sum"], 1)
                    elif kb > 0:
                        pool.tensor_tensor(b[:, :, P:n], b[:, :, P:n], s[:, :, 0:n - P], ALU.add
                                           ).then_inc(S["pool_c"], 1)
                        cnt[0] += 1
                        pool.wait_ge(S["pool_c"], cnt[0])
                        pool.tensor_copy(s[:, :, 0:n], b[:, :, 0:n]).then_inc(S["s_sum"], 1)
                    else:
                        pool.memset(s[:, 0, :], 0.0).then_inc(S["s_sum"], 1)
                else:
                    n = P if kb < KB else DEC
                    pool.tensor_tensor(s[0:n, 0, :], s[0:n, 0, :], b[0:n, 0, :], ALU.add).then_inc(S["s_sum"], 1)

            cnt = [1]

            def lru_weights():
                pool.wait_ge(S["s_sum"], NATT)
                pool.wait_ge(S["conv_c"], XT + WT)
                pool.wait_ge(S["o_out"], PAIRS + 1)
                pool.memset(lru_w, 0.0).then_inc(S["lruw_z"], 1)
                pool.wait_ge(S["lruw_z"], 1)
                for g, name in enumerate(("lru_w_a", "lru_w_x")):
                    for b in range(HEADS):
                        r0 = (b % 2) * HD
                        pool.dma_start(lru_w[r0:r0 + HD, g, b // 2, r0:r0 + HD], a[name][0, b]
                                       ).then_inc(S["lruw_in"], 16)
                pool.dma_start(ss_in, a["state_ssm_h"][0, 0].rearrange("(j q) p n -> (q p) j n", q=2)
                               ).then_inc(S["ssin_in"], 16)

            def lru(c):
                r, i, la, m, gl = lt
                g = gb[:, c, :]
                if c > 0:
                    pool.wait_ge(S["ob_r"], c)
                pool.tensor_tensor(gl, g, g, ALU.mult).then_inc(S["lru_g2"], 1)
                pool.wait_ge(S["lru_g2"], 2 * c + 1)
                pool.tensor_scalar(gl, gl, GELU_A, 1.0, ALU.mult, ALU.add).then_inc(S["lru_g2"], 1)
                pool.wait_ge(S["lru_g2"], 2 * c + 2)
                pool.tensor_tensor(gl, gl, g, ALU.mult).then_inc(S["lru_g3"], 1)
                pool.wait_ge(S["lru_ac"], 2 * c + 1)
                pool.tensor_tensor(m, la, la, ALU.mult).then_inc(S["lru_a2"], 1)

            def decays(c):
                n = TT[c][1]
                td = at(td_flat, HEADS, n)[0:n]
                if c == NT - 1:
                    pool.wait_ge(S["so_out"], 16)
                if c == 0:
                    pool.wait_ge(S["dt_r"], 1)
                pool.tensor_tensor(td, bc(u_incl[0:n, 0:n].unsqueeze(1), n, HEADS, n),
                                   bc(dA[0:n, c, :].unsqueeze(2), n, HEADS, n), ALU.mult).then_inc(S["td_r"], 1)

            def ssd_decay(c):
                n = TT[c][1]
                e = at(e_flat, HEADS, n)[0:n]
                if c == 0 or c == NT - 1:
                    decays(c)
                pool.wait_ge(S["d_r"], c + 1)
                pool.tensor_tensor(e, e, bc(ssd_mask[0:n, 0:n].unsqueeze(1), n, HEADS, n), ALU.add
                                   ).then_inc(S["em_r"], 1)
                if c == 0:
                    pool.wait_ge(S["turn_r"], 2 * NT)
                if c > 0:
                    pool.wait_ge(S["mix_ps"], c)
                xs3 = xs_tok[0:n, c, :].rearrange("p (e d) -> p e d", e=HEADS)
                pool.tensor_tensor(xdt[0:n], xs3, bc(dt_sb[0:n, c, :].unsqueeze(2), n, HEADS, HD), ALU.mult
                                   ).then_inc(S["xdt_r"], 1)
                pool.wait_ge(S["xdt_r"], c + 1)
                pool.wait_ge(S["e_r"], c + 1)
                pool.tensor_tensor(xdd[0:n], xdt[0:n], bc(e[:, :, n - 1:n], n, HEADS, HD), ALU.mult
                                   ).then_inc(S["xdd_r"], 1)

            def ssd_mix(c):
                n = TT[c][1]
                state = hT if c < NT - 1 else hS
                pool.wait_ge(S["mix_ps"], c + 1)
                if c > 0:
                    pool.wait_ge(S["ea_r"], c + 1)
                    s3 = state.rearrange("p (e d) -> p e d", e=HEADS)
                    pool.tensor_tensor(s3, s3, bc(cd.unsqueeze(2), P, HEADS, HD), ALU.mult).then_inc(S["hcd_r"], 1)
                xs3 = xs_tok[0:n, c, :].rearrange("p (e d) -> p e d", e=HEADS)
                pool.tensor_tensor(xs3, xs3, bc(rowc[0:n, 16:24].unsqueeze(2), n, HEADS, HD), ALU.mult
                                   ).then_inc(S["y2_r"], 1)
                pool.wait_ge(S["y2_r"], 2 * c + 1)
                pool.wait_ge(S["y0_r"], c + 1)
                pool.tensor_tensor(y_sb[0:n, :], y_sb[0:n, :], xs_tok[0:n, c, :], ALU.add).then_inc(S["y2_r"], 1)
                pool.wait_ge(S["y2_r"], 2 * c + 2)
                pool.wait_ge(S["y1_r"], c + 1)
                pool.tensor_tensor(y_sb[0:n, :], y_sb[0:n, :], tz[0:n, :], ALU.mult).then_inc(S["yg_r"], 1)
                if c + 1 < NT - 1:
                    decays(c + 1)

            def item(n):
                it = ITEMS[n]
                if it[0] == "b" and it[5] > 0:
                    _, c, hh = it[:3]
                    k = (n - MIX1) // 2
                    wait_drained(pool, n)
                    v = merged[:, c, hh * HALF:(hh + 1) * HALF]
                    pool.tensor_tensor(v, v, gtmp[k % 2], ALU.add).then_inc(S["gm_r"], 1)

            def ffn_norm(t):
                n = TT[t][1]
                if t == 0:
                    pool.wait_ge(S["gm_r"], 4 * KD)
                    pool.dma_start(g_ffn, a["g_ffn"][0:1, :].partition_broadcast(P)).then_inc(S["gains_in"], 16)
                    for lo, k, name in ((0, NG, "w_router_group"), (NG, NE, "w_router_expert")):
                        pool.dma_start(w_r[:, :, lo:lo + k], a[name][0].rearrange("(k p) n -> p k n", p=P)
                                       ).then_inc(S["wr_in"], 16)
                    pool.wait_ge(S["gains_in"], 16)
                pool.wait_ge(S["u2_a"], t + 1)
                pool.tensor_tensor(u2[t % 2][0:n, :], u2[t % 2][0:n, :], g_ffn[0:n, :], ALU.mult
                                   ).then_inc(S["u2_r"], 1)

            steps = {f.__name__: f for f in (att_soft, att_after, lru, ssd_decay, ssd_mix, ffn_norm)}
            for n in range(NITEM + 1):
                if n == MIX1:
                    lru_weights()
                for name, i in JOBS.get(n, []):
                    if name in steps:
                        steps[name](i)
                if n < NITEM:
                    item(n)
            pool.wait_ge(S["lg_ps"], NT)
            pool.dma_start(g_fin, a["g_final"].rearrange("(o d) -> o d", o=1).partition_broadcast(P)
                           ).then_inc(S["gains_in"], 16)
            pool.wait_ge(S["rows_r"], 1)
            pool.wait_ge(S["tab_moved"], 16)
            for s in range(2):
                for t, (o0, n) in enumerate(TT):
                    c = s * NT + t
                    pool.indirect_dma_start(out=tabd, out_offset=bass.IndirectOffsetOnAxis(
                        ap=tab_row[0:n, c:c + 1], axis=0), in_=tok_id[0:n, t:t + 1], in_offset=None
                                            ).then_inc(S["tab_out"], 16)
            pool.wait_ge(S["tab_out"], 16 * 2 * NT)
            pool.dma_start(tab, tabd.rearrange("(p c) o -> p (c o)", p=P)).then_inc(S["tab_moved"], 16)
            pool.wait_ge(S["tab_moved"], 32)
            for s in range(2):
                pool.wait_ge(u2_out[s], 16 * ((NT + 1 - s) // 2))

            def expert_pair(i, before=True):
                if before:
                    pool.wait_ge(S["xg_in"], i * 16)
                    pool.wait_ge(S["xt2_ps"], i)
                pool.tensor_copy(idx_now, tab[:, bass.ds(i, 1)]).then_inc(S["idx_r"], 1)
                pool.wait_ge(S["idx_r"], i + 1)
                pool.sem_inc(S["idx_seen"], 1)
                pool.indirect_dma_start(out=xg, out_offset=None, in_=u2d, in_offset=bass.IndirectOffsetOnAxis(
                    ap=idx_now, axis=0)).then_inc(S["xg_in"], 16)

            expert_pair(0, before=False)
            with pool.Fori(1, EPAIRS) as i:
                expert_pair(i)
            pool.wait_ge(S["over_r"], 1)
            total = pool.value_load(over_total[0:1, 0:1], min_val=0, max_val=OVB)
            for j in range(OPAIRS):
                with pool.If(total > j):
                    expert_pair(EPAIRS + j)
            pool.wait_ge(S["experts_done"], 1)
            for t, (o0, n) in enumerate(TT):
                if t >= 2:
                    pool.wait_ge(S["ssq_r"], 2 * NT + t - 1)
                for s in range(2):
                    c = s * NT + t
                    pool.indirect_dma_start(out=y_back[t % 2][s][0:n, :], out_offset=None, in_=yd,
                                            in_offset=bass.IndirectOffsetOnAxis(ap=y_row[0:n, c:c + 1], axis=0)
                                            ).then_inc(back_in[t % 2], 16)


OUTS = [("y_p", (1, SEQ, D)), ("y_s", (1, DEC, D)),
        ("k_p", (1, 1, SEQ, HEADS, HD)), ("v_p", (1, 1, SEQ, HEADS, HD)),
        ("lru_conv_p", (1, 1, GAP, W)), ("lru_h_p", (1, 1, W)), ("ssm_conv_p", (1, 1, GAP, XBC)),
        ("ssm_h_p", (1, 1, HEADS, HD, STATE)),
        ("k_s", (1, 1, DEC, HEADS, HD)), ("v_s", (1, 1, DEC, HEADS, HD)),
        ("lru_conv_s", (1, 1, GAP, W)), ("lru_h_s", (1, 1, W)), ("ssm_conv_s", (1, 1, GAP, XBC)),
        ("ssm_h_s", (1, 1, HEADS, HD, STATE))]


def kernel(**inputs):
    import numpy as np
    from concourse import bacc
    from concourse.bass_utils import run_bass_kernel_spmd

    nc = bacc.Bacc("TRN2", target_bir_lowering=False, num_devices=1)
    arrays, a, o = {}, {}, {}
    for name, x in inputs.items():
        arrays["in_" + name] = np.ascontiguousarray(x)
        a[name] = nc.dram_tensor("in_" + name, arrays["in_" + name].shape, F32, kind="ExternalInput").ap()
    for name, shape in OUTS:
        o[name] = nc.dram_tensor("out_" + name, shape, F32, kind="ExternalOutput").ap()
    trunk_and_experts(nc, a, o)
    r = run_bass_kernel_spmd(nc, [arrays], core_ids=[0])
    return tuple(r.results[0]["out_" + name] for name, _ in OUTS)
```

```python
from contextlib import ExitStack

import concourse.bass as bass
from concourse import mybir

F32 = mybir.dt.float32
F32R = mybir.dt.float32r
I32 = mybir.dt.int32
U32 = mybir.dt.uint32
ALU = mybir.AluOpType
ACT = mybir.ActivationFunctionType
AXX = mybir.AxisListType.X

P = 128
D = 1024
SEQ = 512
DEC = 64
PAST = 512
T = SEQ + DEC
HALF = T // 2
KD = D // P
TT = [(t * P, P) for t in range(SEQ // P)] + [(SEQ, DEC)]
NT = len(TT)
HEADS = 8
HD = 64
PAIRS = HEADS // 2
KB = SEQ // P
W = 512
WT = W // P
STATE = 128
GROUPS = 2
XBC = W + 2 * GROUPS * STATE
XT = XBC // P
CW = 4
GAP = CW - 1
TW = SEQ + GAP + DEC + 1
SAMP = SEQ + GAP
XP = TW + GAP
EPS = 1e-6
NEG = -1.0e30
BIG = 3.0e38
GELU_C = 0.7978845608028654
GELU_A = 0.044715

NG = 4
EPG = 8
NE = NG * EPG
DE = D // 2
BLK = 64
NA = T * 2
OVB = NA // (BLK + 1) + 1
OVB += OVB % 2
EPAIRS = NE // 2
OPAIRS = OVB // 2
NPC = EPAIRS + OPAIRS

PAR_ROWS = [("g_mix", 8), ("b_gate", 24), ("lru_conv_w", 16), ("lru_conv_b", 4), ("ssm_conv_w", 32),
            ("ssm_conv_b", 8), ("lru_b_a", 4), ("lru_b_x", 4), ("lru_lambda", 4), ("ssm_norm_g", 4),
            ("state_lru_h", 4)]
PAR = {}
_n = 0
for _name, _k in PAR_ROWS:
    PAR[_name] = _n
    _n += _k
NPAR = _n
NST = 36
TAILS = 80
SMALL = 1312
ARENA = 53200
ROUND = 12582912.0

UNITS = [("in", P * i) for i in range(12)] + [("in", 3072 + P * i) for i in range(8)]
UNITS += [("in", 1536 + P * i) for i in range(8)] + [("in", 2560 + P * i) for i in range(4)]
GATE0 = len(UNITS)
for _b in range(3):
    for _c in range(KD):
        UNITS += [("gate", _b * D + _c * P)]
        if _c in (0, KD // 2):
            UNITS += [("branch", _b, _c // (KD // 2))]
OUTU = len(UNITS)
UNITS += [("out", 256 * i) for i in range(4)]
UIX = {u: i for i, u in enumerate(UNITS)}
NSLOT = 4

ITEMS = []
for _c in range(WT):
    ITEMS += [("q", _c, h, _c, 0) for h in range(2)]
for _c in range(WT):
    ITEMS += [("k", _c, h, 4 + _c, 0) for h in range(2)]
for _u in range(2):
    ITEMS += [("v", _u, t, 8 + 2 * _u, 0) for t in range(NT)]
ITEMS += [("dt", 0, h, None, 0) for h in range(2)]
MIX0 = len(ITEMS)
for _c in range(XT):
    ITEMS += [("x", _c, h, 12 + _c, 0) for h in range(2)]
for _c in range(WT):
    ITEMS += [("r", _c, h, 20 + _c, 0) for h in range(2)]
for _c in range(WT):
    ITEMS += [("gb", _c, h, 24 + _c, 0) for h in range(2)]
for _u in range(2):
    ITEMS += [("z", _u, t, 28 + 2 * _u, 0) for t in range(NT)]
MIX1 = len(ITEMS)
for _b in range(3):
    for _c in range(KD):
        for _h in range(2):
            ITEMS += [("g", _c, _h, UIX[("gate", _b * D + _c * P)], 0, _b),
                      ("b", _c, _h, UIX[("branch", _b, _c // 4)], _c % 4, _b)]
OUT0 = len(ITEMS)
for _t in range(NT):
    ITEMS += [("o", _t, q, OUTU + q, 0) for q in range(4)]
DVE_KINDS = ("k", "b", "o")
IDX = {}
for _i, _it in enumerate(ITEMS):
    IDX[(_it[0],) + _it[1:3] + _it[5:]] = _i
FIRST_OF, LAST_OF = {}, {}
for _i, _it in enumerate(ITEMS):
    for _u in ((_it[3], _it[3] + 1) if _it[0] in "vz" else (_it[3],)):
        FIRST_OF.setdefault(_u, _i)
        LAST_OF[_u] = _i
SLOT, BEFORE, ARRIVAL = {}, {}, {}
_in_slot = [None] * NSLOT
_arrived = [0] * NSLOT
for _u in range(len(UNITS)):
    _free = [-1 if w is None else LAST_OF[w] for w in _in_slot]
    if _u in (8, 10, 28, 30):
        _s = min((0, 2), key=lambda s: max(_free[s], _free[s + 1]))
    elif _u in (9, 11, 29, 31):
        _s = SLOT[_u - 1] + 1
    else:
        _s = min(range(NSLOT), key=lambda s: _free[s])
    BEFORE[_u] = _in_slot[_s]
    SLOT[_u] = _s
    _in_slot[_s] = _u
    _arrived[_s] += 1
    ARRIVAL[_u] = _arrived[_s]
SPLITS = [u for u, v in enumerate(UNITS) if v[0] in ("in", "gate")]
SPLIT_NO = {u: n for n, u in enumerate(SPLITS)}
DRAINED = []
_cnt = [0, 0]
for _it in ITEMS:
    _e = 1 if _it[0] in DVE_KINDS else 0
    _cnt[_e] += 1
    DRAINED.append((_e, _cnt[_e]))

ATT = [("p", hp, kb) for hp in range(PAIRS) for kb in reversed(range(KB))]
ATT += [("d", 0, kb) for kb in reversed(range(PAST // P + 1))]
NATT = len(ATT)


def att_at(u):
    return (3 * u) // 2


JOBS = {}


def job(item, *what):
    JOBS.setdefault(item, []).append(what)


AHEAD = 3
for _u in SPLITS:
    job(max(0, FIRST_OF[_u] - AHEAD), "split", _u)
job(4, "params", 0)
_v0 = IDX[("v", 0, 0)]
for _i in range(4):
    job(_v0 + 1 + _i, "past_keys", _i)
for _i in range(NT):
    job(_v0 + 5 + _i, "keys_out", _i)
job(MIX0, "dt_turn", 0)
for _s in range(MIX1 - MIX0):
    for _u in range(NATT):
        if att_at(_u) + 3 == _s:
            job(MIX0 + _s, "att_values", _u)
    for _u in range(NATT):
        if att_at(_u) + 2 == _s:
            job(MIX0 + _s, "att_after", _u)
    for _u in range(NATT):
        if att_at(_u) == _s:
            job(MIX0 + _s, "att_scores", _u)
for _c in range(XT):
    job(IDX[("x", _c, 1)] + 1, "conv", _c)
for _c in range(WT):
    job(IDX[("r", _c, 1)] + 1, "conv", XT + _c)
for _u in range(NATT):
    job(MIX0 + att_at(_u) + 1, "att_soft", _u)


def mix3(s):
    return MIX1 + 2 * s


job(mix3(1), "state_in", 0)
for _i in range(XT):
    job(mix3(_i // 4), "silu", _i)
for _t in range(NT):
    job(mix3(2 + _t // 2), "ssm_turn", _t)
LRU0, SSD0 = 8, 22
for _c in range(WT):
    job(MIX1 + LRU0 + 4 * _c, "lru", _c)
    job(MIX1 + LRU0 + 4 * _c + 2, "lru_scan", _c)
for _c in range(NT):
    _s = MIX1 + SSD0 + 8 * _c
    job(_s, "ssd_decay", _c)
    job(_s + 2, "ssd_exp", _c)
    job(_s + 3, "ssd_mix", _c)
    job(_s + 5, "ssd_norm", _c)
    job(_s + 8, "ssd_turn", _c)
job(MIX1 + SSD0 + 4, "tails_turn", 0)
job(MIX1 + SSD0 + 8 * 3 + 7, "state_out", 0)
job(MIX1 + SSD0 + 8 * 4 + 7, "state_out", 1)
for _t in range(NT):
    job(OUT0 + 4 * (_t + 1), "ffn_norm", _t)
    job(OUT0 + 4 * (_t + 1) + 2, "ffn_turn", _t)
NITEM = len(ITEMS)
for _i, _j in [(k, v) for k, v in JOBS.items() if k > NITEM]:
    JOBS.setdefault(NITEM, []).extend(_j)
    del JOBS[_i]


def trunk_and_experts(nc, a, o):
    ctx = ExitStack()
    with ctx:
        def sb(name, shape, dt=F32):
            return ctx.enter_context(nc.sbuf_tensor(name, shape, dt))

        def ps(name, shape):
            return ctx.enter_context(nc.psum_tensor(name, shape, F32))

        def sem(name):
            return ctx.enter_context(nc.semaphore(name))

        arena_at = -(-nc.sbuf_base // 32) * 32
        arena = sb("arena", [P, ARENA])
        cut = [0]

        def take(n):
            cut[0] += n
            assert cut[0] <= ARENA, cut[0]
            return cut[0] - n

        def at(off, *dims):
            n = 1
            for d in dims:
                n *= d
            v = arena[:, off:off + n]
            if len(dims) == 2:
                v = v.rearrange("p (a b) -> p a b", a=dims[0])
            if len(dims) == 3:
                v = v.rearrange("p (a b c) -> p a b c", a=dims[0], b=dims[1])
            return v

        def region(name, off, n, dt=F32R):
            return nc.alloc_sbuf_tensor_at(name, [P, n], dt, offset=arena_at + 4 * off)[:, :]

        ident, u_incl, u_strict, neg_l, neg_ones, ones, att_mask, ssd_mask = (
            at(take(P), P) for _ in range(8))
        cpar = at(take(NPAR), NPAR)
        cst = at(take(NST), NST)
        rowc = at(take(60), 60)
        tails = at(take(TAILS), TAILS)
        small = take(SMALL)
        gains_mix = region("gains_mix", take(KD), KD, F32)
        w_dt_off = take(KD * 8)
        w_dt = at(w_dt_off, KD, 8)
        h_off = take(NT * D)
        h = at(h_off, NT, D)
        merged_off = take(KD * T)
        merged = at(merged_off, KD, T)
        ring_off = take(NSLOT * 2048)
        ring = region("ring", ring_off, NSLOT * 2048, F32)
        ring8 = [at(ring_off + 2048 * s, KD, 256) for s in range(NSLOT)]
        ring4 = [at(ring_off + 2048 * s, WT, 512) for s in range(NSLOT)]
        raw = [ring[:, 2048 * s:2048 * s + 1024].rearrange("p (k n) -> p k n", k=KD) for s in range(NSLOT)]
        ring_r = region("ring_r", ring_off, NSLOT * 2048).rearrange("p (s k n) -> p s k n", s=2 * NSLOT, k=KD)
        rest_r = [ring_r[:, 2 * s] for s in range(NSLOT)]
        high_r = [ring_r[:, 2 * s + 1] for s in range(NSLOT)]

        def pair_r(s, part, k):
            return ring_r[:, 2 * s + part:2 * s + part + 3:2, k, :]

        front = cut[0]
        uh_off = take(KD * T)
        u_high_r = region("u_high_r", uh_off, KD * T).rearrange("p (k t) -> p k t", k=KD)
        u_rest = region("u_rest", h_off, KD * T, F32).rearrange("p (k t) -> p k t", k=KD)
        u_rest_r = region("u_rest_r", h_off, KD * T).rearrange("p (k t) -> p k t", k=KD)
        q2_off = take(2 * PAIRS * T)
        q2 = at(q2_off, 2, PAIRS, T)
        oAT = at(q2_off, PAIRS, T)
        oBT = at(q2_off + PAIRS * T, PAIRS, T)
        xconv_off = take(XT * TW)
        xconv = at(xconv_off, XT, TW)
        oCT = at(xconv_off, WT, T)
        xc_off = take(WT * TW)
        xc = at(xc_off, WT, TW)
        gb_off = take(WT * TW)
        gb = at(gb_off, WT, TW)
        z2_off = take(NT * W)
        z2 = at(z2_off, NT, W)
        x0 = at(xc_off, NT, D)
        tmp = cut[0]
        kT = at(take(PAIRS * T), PAIRS, T)
        kpT = at(take(PAIRS * PAST), PAIRS, PAST)
        att_a = [at(take(1024), 2, 512) for _ in range(2)]
        att_b = [at(take(1024), 2, 512) for _ in range(2)]
        att_s = at(take(1024), 2, 512)
        xp_off = [take(584) for _ in range(2)]
        xp = [at(x, 584) for x in xp_off]
        v_sb = at(merged_off, NT, W)
        vp_sb = at(merged_off + NT * W, KB, W)
        kp_raw = at(xconv_off, KB, W)
        st_a = at(xconv_off + 2048, P)
        st_b = at(xconv_off + 2048 + P, P)
        junk = at(xconv_off + 2048 + 2 * P, D)
        ko = [at(z2_off + 512 + 512 * i, W) for i in range(2)]
        dtT = at(z2_off + 1536, T)
        assert xc_off + NT * D <= z2_off + 512
        cut[0] = tmp
        xs_tok = at(take(NT * W), NT, W)
        b_tok = at(take(NT * 256), NT, 256)
        xdt_off = take(W)
        xdt = at(xdt_off, HEADS, HD)
        ss_in = at(xdt_off, WT, P)
        xdd_off = take(W)
        xdd = at(xdd_off, HEADS, HD)
        y_off_sb = at(take(W), W)
        y_sb = at(take(W), W)
        th = [at(xdd_off + TW * i, TW) for i in range(2)]
        lt_off = take(5 * TW)
        lt = [at(lt_off + TW * i, TW) for i in range(5)]
        lru_w = at(take(8 * P), 2, WT, P)
        gsb = [at(take(HALF), HALF) for _ in range(2)]
        gtmp = [at(take(HALF), HALF) for _ in range(2)]
        hS = at(take(W), W)
        e_flat = lt_off
        m_flat = lt_off + 1024
        td_flat = lt_off + 2048
        hT = at(xc_off, W)
        tz = at(xc_off + W, W)
        h_out = at(td_flat, WT, P)
        tail_row = at(gb_off, P)

        wexp_off = front
        w_g = at(wexp_off, 2 * KD, DE)
        w_u = at(wexp_off + 8192, 2 * KD, DE)
        w_d = at(wexp_off + 16384, 2 * (DE // P), D)
        cut[0] = front + 24576
        u2 = [at(take(D), D) for _ in range(2)]
        u2T = [at(take(D), KD, P) for _ in range(2)]
        g_ffn = at(take(D), D)
        lg = at(take(NT * 36), NT, 36)
        v_top = [at(take(NT), NT) for _ in range(2)]
        rank_full = at(take(NT * NE), NT, NE)
        e_masked = at(take(NT * NE), NT, NE)
        e_cand = at(take(NT * NE), NT, NE)
        e_hot = [at(take(NT * NE), NT, NE) for _ in range(2)]
        hot_sum = at(take(NT * NE), NT, NE)
        g_cand = at(take(NT * NG), NT, NG)
        g_hot = at(take(NT * NG), NT, NG)
        g_max, g_key, e_key, p_sel = (at(take(NT), NT) for _ in range(4))
        for_exp = at(take(NT * NG + NT), NT * NG + NT)
        tile_base = at(take((NT + 1) * NE), NT + 1, NE)
        n_over, over_incl, over_start = (at(take(NE), NE) for _ in range(3))
        rank, first, expert, blk_no, place, col, side, is_over, div = (at(take(2 * NT), 2, NT) for _ in range(9))
        eid = at(take(OVB), OVB)
        cut[0] = merged_off
        xg = at(take(D), D)
        xT = at(take(D), KD, P)
        hidT = at(take(DE), DE // P, P)
        gate_t = at(take(DE), DE)
        gate_a = at(take(DE), DE)
        hid = at(take(DE), DE)
        y_out_sb = at(take(D), D)
        y_back = [[at(take(D), D) for _ in range(2)] for _ in range(2)]
        g_fin = at(take(D), D)
        over_cmp = at(take(OVB * NE), OVB, NE)
        assert cut[0] <= front

        cs = [small]

        def tiny(*dims):
            n = 1
            for d in dims:
                n *= d
            cs[0] += n
            assert cs[0] <= small + SMALL
            return at(cs[0] - n, *dims)

        w_dt_h = tiny(KD * 8)
        ssq = tiny(8)
        rstd = tiny(8)
        sp_x, sp_e, sp_u, sp_l, sp_m, sp_p = (tiny(44) for _ in range(6))
        dt_sb = sp_x[:, 0:40].rearrange("p (t h) -> p t h", t=NT)
        a_exp = tiny(8)
        dA = tiny(NT, 8)
        ls4 = tiny(WT)
        ls4n = tiny(WT)
        acs = tiny(8)
        ea = tiny(8)
        cd = tiny(8)
        ssy = tiny(2)
        rsy = tiny(2)
        ss2 = tiny(8)
        rs2 = tiny(8)

        w_r = tiny(KD, 36)
        w_dt_hr = region("w_dt_high_r", small, KD * 8).rearrange("p (k n) -> p k n", k=KD)
        w_dt_rr = region("w_dt_rest_r", w_dt_off, KD * 8).rearrange("p (k n) -> p k n", k=KD)
        w_sel = tiny(2, NT)
        ss3 = tiny(8)
        rs3 = tiny(8)
        rev = tiny(NE)
        iota_f = tiny(NE)
        tok_id = tiny(NT).bitcast(I32)
        iota_i = tiny(NE).bitcast(I32)
        no_token = tiny(NPC).bitcast(I32)
        tab = tiny(NPC).bitcast(I32)
        idx_now = tiny(1).bitcast(I32)
        tab_row = tiny(2 * NT).bitcast(I32)
        y_row = tiny(2 * NT).bitcast(I32)
        over_total = tiny(1).bitcast(I32)
        over_expert = tiny(OVB).bitcast(I32)
        assert cs[0] <= small + SMALL

        pj = ps("pj", [P, 2, 512])
        za = ps("za", [P, 2, 512])
        zb = ps("zb", [P, 2, 512])
        zz = [za, zb]
        oa = ps("oa", [P, 512])
        ms = ps("ms", [P, 512])

        u2d = nc.dram_tensor("u2d", (T, D), F32, kind="Internal").ap()
        tabd = nc.dram_tensor("tabd", (P * NPC, 1), I32, kind="Internal").ap()
        yd = nc.dram_tensor("yd", ((NE + OVB) * BLK, D), F32, kind="Internal").ap()

        names = """
            vp_in
            consts gmix_in ut_u ut_h high_r rest_r wdt_r gb_zero par_in bc_in kp_in par_up ssq_r
            var_r std_r xn_r pe_par xt_ps ut_r pj_full pj_act pj_dve kp_ps kp_r ko_ps ko_r dt_ps dt_raw dt_r
            z_r nab_r ln_e l_r sp_r zw_r s_sum w_r_ o_r o_out q_zero masked conv_c silu_t silu_r turn_ps
            turn_r lruw_in lruw_z lru_ps lru_tr lru_ac lru_gt lru_m2 lru_mu lru_h ob_r hs_ps hs_r td_r
            dec_ps acs_r d_r ea_r em_r e_r m_r xdt_r xdd_r tz_r mix_ps hcd_r h_r y0_r y1_r y2_r yg_r ssy_r
            vy_r sy_r yn_r yt_ps oc_r so_ps so_r so_out v_out tl_out tl_ps tl_r gm_r gains_in u2_a u2_r
            u2t_ps u2t_r lg_ps lg_r ids_r tab_moved tab_out fexp_in fexp_r hots_r rank_ps rows_r over_r idx_r
            idx_seen xg_in xt2_ps xt2_a xt2_d wg_in wu_in wd_in gate_done up_done gate_th gate_mul hid_r
            hidt_ps hidt_r down_a down_b y_a y_b y_out experts_done hy_r fin_r fin_out dve_c pool_c sp_dve
            sp_act lru_pool side_dma""".split()
        S = {n: sem(n) for n in names}
        x_in = [sem(f"x_in{t}") for t in range(NT)]
        back_in = [sem(f"back_in{s}") for s in range(2)]
        ko_out = [sem(f"ko_out{s}") for s in range(2)]
        u2_out = [sem(f"u2_out{s}") for s in range(2)]
        unit_in = [sem(f"unit_in{s}") for s in range(NSLOT)]

        def drained(n):
            e, v = DRAINED[n]
            return S["pj_act"] if e == 0 else S["pj_dve"], v

        def wait_drained(eng, n):
            s, v = drained(n)
            eng.wait_ge(s, v)

        def rows(ap, lo, n):
            return ap.rearrange("l (r p) -> (l r) p", p=P)[lo:lo + n, :]

        def att_view(buf, u):
            kind, hp, kb = ATT[u]
            if kind == "p":
                return buf[:, :, 0:SEQ - kb * P]
            return buf[0:P if kb < KB else DEC, 0, :]

        def tw_cols(t):
            o0, n = TT[t]
            lo = o0 if t < NT - 1 else SAMP
            return lo, n

        block = ctx.enter_context(nc.Block())

        @block.sync
        def _(sp):
            def reload_x(t):
                o0, n = TT[t]
                src = a["x_prompt"][0, o0:o0 + n, :] if t < NT - 1 else a["x_sample"][0]
                sp.dma_start(h[0:n, t, :], src).then_inc(x_in[t], 16)

            for t, (o0, n) in enumerate(TT):
                src = a["x_prompt"][0, o0:o0 + n, :] if t < NT - 1 else a["x_sample"][0]
                sp.dma_start(x0[0:n, t, :], src).then_inc(x_in[t], 16)
            for u, unit in enumerate(UNITS):
                if u == 4:
                    sp.dma_start(kp_raw, a["cache_sb_k"][0, 0].rearrange("(b p) h d -> p b (h d)", p=P)
                                 ).then_inc(S["kp_in"], 16)
                if u == 8:
                    sp.dma_start(vp_sb, a["cache_sb_v"][0, 0].rearrange("(b p) h d -> p b (h d)", p=P)
                                 ).then_inc(S["vp_in"], 16)
                if BEFORE[u] is not None:
                    sp.wait_ge(S["pj_full"], LAST_OF[BEFORE[u]] + 1)
                if u == OUTU + 2:
                    sp.wait_ge(S["pj_full"], IDX[("g", KD - 1, 1, 2)] + 1)
                    reload_x(0)
                if unit[0] == "branch":
                    src = a["w_branch_out"][0, unit[1] * W:(unit[1] + 1) * W, 512 * unit[2]:512 * unit[2] + 512]
                    dst = ring4[SLOT[u]]
                else:
                    w = a[{"in": "w_in", "gate": "w_gate", "out": "w_out"}[unit[0]]]
                    src = w[0, :, unit[1]:unit[1] + (256 if unit[0] == "out" else P)]
                    dst = (ring8 if unit[0] == "out" else raw)[SLOT[u]]
                sp.dma_start(dst, src.rearrange("(k p) n -> p k n", p=P)).then_inc(unit_in[SLOT[u]], 16)
            for t in range(1, NT):
                reload_x(t)
            def load_experts(i, first, second):
                for j, w in enumerate((first, second)):
                    if j == 0 and i is not None:
                        sp.wait_ge(S["gate_done"], i)
                    sp.dma_start(w_g[:, KD * j:KD * (j + 1), :], expert_w("w_expert_gate", w)).then_inc(S["wg_in"], 16)
                for j, w in enumerate((first, second)):
                    if j == 0 and i is not None:
                        sp.wait_ge(S["up_done"], i)
                    sp.dma_start(w_u[:, KD * j:KD * (j + 1), :], expert_w("w_expert_up", w)).then_inc(S["wu_in"], 16)
                for j, w in enumerate((first, second)):
                    if j == 0 and i is not None:
                        sp.wait_ge(S["down_b"], i)
                    sp.dma_start(w_d[:, DE // P * j:DE // P * (j + 1), :], expert_w("w_expert_down", w)
                                 ).then_inc(S["wd_in"], 16)

            def expert_w(name, e):
                rows_e = D if name != "w_expert_down" else DE
                v = a[name][0].rearrange("e (k p) f -> p (e k) f", p=P)
                k = rows_e // P
                return v[:, bass.ds(e * k, k), :]

            def store_y(i):
                sp.wait_ge(S["y_a"], i + 1)
                sp.wait_ge(S["y_b"], i + 1)
                sp.dma_start(yd[bass.ds(i * P, P), :], y_out_sb).then_inc(S["y_out"], 16)

            sp.wait_ge(S["gm_r"], 4 * KD)
            sp.wait_ge(S["so_out"], 32)
            sp.wait_ge(S["tl_out"], 16 * 6)
            load_experts(None, 0, EPAIRS)
            with sp.Fori(0, EPAIRS - 1) as i:
                load_experts(i + 1, i + 1, i + 1 + EPAIRS)
                store_y(i)
            store_y(EPAIRS - 1)
            sp.wait_ge(S["y_out"], 16 * EPAIRS)
            sp.wait_ge(S["over_r"], 1)
            total = sp.value_load(over_total[0:1, 0:1], min_val=0, max_val=OVB)
            for j in range(OPAIRS):
                with sp.If(total > j):
                    ids = [sp.value_load(over_expert[0:1, c:c + 1], min_val=0, max_val=NE - 1)
                           for c in (j, j + OPAIRS)]
                    load_experts(EPAIRS + j, *ids)
                    store_y(EPAIRS + j)
                    sp.wait_ge(S["y_out"], 16 * (EPAIRS + j + 1))
            sp.sem_inc(S["experts_done"], 1)
            sp.wait_ge(S["fin_out"], 16 * NT)
            for name, n in (("v_out", 2), ("tl_out", 6), ("so_out", 2)):
                sp.wait_ge(S[name], 16 * n)
            for s in range(2):
                sp.wait_ge(ko_out[s], 16 * ((NT + 1 - s) // 2))
                sp.wait_ge(u2_out[s], 16 * ((NT + 1 - s) // 2))

        @block.tensor
        def _(pe):
            def gain_turn():
                pe.wait_ge(S["gmix_in"], 16)
                pe.transpose(ms[:, 0:KD], st_a[0:KD, :], ident[0:KD, 0:KD]).then_inc(S["pe_par"], 1)

            def params(_):
                pe.wait_ge(S["consts"], 7)
                pe.wait_ge(S["par_in"], 16 * (len(PAR_ROWS) + 2))
                pe.wait_ge(S["par_up"], 1)
                pe.transpose(ms[:, 0:NPAR], st_a[0:NPAR, :], ident[0:NPAR, 0:NPAR])
                pe.transpose(oa[:, 0:NST], st_b[0:NST, :], ident[0:NST, 0:NST]).then_inc(S["pe_par"], 1)

            def x_turn(t):
                n = TT[t][1]
                z = zz[t % 2]
                if t == 0:
                    pe.wait_ge(S["consts"], 1)
                pe.wait_ge(S["xn_r"], t + 1)
                if t >= 2:
                    pe.wait_ge(S["ut_u"], t - 1)
                for k in range(KD):
                    m = pe.transpose(z[:, k // 4, (k % 4) * P:(k % 4) * P + n], x0[0:n, t, k * P:(k + 1) * P],
                                     ident[0:n, 0:n])
                m.then_inc(S["xt_ps"], 1)

            def product(out, left, right, k):
                pe.matmul(out, left[0], right[0], start=k == 0, stop=False)
                pe.matmul(out, left[0], right[1], start=False, stop=False)
                return pe.matmul(out, left[1], right[0], start=False, stop=k == KD - 1)

            def item(n):
                it = ITEMS[n]
                kind, c, hh, u, ct = it[:5]
                if n >= 2:
                    wait_drained(pe, n - 2)
                s = SLOT.get(u)
                if u in SPLIT_NO:
                    pe.wait_ge(S["rest_r"], SPLIT_NO[u + 1 if kind in "vz" else u] + 1)
                elif u is not None:
                    pe.wait_ge(unit_in[s], 16 * ARRIVAL[u])
                cols = slice(hh * HALF, (hh + 1) * HALF)
                bank = pj[:, n % 2, :]
                if kind == "b":
                    br = it[5]
                    if hh == 0 and c == 0:
                        pe.wait_ge(*[(S["o_out"], PAIRS + 1), (S["ob_r"], WT), (S["oc_r"], NT)][br])
                    src = [oAT, oBT, oCT][br]
                    for k in range(WT):
                        m = pe.matmul(bank[:, 0:HALF], ring4[s][:, k, ct * P:(ct + 1) * P],
                                      src[:, k, cols], start=k == 0, stop=k == WT - 1)
                elif kind == "o":
                    o0, rows_n = TT[c]
                    if n == OUT0:
                        pe.wait_ge(S["gm_r"], 32)
                    for k in range(KD):
                        m = pe.matmul(bank[0:rows_n, 0:256], merged[:, k, o0:o0 + rows_n], ring8[s][:, k, :],
                                      start=k == 0, stop=k == KD - 1)
                elif kind in "vz":
                    o0, rows_n = TT[hh]
                    out = bank[0:rows_n, 0:256].rearrange("p (a b) -> p a b", a=2)
                    for k in range(KD):
                        uh, ur = (x[:, k, o0:o0 + rows_n] for x in (u_high_r, u_rest_r))
                        m = product(out, (uh, ur), (pair_r(s, 1, k), pair_r(s, 0, k)), k)
                elif kind == "dt":
                    if hh == 0:
                        pe.wait_ge(S["wdt_r"], 2)
                    for k in range(KD):
                        m = product(bank[0:8, 0:HALF], (w_dt_hr[:, k, :], w_dt_rr[:, k, :]),
                                    (u_high_r[:, k, cols], u_rest_r[:, k, cols]), k)
                else:
                    for k in range(KD):
                        m = product(bank[:, 0:HALF], (high_r[s][:, k, :], rest_r[s][:, k, :]),
                                    (u_high_r[:, k, cols], u_rest_r[:, k, cols]), k)
                m.then_inc(S["pj_full"], 1)

            def past_keys(i):
                if i == 0:
                    pe.wait_ge(S["kp_in"], 16)
                    pe.wait_ge(S["ut_r"], NT)
                z = zz[i // 2]
                for b in range(KB):
                    m = pe.transpose(z[:, i % 2, b * P:(b + 1) * P], kp_raw[:, b, i * P:(i + 1) * P], ident)
                m.then_inc(S["kp_ps"], 1)

            def keys_out(t):
                o0, n = TT[t]
                z = [oa, ms][t % 2]
                if t == 0:
                    pe.wait_ge(S["par_up"], 3)
                    wait_drained(pe, IDX[("k", WT - 1, 1)])
                if t >= 2:
                    pe.wait_ge(S["ko_r"], t - 1)
                for c in range(WT):
                    m = pe.transpose(z[0:n, c * P:(c + 1) * P], kT[:, c, o0:o0 + n], ident)
                m.then_inc(S["ko_ps"], 1)

            def dt_turn(_):
                wait_drained(pe, IDX[("dt", 0, 1)])
                pe.wait_ge(S["ko_r"], NT)
                for t, (o0, n) in enumerate(TT):
                    m = pe.transpose(ms[0:n, t * 8:t * 8 + 8], dtT[0:8, o0:o0 + n], ident[0:8, 0:8])
                m.then_inc(S["dt_ps"], 1)

            def att_scores(u):
                kind, hp, kb = ATT[u]
                z = zz[u % 2]
                if u == 0:
                    wait_drained(pe, IDX[("q", WT - 1, 1)])
                    wait_drained(pe, IDX[("k", WT - 1, 1)])
                    pe.wait_ge(S["q_zero"], 1)
                    pe.wait_ge(S["kp_r"], 4)
                if u >= 2:
                    pe.wait_ge(S["w_r_"], u - 1)
                if kind == "p":
                    q0 = kb * P
                    for e in range(2):
                        m = pe.matmul(z[:, e, 0:SEQ - q0], kT[:, hp, q0:q0 + P], q2[:, e, hp, q0:SEQ],
                                      start=True, stop=False, skip_group_check=True)
                else:
                    n = P if kb < KB else DEC
                    for c in range(PAIRS):
                        key = kpT[:, c, kb * P:(kb + 1) * P] if kb < KB else kT[:, c, SEQ:T]
                        m = pe.matmul(z[0:n, 0, c * P:(c + 1) * P], key, q2[:, :, c, SEQ:T],
                                      start=c == 0, stop=False, skip_group_check=True)
                m.then_inc(S["z_r"], 1)

            def att_after(u):
                kind, hp, kb = ATT[u]
                z = zz[u % 2]
                pe.wait_ge(S["sp_r"], u + 1)
                first = kb == (KB - 1 if kind == "p" else KB)
                if not first or kind == "d":
                    pe.wait_ge(S["s_sum"], u)
                b = att_b[u % 2]
                sums = att_s
                if kind == "p":
                    n = SEQ - kb * P
                    for e in range(2):
                        if not first:
                            pe.matmul(z[:, e, P:n], neg_ones, sums[:, e, 0:n - P],
                                      start=False, stop=False, skip_group_check=True)
                        m = pe.matmul(z[:, e, 0:n], neg_l, b[:, e, 0:n],
                                      start=False, stop=True, skip_group_check=True)
                else:
                    n = P if kb < KB else DEC
                    if not first:
                        pe.matmul(z[:, 0, :], neg_ones, sums[:, 0, :], start=False, stop=False,
                                  skip_group_check=True)
                    m = pe.matmul(z[0:n, 0, :], neg_l[0:n, 0:n], b[0:n, 0, :], start=False, stop=True,
                                  skip_group_check=True)
                m.then_inc(S["zw_r"], 1)

            def att_values(u):
                kind, hp, kb = ATT[u]
                w = att_a[u % 2]
                if u == 0:
                    wait_drained(pe, IDX[("v", 1, NT - 1)])
                    pe.wait_ge(S["vp_in"], 16)
                    pe.wait_ge(S["ko_r"], NT)
                pe.wait_ge(S["w_r_"], u + 1)
                if kind == "p":
                    q0 = kb * P
                    if kb == KB - 1 and hp > 0:
                        pe.wait_ge(S["o_out"], hp)
                    for e in range(2):
                        c0 = (2 * hp + e) * HD
                        m = pe.matmul(oa[e * HD:(e + 1) * HD, q0:SEQ], v_sb[:, kb, c0:c0 + HD],
                                      w[:, e, 0:SEQ - q0], start=kb == KB - 1, stop=kb == 0,
                                      skip_group_check=True)
                else:
                    if kb == KB:
                        pe.wait_ge(S["o_out"], PAIRS)
                    n = P if kb < KB else DEC
                    for c in range(PAIRS):
                        for e in range(2):
                            c0 = (2 * c + e) * HD
                            v = vp_sb[:, kb, c0:c0 + HD] if kb < KB else v_sb[0:n, kb, c0:c0 + HD]
                            w0 = c * P + e * HD
                            m = pe.matmul(oa[e * HD:(e + 1) * HD, c * HD:(c + 1) * HD], v,
                                          w[0:n, 0, w0:w0 + HD], start=kb == KB and c == 0, stop=kb == 0,
                                          skip_group_check=True)
                m.then_inc(S["o_r"], 1)

            def state_in(_):
                pe.wait_ge(S["lruw_in"], 16 * (2 * HEADS + 1))
                pe.wait_ge(S["dt_raw"], 1)
                for j in range(WT):
                    m = pe.transpose(ms[:, j * P:(j + 1) * P], ss_in[:, j, :], ident)
                m.then_inc(S["hs_ps"], 1)

            def ssm_turn(t):
                lo, n = tw_cols(t)
                if t == 0:
                    pe.wait_ge(S["silu_r"], XT)
                    pe.wait_ge(S["hs_r"], 1)
                    pe.wait_ge(S["o_out"], PAIRS + 1)
                else:
                    pe.wait_ge(S["turn_r"], 2 * t)
                for j in range(6):
                    z = ms if j < WT else oa
                    m = pe.transpose(z[0:n, (j % WT) * P:(j % WT + 1) * P], xconv[:, j, lo:lo + n], ident)
                m.then_inc(S["turn_ps"], 1)

            def lru(c):
                if c == 0:
                    pe.wait_ge(S["lruw_in"], 16 * (2 * HEADS + 1))
                    pe.wait_ge(S["conv_c"], XT + WT)
                else:
                    pe.wait_ge(S["lru_tr"], 2 * c)
                for g in range(2):
                    for hh in range(2):
                        m = pe.matmul(zz[g][:, hh, 0:TW // 2], lru_w[:, g, c, :],
                                      xc[:, c, hh * (TW // 2):(hh + 1) * (TW // 2)], start=True, stop=True)
                m.then_inc(S["lru_ps"], 1)

            def ssd_decay(c):
                o0, n = TT[c]
                pe.wait_ge(S["td_r"], c + 1)
                if c == 0:
                    pe.wait_ge(S["lru_tr"], 2 * WT)
                else:
                    pe.wait_ge(S["m_r"], c)
                    pe.wait_ge(S["ea_r"], c)
                td = at(td_flat, HEADS, n)
                if n == P:
                    for b in range(2):
                        pe.matmul(za[:, b, :], ones[0:n, :], td[0:n, b * 4:(b + 1) * 4, :], start=True, stop=True)
                else:
                    pe.matmul(za[:, 0, :], ones[0:n, :], td[0:n, :, :], start=True, stop=True)
                pe.matmul(zb[0:n, 0, 256:264], u_incl[0:n, 0:n], dA[0:n, c, :], start=True, stop=True)
                lo, _ = tw_cols(c)
                for g in range(GROUPS):
                    m = pe.matmul(zb[0:n, 0, g * n:(g + 1) * n], xconv[:, 4 + g, lo:lo + n],
                                  xconv[:, 6 + g, lo:lo + n], start=True, stop=True)
                m.then_inc(S["dec_ps"], 1)

            def ssd_mix(c):
                o0, n = TT[c]
                lo, _ = tw_cols(c)
                pe.wait_ge(S["m_r"], c + 1)
                pe.wait_ge(S["xdd_r"], c + 1)
                if c == 0:
                    pe.wait_ge(S["turn_r"], 2 * NT)
                else:
                    pe.wait_ge(S["h_r"], c)
                    pe.wait_ge(S["oc_r"], c)
                    if c == NT - 1:
                        pe.wait_ge(S["so_r"], 1)
                m_sb = at(m_flat, HEADS, n)
                for hd in range(HEADS):
                    pe.matmul(zb[0:n, 1, hd * HD:(hd + 1) * HD], m_sb[0:n, hd, :], xdt[0:n, hd, :],
                              start=True, stop=True)
                if c > 0:
                    state = hT if c < NT - 1 else hS
                    for g in range(GROUPS):
                        pe.matmul(oa[0:n, g * 256:(g + 1) * 256], xconv[:, 6 + g, lo:lo + n],
                                  state[:, g * 256:(g + 1) * 256], start=True, stop=True)
                for g in range(GROUPS):
                    m = pe.matmul(ms[:, g * 256:(g + 1) * 256], b_tok[0:n, c, g * P:(g + 1) * P],
                                  xdd[0:n, 4 * g:4 * g + 4, :], start=True, stop=True)
                m.then_inc(S["mix_ps"], 1)

            def ssd_turn(c):
                o0, n = TT[c]
                pe.wait_ge(S["yn_r"], c + 1)
                if c == 0:
                    pe.wait_ge(S["tl_r"], 1)
                for j in range(WT):
                    m = pe.transpose(oa[:, j * P:j * P + n], y_sb[0:n, j * P:(j + 1) * P], ident[0:n, 0:n])
                m.then_inc(S["yt_ps"], 1)

            def tails_turn(_):
                pe.wait_ge(S["lru_h"], 2 * WT)
                pe.wait_ge(S["turn_r"], 2 * NT)
                pe.transpose(oa[0:TAILS, 0:P], tails, ident).then_inc(S["tl_ps"], 1)

            def state_out(i):
                pe.wait_ge(S["h_r"], NT - 1 + i)
                state = [hT, hS][i]
                for j in range(WT):
                    m = pe.transpose(ms[:, j * P:(j + 1) * P], state[:, j * P:(j + 1) * P], ident)
                m.then_inc(S["so_ps"], 1)

            def ffn_turn(t):
                o0, n = TT[t]
                z = zz[t % 2]
                pe.wait_ge(S["u2_r"], t + 1)
                if t >= 2:
                    pe.wait_ge(S["u2t_r"], t - 1)
                for k in range(KD):
                    m = pe.transpose(z[:, k // 4, (k % 4) * P:(k % 4) * P + n], u2[t % 2][0:n, k * P:(k + 1) * P],
                                     ident[0:n, 0:n])
                m.then_inc(S["u2t_ps"], 1)
                if t == 0:
                    pe.wait_ge(S["side_dma"], 48)
                    pe.wait_ge(S["so_r"], 2)
                pe.wait_ge(S["u2t_r"], t + 1)
                for k in range(KD):
                    m = pe.matmul(ms[0:n, t * 36:(t + 1) * 36], u2T[t % 2][:, k, 0:n], w_r[:, k, :],
                                  start=k == 0, stop=k == KD - 1)
                m.then_inc(S["lg_ps"], 1)

            def expert_pair(i, before=True):
                pe.wait_ge(S["xg_in"], (i + 1) * 16)
                if before:
                    pe.wait_ge(S["hidt_r"], i)
                for k in range(KD):
                    z = oa if k < KD // 2 else ms
                    m = pe.transpose(z[:, (k % 4) * P:(k % 4 + 1) * P], xg[:, k * P:(k + 1) * P], ident)
                m.then_inc(S["xt2_ps"], 1)
                pe.wait_ge(S["xt2_a"], i + 1)
                pe.wait_ge(S["xt2_d"], i + 1)
                for b, (w, loaded, done) in enumerate(((w_g, "wg_in", "gate_done"), (w_u, "wu_in", "up_done"))):
                    pe.wait_ge(S[loaded], (i + 1) * 32)
                    for k in range(KD):
                        for j in range(2):
                            m = pe.matmul(za[j * BLK:(j + 1) * BLK, b, :], xT[:, k, j * BLK:(j + 1) * BLK],
                                          w[:, j * KD + k, :], start=k == 0, stop=k == KD - 1)
                    m.then_inc(S[done], 1)
                pe.wait_ge(S["hid_r"], i + 1)
                for k in range(DE // P):
                    m = pe.transpose(oa[:, k * P:(k + 1) * P], hid[:, k * P:(k + 1) * P], ident)
                m.then_inc(S["hidt_ps"], 1)
                pe.wait_ge(S["hidt_r"], i + 1)
                pe.wait_ge(S["wd_in"], (i + 1) * 32)
                for q, (done, free) in enumerate((("down_a", "y_a"), ("down_b", "y_b"))):
                    if before:
                        pe.wait_ge(S[free], i)
                    for k in range(DE // P):
                        for j in range(2):
                            m = pe.matmul(zb[j * BLK:(j + 1) * BLK, q, :], hidT[:, k, j * BLK:(j + 1) * BLK],
                                          w_d[:, j * (DE // P) + k, q * 512:(q + 1) * 512],
                                          start=k == 0, stop=k == DE // P - 1)
                    m.then_inc(S[done], 1)

            def ranks():
                pe.wait_ge(S["hots_r"], 1)
                pe.matmul(ms[:, 0:NT * NE], u_strict, hot_sum, start=True, stop=True)
                pe.matmul(ms[:, NT * NE:2 * NT * NE], ones, hot_sum, start=True, stop=True
                          ).then_inc(S["rank_ps"], 1)

            steps = {f.__name__: f for f in (past_keys, keys_out, dt_turn, att_scores, att_after, att_values,
                                             state_in, ssm_turn, lru, ssd_decay, ssd_mix, ssd_turn, tails_turn,
                                             state_out, ffn_turn, params)}
            for t in range(NT):
                x_turn(t)
                if t == 0:
                    gain_turn()
            pe.wait_ge(S["ut_r"], NT)
            for n in range(NITEM + 1):
                for name, i in JOBS.get(n, []):
                    if name in steps:
                        steps[name](i)
                if n < NITEM:
                    item(n)
            ranks()
            expert_pair(0, before=False)
            with pe.Fori(1, EPAIRS) as i:
                expert_pair(i)
            pe.wait_ge(S["over_r"], 1)
            total = pe.value_load(over_total[0:1, 0:1], min_val=0, max_val=OVB)
            for j in range(OPAIRS):
                with pe.If(total > j):
                    expert_pair(EPAIRS + j)

        @block.scalar
        def _(act):
            act.dma_start(st_a[0:KD, :], a["g_mix"][0].rearrange("(r p) -> r p", p=P)).then_inc(S["gmix_in"], 16)

            def x_norm(t):
                n = TT[t][1]
                act.wait_ge(x_in[t], 16)
                act.activation(junk[0:n, :], x0[0:n, t, :], ACT.Square, accum_out=ssq[0:n, t:t + 1]
                               ).then_inc(S["ssq_r"], 1)
                act.wait_ge(S["var_r"], t + 1)
                act.activation(rstd[0:n, t:t + 1], ssq[0:n, t:t + 1], ACT.Sqrt).then_inc(S["std_r"], 1)

            def gain_up():
                act.wait_ge(S["pe_par"], 1)
                act.activation(gains_mix, ms[:, 0:KD], ACT.Copy).then_inc(S["par_up"], 1)

            def u_split(t):
                o0, n = TT[t]
                act.wait_ge(S["ut_u"], t + 1)
                act.activation(u_high_r[:, :, o0:o0 + n], u_rest[:, :, o0:o0 + n], ACT.Copy).then_inc(S["ut_h"], 1)

            def split(u):
                s = SLOT[u]
                act.wait_ge(unit_in[s], 16 * ARRIVAL[u])
                act.activation(high_r[s], raw[s], ACT.Copy).then_inc(S["high_r"], 1)

            def params(_):
                act.wait_ge(S["par_in"], 16 * (len(PAR_ROWS) + 2))
                act.activation(w_dt_hr, w_dt, ACT.Copy).then_inc(S["wdt_r"], 1)
                act.wait_ge(S["pe_par"], 2)
                act.wait_ge(S["ut_u"], NT)
                act.activation(cpar, ms[:, 0:NPAR], ACT.Copy).then_inc(S["par_up"], 1)
                act.activation(cst, oa[:, 0:NST], ACT.Copy).then_inc(S["par_up"], 1)

            def item(n):
                it = ITEMS[n]
                kind, c, hh = it[:3]
                if kind in DVE_KINDS:
                    return
                act.wait_ge(S["pj_full"], n + 1)
                bank = pj[:, n % 2, :]
                lo = hh * HALF
                if kind == "q":
                    if n == 0:
                        act.wait_ge(S["q_zero"], 1)
                    act.activation(q2[0:HD, 0, c, lo:lo + HALF], bank[0:HD, 0:HALF], ACT.Copy, scale=HD ** -0.5)
                    m = act.activation(q2[HD:P, 1, c, lo:lo + HALF], bank[HD:P, 0:HALF], ACT.Copy,
                                       scale=HD ** -0.5)
                elif kind in "vz":
                    t, r = hh, TT[hh][1]
                    if n == IDX[("z", 0, 0)]:
                        act.wait_ge(ko_out[0], 16 * 3)
                        act.wait_ge(ko_out[1], 16 * 2)
                        act.wait_ge(S["dt_ps"], 1)
                    dst = v_sb if kind == "v" else z2
                    m = act.activation(dst[0:r, t, 256 * c:256 * (c + 1)], bank[0:r, 0:256], ACT.Copy,
                                       scale=1.0 if kind == "v" else 0.5)
                elif kind == "dt":
                    if hh == 0:
                        act.wait_ge(S["xt_ps"], NT)
                    m = act.activation(dtT[0:8, lo:lo + HALF], bank[0:8, 0:HALF], ACT.Copy)
                elif kind in ("x", "r"):
                    j = c + (XT if kind == "r" else 0)
                    dst = xp[j % 2]
                    if j < 2 and hh == 0:
                        act.wait_ge(S["masked"], 1)
                    if j >= 2 and hh == 0:
                        act.wait_ge(S["conv_c"], j - 1)
                    if hh == 0:
                        m = act.activation(dst[:, GAP:GAP + HALF], bank[:, 0:HALF], ACT.Copy)
                    else:
                        act.activation(dst[:, GAP + HALF:GAP + SEQ], bank[:, 0:SEQ - HALF], ACT.Copy)
                        m = act.activation(dst[:, SAMP + GAP:SAMP + GAP + DEC], bank[:, SEQ - HALF:HALF], ACT.Copy)
                elif kind == "gb":
                    if hh == 0:
                        m = act.activation(gb[:, c, 0:HALF], bank[:, 0:HALF], ACT.Copy)
                    else:
                        act.activation(gb[:, c, HALF:SEQ], bank[:, 0:SEQ - HALF], ACT.Copy)
                        m = act.activation(gb[:, c, SAMP:SAMP + DEC], bank[:, SEQ - HALF:HALF], ACT.Copy)
                elif kind == "g":
                    br = it[5]
                    k = (n - MIX1) // 2
                    if k == 0:
                        act.wait_ge(S["conv_c"], XT + WT)
                        act.wait_ge(S["s_sum"], NATT)
                    if k >= 2:
                        wait_drained(act, n - 3)
                    j = PAR["b_gate"] + br * KD + c
                    m = act.activation(gsb[k % 2], bank[:, 0:HALF], ACT.Tanh, scale=0.5, bias=cpar[:, j:j + 1])
                m.then_inc(S["pj_act"], 1)
                if n == IDX[("v", 1, NT - 1)]:
                    act.wait_ge(*drained(n))
                    act.dma_start(o["v_p"][0, 0].rearrange("(t p) h d -> p t (h d)", p=P),
                                  v_sb[:, 0:NT - 1, :]).then_inc(S["v_out"], 16)
                    act.dma_start(o["v_s"][0, 0].rearrange("s h d -> s (h d)"),
                                  v_sb[0:DEC, NT - 1, :]).then_inc(S["v_out"], 16)

            def keys_out(t):
                o0, n = TT[t]
                act.wait_ge(S["ko_ps"], t + 1)
                if t == 0:
                    act.wait_ge(S["xt_ps"], NT)
                if t >= 2:
                    act.wait_ge(ko_out[t % 2], 16 * (t // 2))
                act.activation(ko[t % 2][0:n, :], [oa, ms][t % 2][0:n, :], ACT.Copy).then_inc(S["ko_r"], 1)
                act.wait_ge(S["ko_r"], t + 1)
                dst = o["k_p"][0, 0, o0:o0 + n] if t < NT - 1 else o["k_s"][0, 0]
                act.dma_start(dst.rearrange("s h d -> s (h d)"), ko[t % 2][0:n, :]).then_inc(ko_out[t % 2], 16)

            def dt_turn(_):
                act.wait_ge(S["sp_dve"], 1)
                act.activation(sp_e, sp_e, ACT.Exp).then_inc(S["sp_act"], 1)
                act.activation(a_exp, rowc[:, 8:16], ACT.Exp).then_inc(S["sp_act"], 1)
                act.wait_ge(S["sp_dve"], 2)
                act.activation(sp_l, sp_u, ACT.Ln).then_inc(S["sp_act"], 1)

            def att_scores(u):
                b = att_view(att_a[u % 2], u)
                act.wait_ge(S["nab_r"], u + 1)
                act.activation(b, b, ACT.Exp).then_inc(S["ln_e"], 1)
                act.wait_ge(S["ln_e"], u + 1)
                act.activation(b, b, ACT.Ln, bias=1.0).then_inc(S["l_r"], 1)

            def att_after(u):
                act.wait_ge(S["zw_r"], u + 1)
                act.activation(att_view(att_a[u % 2], u), att_view(zz[u % 2], u), ACT.Exp).then_inc(S["w_r_"], 1)

            def att_values(u):
                kind, hp, kb = ATT[u]
                if kb == 0:
                    act.wait_ge(S["o_r"], u + 1)
                    if kind == "p":
                        act.activation(oAT[:, hp, 0:SEQ], oa[:, :], ACT.Copy).then_inc(S["o_out"], 1)
                    else:
                        act.activation(oAT[:, :, SEQ:T], oa[:, 0:PAIRS * HD].rearrange("p (c q) -> p c q", c=PAIRS),
                                       ACT.Copy).then_inc(S["o_out"], 1)

            def silu(i):
                if i == 0:
                    act.wait_ge(S["o_r"], NATT)
                    act.wait_ge(S["s_sum"], NATT)
                if i >= 2:
                    act.wait_ge(S["silu_r"], i - 1)
                act.wait_ge(S["conv_c"], i + 1)
                act.activation(th[i % 2], xconv[:, i, :], ACT.Tanh).then_inc(S["silu_t"], 1)

            def state_in(_):
                act.wait_ge(S["hs_ps"], 1)
                act.activation(hS, ms[:, :], ACT.Copy).then_inc(S["hs_r"], 1)

            def ssm_turn(t):
                n = TT[t][1]
                act.wait_ge(S["turn_ps"], t + 1)
                act.activation(b_tok[0:n, t, :], oa[0:n, 0:256], ACT.Copy).then_inc(S["turn_r"], 1)

            def both(z):
                return z[:, :, 0:TW // 2]

            def lru(c):
                r, i, la, m, gl = [x.rearrange("p (a b) -> p a b", a=2) for x in lt]
                act.wait_ge(S["lru_ps"], c + 1)
                if c > 0:
                    act.wait_ge(S["ob_r"], c)
                ba = PAR["lru_b_a"] + c
                bx = PAR["lru_b_x"] + c
                act.activation(r, both(za), ACT.Tanh, scale=0.5, bias=cpar[:, ba:ba + 1]).then_inc(S["lru_tr"], 1)
                act.activation(i, both(zb), ACT.Tanh, scale=0.5, bias=cpar[:, bx:bx + 1]).then_inc(S["lru_tr"], 1)
                act.wait_ge(S["lru_tr"], 2 * c + 2)
                act.activation(la, r, ACT.Exp, scale=ls4[:, c:c + 1], bias=ls4[:, c:c + 1]
                               ).then_inc(S["lru_ac"], 1)
                act.activation(r, r, ACT.Tanh, scale=ls4n[:, c:c + 1], bias=ls4n[:, c:c + 1]
                               ).then_inc(S["lru_ac"], 1)
                act.wait_ge(S["lru_pool"], 4 * c + 3)
                act.activation(gl, gl, ACT.Tanh, scale=GELU_C).then_inc(S["lru_gt"], 1)

            def lru_scan(c):
                r, _, _, m, _ = [x.rearrange("p (a b) -> p a b", a=2) for x in lt]
                act.wait_ge(S["lru_m2"], c + 1)
                act.activation(r, m, ACT.Sqrt).then_inc(S["lru_mu"], 1)

            def ssd_decay(c):
                n = TT[c][1]
                act.wait_ge(S["acs_r"], c + 1)
                if c == 0:
                    act.wait_ge(S["ob_r"], WT)
                act.activation(ea[0:n, :], acs[0:n, :], ACT.Exp)
                act.wait_ge(S["d_r"], c + 1)
                if c > 1:
                    act.wait_ge(S["hcd_r"], c - 1)
                last = za[:, :, :].rearrange("p a (b l) -> p (a b) l", l=P)[:, :, P - 1] if n == P else \
                    za[:, 0, :].rearrange("p (b l) -> p b l", l=n)[:, :, n - 1]
                act.activation(cd, last, ACT.Exp).then_inc(S["ea_r"], 1)

            def ssd_exp(c):
                n = TT[c][1]
                act.wait_ge(S["em_r"], c + 1)
                e = at(e_flat, HEADS, n)[0:n]
                act.activation(e, e, ACT.Exp).then_inc(S["e_r"], 1)
                if c > 0:
                    act.wait_ge(S["yg_r"], c)
                act.activation(tz[0:n, :], z2[0:n, c, :], ACT.Tanh).then_inc(S["tz_r"], 1)

            def ssd_norm(c):
                n = TT[c][1]
                act.wait_ge(S["yg_r"], c + 1)
                for g in range(GROUPS):
                    m = act.activation(y_off_sb[0:n, g * 256:(g + 1) * 256], y_sb[0:n, g * 256:(g + 1) * 256],
                                       ACT.Square, accum_out=ssy[0:n, g:g + 1])
                m.then_inc(S["ssy_r"], 1)
                act.wait_ge(S["vy_r"], c + 1)
                act.activation(rsy[0:n, :], ssy[0:n, :], ACT.Sqrt).then_inc(S["sy_r"], 1)

            def tails_turn(_):
                act.wait_ge(S["tl_ps"], 1)
                act.wait_ge(S["ob_r"], WT)
                act.activation(tail_row[0:TAILS, :], oa[0:TAILS, 0:P], ACT.Copy).then_inc(S["tl_r"], 1)
                act.wait_ge(S["tl_r"], 1)
                for q, tag in enumerate("ps"):
                    r0 = q * 36
                    act.dma_start(o["lru_conv_" + tag][0, 0].rearrange("k (r p) -> (k r) p", p=P),
                                  tail_row[r0:r0 + 12, :]).then_inc(S["tl_out"], 16)
                    act.dma_start(o["ssm_conv_" + tag][0, 0].rearrange("k (r p) -> (k r) p", p=P),
                                  tail_row[r0 + 12:r0 + 36, :]).then_inc(S["tl_out"], 16)
                    act.dma_start(o["lru_h_" + tag][0, 0].rearrange("(r p) -> r p", p=P),
                                  tail_row[72 + 4 * q:76 + 4 * q, :]).then_inc(S["tl_out"], 16)

            def state_out(i):
                act.wait_ge(S["so_ps"], i + 1)
                act.wait_ge(S["dec_ps"], NT - 1 + i)
                if i == 1:
                    act.wait_ge(S["so_out"], 16)
                act.activation(h_out, ms[:, :].rearrange("p (j n) -> p j n", j=WT), ACT.Copy).then_inc(S["so_r"], 1)
                act.wait_ge(S["so_r"], i + 1)
                act.dma_start(o["ssm_h_" + "ps"[i]][0, 0].rearrange("(j q) p n -> (q p) j n", q=2), h_out
                              ).then_inc(S["so_out"], 16)

            def ffn_norm(t):
                n = TT[t][1]
                wait_drained(act, IDX[("o", t, 3)])
                if t >= 2:
                    act.wait_ge(S["u2t_ps"], t - 1)
                    act.wait_ge(u2_out[t % 2], 16 * (t // 2))
                act.activation(u2[t % 2][0:n, :], h[0:n, t, :], ACT.Square, accum_out=ss2[0:n, t:t + 1]
                               ).then_inc(S["ssq_r"], 1)
                act.wait_ge(S["var_r"], NT + t + 1)
                act.activation(rs2[0:n, t:t + 1], ss2[0:n, t:t + 1], ACT.Sqrt).then_inc(S["std_r"], 1)

            def ffn_turn(t):
                o0, n = TT[t]
                act.wait_ge(S["u2_r"], t + 1)
                act.dma_start(u2d[o0:o0 + n, :], u2[t % 2][0:n, :]).then_inc(u2_out[t % 2], 16)
                act.wait_ge(S["u2t_ps"], t + 1)
                if t >= 2:
                    act.wait_ge(S["lg_ps"], t - 1)
                act.activation(u2T[t % 2][:, :, 0:n], zz[t % 2][:, :, :].rearrange("p a (b l) -> p (a b) l", l=P)
                               [:, :, 0:n], ACT.Copy).then_inc(S["u2t_r"], 1)

            def routing():
                act.wait_ge(S["fexp_in"], 1)
                act.activation(for_exp, for_exp, ACT.Exp).then_inc(S["fexp_r"], 1)

            def expert_pair(i, before=True):
                act.wait_ge(S["xt2_ps"], i + 1)
                act.activation(xT[:, 0:KD // 2, :], oa[:, :].rearrange("p (k l) -> p k l", k=4), ACT.Copy
                               ).then_inc(S["xt2_a"], 1)
                act.wait_ge(S["gate_done"], i + 1)
                act.activation(gate_t, za[:, 0, :], ACT.Tanh, scale=0.5).then_inc(S["gate_th"], 1)
                act.wait_ge(S["down_a"], i + 1)
                if before:
                    act.wait_ge(S["y_out"], i * 16)
                act.activation(y_out_sb[:, 0:512], zb[:, 0, :], ACT.Copy).then_inc(S["y_a"], 1)

            def final(t):
                o0, n = TT[t]
                act.wait_ge(S["hy_r"], t + 1)
                act.activation(y_back[t % 2][0][0:n, :], h[0:n, t, :], ACT.Square, accum_out=ss3[0:n, t:t + 1]
                               ).then_inc(S["ssq_r"], 1)
                act.wait_ge(S["var_r"], 2 * NT + t + 1)
                act.activation(rs3[0:n, t:t + 1], ss3[0:n, t:t + 1], ACT.Sqrt).then_inc(S["std_r"], 1)
                act.wait_ge(S["fin_r"], t + 1)
                dst = o["y_p"][0, o0:o0 + n, :] if t < NT - 1 else o["y_s"][0]
                act.dma_start(dst, h[0:n, t, :]).then_inc(S["fin_out"], 16)

            steps = {f.__name__: f for f in (keys_out, dt_turn, att_scores, att_after, att_values, silu, state_in,
                                             ssm_turn, lru, lru_scan, ssd_decay, ssd_exp, ssd_norm, tails_turn,
                                             state_out, ffn_norm, ffn_turn, split, params)}
            for t in range(NT):
                x_norm(t)
                if t == 0:
                    gain_up()
                if t > 0:
                    u_split(t - 1)
            u_split(NT - 1)
            for n in range(NITEM + 1):
                for name, i in JOBS.get(n, []):
                    if name in steps:
                        steps[name](i)
                if n < NITEM:
                    item(n)
            routing()
            expert_pair(0, before=False)
            with act.Fori(1, EPAIRS) as i:
                expert_pair(i)
            act.wait_ge(S["over_r"], 1)
            total = act.value_load(over_total[0:1, 0:1], min_val=0, max_val=OVB)
            for j in range(OPAIRS):
                with act.If(total > j):
                    expert_pair(EPAIRS + j)
            for t in range(NT):
                final(t)

        def bc(v, *shape):
            return v.to_broadcast(list(shape))

        @block.vector
        def _(dve):
            links = [0]

            def link(ins):
                links[0] += 1
                ins.then_inc(S["dve_c"], 1)
                dve.wait_ge(S["dve_c"], links[0])

            def x_norm(t):
                n = TT[t][1]
                dve.wait_ge(S["ssq_r"], t + 1)
                dve.tensor_scalar(ssq[0:n, t:t + 1], ssq[0:n, t:t + 1], 1.0 / D, EPS, ALU.mult, ALU.add
                                  ).then_inc(S["var_r"], 1)
                dve.wait_ge(S["std_r"], t + 1)
                link(dve.reciprocal(rstd[0:n, t:t + 1], rstd[0:n, t:t + 1]))
                dve.tensor_scalar(x0[0:n, t, :], x0[0:n, t, :], rstd[0:n, t:t + 1], None, ALU.mult
                                  ).then_inc(S["xn_r"], 1)

            def x_turn(t):
                o0, n = TT[t]
                z = zz[t % 2]
                dve.wait_ge(S["xt_ps"], t + 1)
                if t == 0:
                    dve.wait_ge(S["par_up"], 1)
                for b in range(2):
                    m = dve.tensor_tensor(u_rest[:, 4 * b:4 * b + 4, o0:o0 + n],
                                          z[:, b, :].rearrange("p (k l) -> p k l", k=4)[:, :, 0:n],
                                          bc(gains_mix[:, 4 * b:4 * b + 4].unsqueeze(2), P, 4, n), ALU.mult)
                m.then_inc(S["ut_u"], 1)

            def u_split(t):
                o0, n = TT[t]
                dve.wait_ge(S["ut_h"], t + 1)
                v = slice(o0, o0 + n)
                dve.tensor_tensor(u_rest_r[:, :, v], u_rest[:, :, v], u_high_r[:, :, v], ALU.subtract
                                  ).then_inc(S["ut_r"], 1)

            def split(u):
                s = SLOT[u]
                dve.wait_ge(S["high_r"], SPLIT_NO[u] + 1)
                dve.tensor_tensor(rest_r[s], raw[s], high_r[s], ALU.subtract).then_inc(S["rest_r"], 1)

            def params(_):
                par_half()
                dve.wait_ge(S["wdt_r"], 1)
                dve.tensor_tensor(w_dt_rr, w_dt, w_dt_hr, ALU.subtract
                                  ).then_inc(S["wdt_r"], 1)

            def par_half():
                dve.wait_ge(S["par_up"], 3)
                for name, k in (("b_gate", 24), ("ssm_conv_w", 40), ("lru_b_a", 8)):
                    v = cpar[:, PAR[name]:PAR[name] + k]
                    m = dve.tensor_scalar(v, v, 0.5, None, ALU.mult)
                lam = cpar[:, PAR["lru_lambda"]:PAR["lru_lambda"] + 4]
                dve.tensor_scalar(sp_x[:, 40:44], lam, -1.0, None, ALU.mult)

            def item(n):
                it = ITEMS[n]
                kind, c, hh = it[:3]
                if kind not in DVE_KINDS:
                    return
                dve.wait_ge(S["pj_full"], n + 1)
                bank = pj[:, n % 2, :]
                lo = hh * HALF
                if kind == "k":
                    m = dve.tensor_copy(kT[:, c, lo:lo + HALF], bank[:, 0:HALF])
                elif kind == "b":
                    br = it[5]
                    k = (n - MIX1) // 2
                    wait_drained(dve, n - 1)
                    dst = merged[:, c, lo:lo + HALF] if br == 0 else gtmp[k % 2]
                    if k == 0:
                        dve.wait_ge(S["v_out"], 32)
                    if br > 0:
                        kk = k - 2 * KD
                        if kk >= 2:
                            dve.wait_ge(S["gm_r"], kk - 1)
                    m = dve.scalar_tensor_tensor(out=dst, in0=gsb[k % 2], scalar=1.0, in1=bank[:, 0:HALF],
                                                 op0=ALU.add, op1=ALU.mult)
                elif kind == "o":
                    t, q = c, hh
                    r = TT[t][1]
                    if q == 0:
                        dve.wait_ge(x_in[t], 32)
                    v = h[0:r, t, 256 * q:256 * (q + 1)]
                    m = dve.scalar_tensor_tensor(out=v, in0=bank[0:r, 0:256], scalar=0.5, in1=v,
                                                 op0=ALU.mult, op1=ALU.add)
                m.then_inc(S["pj_dve"], 1)

            def past_keys(i):
                dve.wait_ge(S["kp_ps"], i + 1)
                dve.tensor_copy(kpT[:, i, :], zz[i // 2][:, i % 2, :]).then_inc(S["kp_r"], 1)

            def dt_turn(_):
                dve.wait_ge(S["dt_ps"], 1)
                dve.wait_ge(S["bc_in"], 16 * 5)
                link(dve.memset(sp_x[:, 0:40], 0.0))
                link(dve.tensor_tensor(dt_sb[:, 0:4, :], ms[:, 0:32].rearrange("p (t e) -> p t e", t=4),
                                       bc(rowc[:, 0:8].unsqueeze(1), P, 4, 8), ALU.add))
                dve.tensor_tensor(dt_sb[0:DEC, 4, :], ms[0:DEC, 32:40], rowc[0:DEC, 0:8], ALU.add
                                  ).then_inc(S["dt_raw"], 1)
                dve.wait_ge(S["dt_raw"], 1)
                link(dve.tensor_scalar(sp_p, sp_x, 0.0, None, ALU.max))
                dve.scalar_tensor_tensor(out=sp_e, in0=sp_p, scalar=-2.0, in1=sp_x, op0=ALU.mult, op1=ALU.add
                                         ).then_inc(S["sp_dve"], 1)
                dve.wait_ge(S["sp_act"], 2)
                dve.tensor_scalar(sp_u, sp_e, 1.0, None, ALU.add).then_inc(S["sp_dve"], 1)
                dve.wait_ge(S["sp_dve"], 2)
                dve.wait_ge(S["sp_act"], 3)
                link(dve.tensor_scalar(sp_u, sp_u, -1.0, None, ALU.add))
                link(dve.tensor_scalar(sp_m, sp_u, 0.0, None, ALU.is_equal))
                link(dve.tensor_tensor(sp_l, sp_l, sp_m, ALU.add))
                link(dve.tensor_tensor(sp_u, sp_u, sp_m, ALU.add))
                link(dve.reciprocal(sp_u, sp_u))
                link(dve.tensor_tensor(sp_l, sp_l, sp_e, ALU.mult))
                link(dve.tensor_tensor(sp_l, sp_l, sp_u, ALU.mult))
                link(dve.tensor_tensor(sp_x, sp_l, sp_p, ALU.add))
                dve.tensor_scalar(ls4, sp_x[:, 40:44], -4.0, None, ALU.mult)
                dve.tensor_scalar(ls4n, sp_x[:, 40:44], 4.0, None, ALU.mult)
                dve.scalar_tensor_tensor(out=dA, in0=dt_sb, scalar=-1.0, in1=bc(a_exp.unsqueeze(1), P, NT, 8),
                                         op0=ALU.mult, op1=ALU.mult).then_inc(S["dt_r"], 1)

            def att_scores(u):
                kind, hp, kb = ATT[u]
                z = zz[u % 2]
                dve.wait_ge(S["z_r"], u + 1)
                if kind == "p":
                    dve.tensor_tensor(z[:, :, 0:P], z[:, :, 0:P], bc(att_mask.unsqueeze(1), P, 2, P), ALU.add
                                      ).then_inc(S["masked"], 1)
                    dve.wait_ge(S["masked"], u + 2)
                elif kb == KB:
                    v = z[0:DEC, 0, :].rearrange("p (c q) -> p c q", c=HEADS)
                    dve.tensor_tensor(v, v, bc(att_mask[0:DEC, 0:DEC].unsqueeze(1), DEC, HEADS, DEC), ALU.add
                                      ).then_inc(S["masked"], 1)
                    dve.wait_ge(S["masked"], u + 2)
                if u >= 2:
                    dve.wait_ge(S["o_r"], u - 1)
                    dve.wait_ge(S["s_sum"], u - 1)
                link(dve.tensor_scalar(att_view(att_b[u % 2], u), att_view(z, u), 0.0, None, ALU.max))
                dve.scalar_tensor_tensor(out=att_view(att_a[u % 2], u), in0=att_view(att_b[u % 2], u),
                                         scalar=-2.0, in1=att_view(z, u), op0=ALU.mult, op1=ALU.add
                                         ).then_inc(S["nab_r"], 1)

            def att_soft(u):
                b, ln = att_view(att_b[u % 2], u), att_view(att_a[u % 2], u)
                dve.wait_ge(S["l_r"], u + 1)
                dve.tensor_tensor(b, b, ln, ALU.add).then_inc(S["sp_r"], 1)

            def conv(j):
                src = xp[j % 2]
                ssm = j < XT
                c = j if ssm else j - XT
                kind = "x" if ssm else "r"
                nt = XT if ssm else WT
                base = 12 if ssm else 0
                wait_drained(dve, IDX[(kind, c, 1)])
                link(dve.tensor_copy(src[:, SAMP:SAMP + GAP],
                                     cst[:, base:base + GAP * nt].rearrange("p (k c) -> p k c", k=GAP)[:, :, c]))
                for q, lo in enumerate((SEQ, SAMP + DEC)):
                    v = tails[:, q * 36 + base:q * 36 + base + GAP * nt].rearrange("p (k c) -> p k c", k=GAP)
                    dve.tensor_copy(v[:, :, c], src[:, lo:lo + GAP])
                dst = (xconv if ssm else xc)[:, c, :]
                w0 = PAR["ssm_conv_w" if ssm else "lru_conv_w"] + c
                b0 = PAR["ssm_conv_b" if ssm else "lru_conv_b"] + c
                if j == 0:
                    dve.wait_ge(S["kp_ps"], 4)
                link(dve.tensor_scalar(dst, src[:, 0:TW], cpar[:, w0:w0 + 1], cpar[:, b0:b0 + 1],
                                       ALU.mult, ALU.add))
                for k in range(1, CW):
                    w = w0 + k * nt
                    m = dve.scalar_tensor_tensor(out=dst, in0=src[:, k:k + TW], scalar=cpar[:, w:w + 1], in1=dst,
                                                 op0=ALU.mult, op1=ALU.add)
                    if k < CW - 1:
                        link(m)
                m.then_inc(S["conv_c"], 1)

            def silu(i):
                dve.wait_ge(S["silu_t"], i + 1)
                dve.scalar_tensor_tensor(out=xconv[:, i, :], in0=th[i % 2], scalar=1.0, in1=xconv[:, i, :],
                                         op0=ALU.add, op1=ALU.mult).then_inc(S["silu_r"], 1)

            def ssm_turn(t):
                n = TT[t][1]
                if t == 0:
                    dve.wait_ge(S["s_sum"], NATT)
                dve.wait_ge(S["turn_ps"], t + 1)
                dve.tensor_copy(xs_tok[0:n, t, :], ms[0:n, :]).then_inc(S["turn_r"], 1)

            def lru(c):
                r, i, la, m, gl = lt
                dve.wait_ge(S["lru_tr"], 2 * c + 2)
                dve.scalar_tensor_tensor(out=i, in0=i, scalar=1.0, in1=xc[:, c, :], op0=ALU.add, op1=ALU.mult)
                dve.wait_ge(S["lru_pool"], 4 * c + 4)
                dve.wait_ge(S["lru_ac"], 2 * c + 2)
                dve.scalar_tensor_tensor(out=m, in0=m, scalar=1.0, in1=r, op0=ALU.add, op1=ALU.mult
                                         ).then_inc(S["lru_m2"], 1)

            def lru_scan(c):
                r, i, la, m, gl = lt
                dve.wait_ge(S["lru_mu"], c + 1)
                link(dve.scalar_tensor_tensor(out=i, in0=r, scalar=0.5, in1=i, op0=ALU.mult, op1=ALU.mult))
                h0 = PAR["state_lru_h"] + c
                dve.tensor_tensor_scan(m[:, 0:SEQ], la[:, 0:SEQ], i[:, 0:SEQ], 0.0, ALU.mult, ALU.add)
                link(dve.tensor_tensor_scan(m[:, SAMP:SAMP + DEC], la[:, SAMP:SAMP + DEC], i[:, SAMP:SAMP + DEC],
                                            cpar[:, h0:h0 + 1], ALU.mult, ALU.add))
                for q, last in enumerate((SEQ - 1, SAMP + DEC - 1)):
                    col = 72 + 4 * q + c
                    dve.tensor_copy(tails[:, col:col + 1], m[:, last:last + 1]).then_inc(S["lru_h"], 1)
                dve.wait_ge(S["lru_gt"], c + 1)
                link(dve.scalar_tensor_tensor(out=gl, in0=gl, scalar=1.0, in1=gb[:, c, :],
                                              op0=ALU.add, op1=ALU.mult))
                dve.scalar_tensor_tensor(out=oBT[:, c, 0:SEQ], in0=gl[:, 0:SEQ], scalar=0.5, in1=m[:, 0:SEQ],
                                         op0=ALU.mult, op1=ALU.mult)
                dve.scalar_tensor_tensor(out=oBT[:, c, SEQ:T], in0=gl[:, SAMP:SAMP + DEC], scalar=0.5,
                                         in1=m[:, SAMP:SAMP + DEC], op0=ALU.mult, op1=ALU.mult
                                         ).then_inc(S["ob_r"], 1)

            def ssd_decay(c):
                n = TT[c][1]
                e = at(e_flat, HEADS, n)[0:n]
                dve.wait_ge(S["dec_ps"], c + 1)
                dve.tensor_copy(acs[0:n, :], zb[0:n, 0, 256:264]).then_inc(S["acs_r"], 1)
                dve.wait_ge(S["acs_r"], c + 1)
                if c > 0:
                    dve.wait_ge(S["xdd_r"], c)
                src = za[0:n, :, :].rearrange("p a (b l) -> p (a b) l", l=P) if n == P else \
                    za[0:n, 0, :].rearrange("p (b l) -> p b l", l=n)
                dve.tensor_tensor(e, src, bc(acs[0:n, :].unsqueeze(2), n, HEADS, n), ALU.subtract
                                  ).then_inc(S["d_r"], 1)

            def ssd_exp(c):
                n = TT[c][1]
                e = at(e_flat, HEADS, n)[0:n]
                mm = at(m_flat, HEADS, n)[0:n]
                dve.wait_ge(S["e_r"], c + 1)
                if c > 0:
                    dve.wait_ge(S["mix_ps"], c)
                for g in range(GROUPS):
                    k = dve.tensor_tensor(mm[:, 4 * g:4 * g + 4, :], e[:, 4 * g:4 * g + 4, :],
                                          bc(zb[0:n, 0, g * n:(g + 1) * n].unsqueeze(1), n, 4, n), ALU.mult)
                k.then_inc(S["m_r"], 1)

            def ssd_mix(c):
                n = TT[c][1]
                y3 = y_sb[0:n, :].rearrange("p (e d) -> p e d", e=HEADS)
                t3 = y_off_sb[0:n, :].rearrange("p (e d) -> p e d", e=HEADS)
                dve.wait_ge(S["mix_ps"], c + 1)
                dve.wait_ge(S["ea_r"], c + 1)
                state = hT if c < NT - 1 else hS
                if c > 0:
                    dve.wait_ge(S["yt_ps"], c)
                    link(dve.tensor_tensor(t3, oa[0:n, :].rearrange("p (e d) -> p e d", e=HEADS),
                                           bc(ea[0:n, :].unsqueeze(2), n, HEADS, HD), ALU.mult))
                    dve.tensor_tensor(y_sb[0:n, :], zb[0:n, 1, :], y_off_sb[0:n, :], ALU.add
                                      ).then_inc(S["y0_r"], 1)
                    dve.wait_ge(S["hcd_r"], c)
                    dve.tensor_tensor(state, ms[:, :], state, ALU.add).then_inc(S["h_r"], 1)
                else:
                    dve.tensor_copy(y_sb[0:n, :], zb[0:n, 1, :]).then_inc(S["y0_r"], 1)
                    dve.tensor_copy(state, ms[:, :]).then_inc(S["h_r"], 1)
                dve.wait_ge(S["tz_r"], c + 1)
                dve.scalar_tensor_tensor(out=tz[0:n, :], in0=tz[0:n, :], scalar=1.0, in1=z2[0:n, c, :],
                                         op0=ALU.add, op1=ALU.mult).then_inc(S["y1_r"], 1)

            def ssd_norm(c):
                n = TT[c][1]
                dve.wait_ge(S["ssy_r"], c + 1)
                dve.tensor_scalar(ssy[0:n, :], ssy[0:n, :], 1.0 / 256, EPS, ALU.mult, ALU.add
                                  ).then_inc(S["vy_r"], 1)
                dve.wait_ge(S["sy_r"], c + 1)
                link(dve.reciprocal(rsy[0:n, :], rsy[0:n, :]))
                for g in range(GROUPS):
                    v = y_sb[0:n, g * 256:(g + 1) * 256]
                    k = dve.tensor_scalar(v, v, rsy[0:n, g:g + 1], None, ALU.mult)
                k.then_inc(S["yn_r"], 1)

            def ssd_turn(c):
                o0, n = TT[c]
                dve.wait_ge(S["yt_ps"], c + 1)
                g = PAR["ssm_norm_g"]
                dve.tensor_tensor(oCT[:, :, o0:o0 + n], oa[:, :].rearrange("p (j l) -> p j l", j=WT)[:, :, 0:n],
                                  bc(cpar[:, g:g + 4].unsqueeze(2), P, WT, n), ALU.mult).then_inc(S["oc_r"], 1)

            def ffn_norm(t):
                n = TT[t][1]
                dve.wait_ge(S["ssq_r"], NT + t + 1)
                dve.tensor_scalar(ss2[0:n, t:t + 1], ss2[0:n, t:t + 1], 1.0 / D, EPS, ALU.mult, ALU.add
                                  ).then_inc(S["var_r"], 1)
                dve.wait_ge(S["std_r"], NT + t + 1)
                link(dve.reciprocal(rs2[0:n, t:t + 1], rs2[0:n, t:t + 1]))
                dve.tensor_scalar(u2[t % 2][0:n, :], h[0:n, t, :], rs2[0:n, t:t + 1], None, ALU.mult
                                  ).then_inc(S["u2_a"], 1)

            def ffn_turn(t):
                n = TT[t][1]
                if t == 0:
                    link(dve.memset(lg, 0.0))
                dve.wait_ge(S["lg_ps"], t + 1)
                dve.tensor_tensor(lg[0:n, t, :], ms[0:n, t * 36:(t + 1) * 36], rowc[0:n, 24:60], ALU.add
                                  ).then_inc(S["lg_r"], 1)

            def per(v, k):
                return bc(v.unsqueeze(2), P, NT, k)

            def across(v, k=NT):
                return bc(v.unsqueeze(1), P, k, v.shape[-1])

            def one_hot(dst, values, top, cand, key, keys):
                k = values.shape[-1]
                link(dve.tensor_reduce(top, values, AXX, ALU.max))
                link(dve.tensor_tensor(cand, values, per(top, k), ALU.is_equal))
                link(dve.tensor_tensor(cand, cand, across(keys), ALU.mult))
                link(dve.tensor_reduce(key, cand, AXX, ALU.max))
                link(dve.tensor_tensor(dst, across(keys), per(key, k), ALU.is_equal))

            def floor_div(dst, src, d):
                link(dve.tensor_scalar(dst, src, 1.0 / d, 0.5 / d - 0.5, ALU.mult, ALU.add))
                link(dve.tensor_scalar(dst, dst, ROUND, None, ALU.add))
                link(dve.tensor_scalar(dst, dst, ROUND, None, ALU.subtract))

            def routing():
                g_lg, e_lg = lg[:, :, 0:NG], lg[:, :, NG:NG + NE]
                dve.wait_ge(S["lg_r"], NT)
                dve.wait_ge(S["ids_r"], 1)
                dve.tensor_copy(iota_f, iota_i)
                link(dve.tensor_scalar(rev, iota_i, -1.0, float(NE), ALU.mult, ALU.add))
                one_hot(g_hot, g_lg, g_max, g_cand, g_key, rev[:, 0:NG])
                link(dve.tensor_scalar(g_cand, g_hot, BIG, -BIG, ALU.mult, ALU.add))
                for t in range(NT):
                    m = dve.tensor_tensor(e_masked[:, t, :].rearrange("p (g e) -> p g e", g=NG),
                                          e_lg[:, t, :].rearrange("p (g e) -> p g e", g=NG),
                                          bc(g_cand[:, t, :].unsqueeze(2), P, NG, EPG), ALU.add)
                link(m)
                one_hot(e_hot[0], e_masked, v_top[0], e_cand, e_key, rev)
                link(dve.scalar_tensor_tensor(out=e_masked, in0=e_hot[0], scalar=-BIG, in1=e_masked,
                                              op0=ALU.mult, op1=ALU.add))
                one_hot(e_hot[1], e_masked, v_top[1], e_cand, e_key, rev)
                for s in range(2):
                    m = dve.memset(e_hot[s][DEC:P, NT - 1, :], 0.0)
                link(m)
                dve.tensor_tensor(hot_sum, e_hot[0], e_hot[1], ALU.add).then_inc(S["hots_r"], 1)
                dve.tensor_tensor(for_exp[:, 0:NT * NG].rearrange("p (t g) -> p t g", t=NT), g_lg, per(g_max, NG),
                                  ALU.subtract)
                dve.tensor_tensor(for_exp[:, NT * NG:], v_top[1], v_top[0], ALU.subtract).then_inc(S["fexp_in"], 1)
                dve.wait_ge(S["rank_ps"], 1)
                link(dve.memset(tile_base[:, 0, :], 0.0))
                for t in range(NT):
                    link(dve.tensor_tensor(tile_base[:, t + 1, :], tile_base[:, t, :],
                                           ms[:, (NT + t) * NE:(NT + t + 1) * NE], ALU.add))
                link(dve.tensor_tensor(rank_full, ms[:, 0:NT * NE].rearrange("p (t e) -> p t e", t=NT),
                                       tile_base[:, 0:NT, :], ALU.add))
                link(dve.tensor_scalar(n_over, tile_base[:, NT, :], -1.0, None, ALU.add))
                floor_div(n_over, n_over, BLK)
                link(dve.tensor_scalar(n_over, n_over, 0.0, None, ALU.max))
                link(dve.tensor_tensor_scan(over_incl, ones[:, 0:NE], n_over, 0.0, ALU.mult, ALU.add))
                link(dve.tensor_tensor(over_start, over_incl, n_over, ALU.subtract))
                for s in range(2):
                    for dst, v in ((rank, rank_full), (first, across(over_start)), (expert, across(iota_f))):
                        link(dve.tensor_tensor(e_cand, e_hot[s], v, ALU.mult))
                        link(dve.tensor_reduce(dst[:, s, :], e_cand, AXX, ALU.add))
                floor_div(div, rank, BLK)
                link(dve.scalar_tensor_tensor(out=place, in0=div, scalar=-float(BLK), in1=rank,
                                              op0=ALU.mult, op1=ALU.add))
                link(dve.tensor_scalar(is_over, div, 0.0, None, ALU.is_gt))
                link(dve.scalar_tensor_tensor(out=first, in0=first, scalar=-1.0, in1=div, op0=ALU.add, op1=ALU.add))
                link(dve.tensor_scalar(side, expert, float(EPAIRS), None, ALU.is_ge))
                link(dve.scalar_tensor_tensor(out=col, in0=side, scalar=-float(EPAIRS), in1=expert,
                                              op0=ALU.mult, op1=ALU.add))
                link(dve.tensor_scalar(div, first, float(OPAIRS), None, ALU.is_ge))
                link(dve.scalar_tensor_tensor(out=first, in0=div, scalar=-float(OPAIRS), in1=first,
                                              op0=ALU.mult, op1=ALU.add))
                link(dve.tensor_scalar(first, first, float(EPAIRS), None, ALU.add))
                for own, over in ((side, div), (col, first)):
                    link(dve.tensor_tensor(over, over, own, ALU.subtract))
                    link(dve.tensor_tensor(over, over, is_over, ALU.mult))
                    link(dve.tensor_tensor(own, own, over, ALU.add))
                link(dve.scalar_tensor_tensor(out=place, in0=side, scalar=float(BLK), in1=place,
                                              op0=ALU.mult, op1=ALU.add))
                flat = [v.rearrange("p s t -> p (s t)") for v in (place, col)]
                dve.scalar_tensor_tensor(out=tab_row, in0=flat[0], scalar=float(NPC), in1=flat[1],
                                         op0=ALU.mult, op1=ALU.add)
                dve.scalar_tensor_tensor(out=y_row, in0=flat[1], scalar=float(2 * BLK), in1=flat[0],
                                         op0=ALU.mult, op1=ALU.add).then_inc(S["rows_r"], 1)
                link(dve.tensor_tensor(over_cmp, bc(over_incl.unsqueeze(1), P, OVB, NE),
                                       bc(iota_f[:, 0:OVB].unsqueeze(2), P, OVB, NE), ALU.is_le))
                link(dve.tensor_reduce(eid, over_cmp, AXX, ALU.add))
                dve.tensor_scalar(over_expert, eid, float(NE - 1), None, ALU.min)
                dve.tensor_copy(over_total, over_incl[:, NE - 1:NE]).then_inc(S["over_r"], 1)
                dve.wait_ge(S["fexp_r"], 1)
                link(dve.tensor_reduce(p_sel, for_exp[:, 0:NT * NG].rearrange("p (t g) -> p t g", t=NT), AXX,
                                       ALU.add))
                link(dve.tensor_scalar(w_sel[:, 0, :], for_exp[:, NT * NG:], 1.0, None, ALU.add))
                link(dve.tensor_tensor(w_sel[:, 0, :], w_sel[:, 0, :], p_sel, ALU.mult))
                link(dve.reciprocal(w_sel[:, 0, :], w_sel[:, 0, :]))
                link(dve.tensor_tensor(w_sel[:, 1, :], w_sel[:, 0, :], for_exp[:, NT * NG:], ALU.mult))

            def expert_pair(i, before=True):
                dve.wait_ge(S["xt2_ps"], i + 1)
                dve.tensor_copy(xT[:, KD // 2:KD, :], ms[:, :].rearrange("p (k l) -> p k l", k=4)
                                ).then_inc(S["xt2_d"], 1)
                dve.wait_ge(S["gate_th"], i + 1)
                dve.scalar_tensor_tensor(out=gate_a, in0=gate_t, scalar=1.0, in1=za[:, 0, :],
                                         op0=ALU.add, op1=ALU.mult).then_inc(S["gate_mul"], 1)
                dve.wait_ge(S["gate_mul"], i + 1)
                dve.wait_ge(S["up_done"], i + 1)
                dve.scalar_tensor_tensor(out=hid, in0=gate_a, scalar=0.5, in1=za[:, 1, :],
                                         op0=ALU.mult, op1=ALU.mult).then_inc(S["hid_r"], 1)
                dve.wait_ge(S["hidt_ps"], i + 1)
                dve.tensor_copy(hidT, oa[:, :].rearrange("p (k l) -> p k l", k=4)).then_inc(S["hidt_r"], 1)
                dve.wait_ge(S["down_b"], i + 1)
                if before:
                    dve.wait_ge(S["y_out"], i * 16)
                dve.tensor_copy(y_out_sb[:, 512:D], zb[:, 1, :]).then_inc(S["y_b"], 1)

            def final(t):
                n = TT[t][1]
                hv = h[0:n, t, :]
                dve.wait_ge(back_in[t % 2], 32 * (t // 2 + 1))
                link(dve.scalar_tensor_tensor(out=hv, in0=y_back[t % 2][0][0:n, :], scalar=w_sel[0:n, 0, t:t + 1],
                                              in1=hv, op0=ALU.mult, op1=ALU.add))
                dve.scalar_tensor_tensor(out=hv, in0=y_back[t % 2][1][0:n, :], scalar=w_sel[0:n, 1, t:t + 1],
                                         in1=hv, op0=ALU.mult, op1=ALU.add).then_inc(S["hy_r"], 1)

            def final_norm(t):
                n = TT[t][1]
                hv = h[0:n, t, :]
                dve.wait_ge(S["ssq_r"], 2 * NT + t + 1)
                dve.tensor_scalar(ss3[0:n, t:t + 1], ss3[0:n, t:t + 1], 1.0 / D, EPS, ALU.mult, ALU.add
                                  ).then_inc(S["var_r"], 1)
                dve.wait_ge(S["std_r"], 2 * NT + t + 1)
                dve.wait_ge(S["gains_in"], 32)
                link(dve.reciprocal(rs3[0:n, t:t + 1], rs3[0:n, t:t + 1]))
                dve.scalar_tensor_tensor(out=hv, in0=hv, scalar=rs3[0:n, t:t + 1], in1=g_fin[0:n, :],
                                         op0=ALU.mult, op1=ALU.mult).then_inc(S["fin_r"], 1)

            steps = {f.__name__: f for f in (past_keys, dt_turn, att_scores, att_soft, conv, silu, ssm_turn, lru,
                                             lru_scan, ssd_decay, ssd_exp, ssd_mix, ssd_norm, ssd_turn, ffn_norm, ffn_turn,
                                             split, params)}
            x_norm(0)
            x_norm(1)
            x_turn(0)
            for t in range(1, NT):
                if t + 1 < NT:
                    x_norm(t + 1)
                x_turn(t)
                u_split(t - 1)
            u_split(NT - 1)
            for n in range(NITEM + 1):
                for name, i in JOBS.get(n, []):
                    if name in steps:
                        steps[name](i)
                if n < NITEM:
                    item(n)
            routing()
            expert_pair(0, before=False)
            with dve.Fori(1, EPAIRS) as i:
                expert_pair(i)
            dve.wait_ge(S["over_r"], 1)
            total = dve.value_load(over_total[0:1, 0:1], min_val=0, max_val=OVB)
            for j in range(OPAIRS):
                with dve.If(total > j):
                    expert_pair(EPAIRS + j)
            for t in range(NT):
                final(t)
                if t > 0:
                    final_norm(t - 1)
            final_norm(NT - 1)

        @block.gpsimd
        def _(pool):
            pool.memset(att_s, 0.0).then_inc(S["pool_c"], 1)
            pool.wait_ge(S["pool_c"], 1)
            zeros = att_s[:, 0, 0:P]

            def mask(dst, src, op, fill, step, ch):
                pool.affine_select(out=dst, in_=src, pattern=[[step, P]], compare_op=op, fill=fill, base=0,
                                   channel_multiplier=ch).then_inc(S["consts"], 1)

            mask(ident, zeros, ALU.not_equal, 1.0, -1, 1)
            pool.memset(q2, 0.0).then_inc(S["q_zero"], 1)
            lo = 0
            for name, k in PAR_ROWS:
                if name == "g_mix":
                    lo += k
                    continue
                src = a[name][0]
                if len(src.shape) == 1:
                    src = src.rearrange("(r p) -> r p", p=P)
                elif len(src.shape) == 2:
                    src = src.rearrange("k (r p) -> (k r) p", p=P)
                pool.dma_start(st_a[lo:lo + k, :], src).then_inc(S["par_in"], 16)
                lo += k
            pool.dma_start(st_b[0:12, :], a["state_lru_conv"][0, 0].rearrange("k (r p) -> (k r) p", p=P)
                          ).then_inc(S["par_in"], 16)
            pool.dma_start(st_b[12:36, :], a["state_ssm_conv"][0, 0].rearrange("k (r p) -> (k r) p", p=P)
                          ).then_inc(S["par_in"], 16)
            for lo, n, name in ((0, 8, "ssm_dt_bias"), (8, 8, "ssm_a_log"), (16, 8, "ssm_d"),
                                (24, 4, "b_router_group"), (28, 32, "b_router_expert")):
                pool.dma_start(rowc[:, lo:lo + n], a[name][0:1, :].partition_broadcast(P)
                              ).then_inc(S["bc_in"], 16)
            pool.dma_start(w_dt, a["w_in"][0, :, 4096:4104].rearrange("(k p) n -> p k n", p=P)
                           ).then_inc(S["par_in"], 16)
            pool.memset(ones, 1.0)
            pool.memset(neg_ones, -1.0).then_inc(S["pool_c"], 1)
            pool.wait_ge(S["pool_c"], 2)
            mask(u_incl, ones, ALU.is_ge, 0.0, 1, -1)
            mask(u_strict, ones, ALU.is_gt, 0.0, 1, -1)
            mask(neg_l, neg_ones, ALU.is_ge, 0.0, -1, 1)
            mask(att_mask, zeros, ALU.is_gt, NEG, 1, -1)
            mask(ssd_mask, zeros, ALU.is_ge, NEG, 1, -1)
            pool.memset(xp[0], 0.0)
            pool.memset(xp[1], 0.0).then_inc(S["consts"], 1)
            pool.wait_ge(S["consts"], 7)
            pool.sem_inc(S["masked"], 1)
            pool.iota(iota_i, [[1, NE]], base=0, channel_multiplier=0)
            pool.iota(tok_id, [[P, NT]], base=0, channel_multiplier=1)
            pool.memset(no_token, 0).then_inc(S["ids_r"], 1)
            pool.dma_start(yd[NE * BLK:(NE + OVB) * BLK, :].rearrange("(c p) d -> p c d", p=P),
                           att_s[:, :, :].rearrange("p a b -> p (a b)").unsqueeze(1).to_broadcast([P, OPAIRS, D])
                           ).then_inc(S["side_dma"], 16)
            for lo, k, name in ((0, NG, "w_router_group"), (NG, NE, "w_router_expert")):
                pool.dma_start(w_r[:, :, lo:lo + k], a[name][0].rearrange("(k p) n -> p k n", p=P)
                               ).then_inc(S["side_dma"], 16)
            pool.wait_ge(S["ids_r"], 1)
            pool.dma_start(tabd.rearrange("(p c) o -> p (c o)", p=P), no_token).then_inc(S["tab_moved"], 16)

            pool.wait_ge(S["xt_ps"], NT)
            pool.memset(gb[:, :, SEQ:TW], 0.0).then_inc(S["gb_zero"], 1)

            def att_after(u):
                kind, hp, kb = ATT[u]
                s, b = att_s, att_b[u % 2]
                pool.wait_ge(S["zw_r"], u + 1)
                if u == 0:
                    pool.wait_ge(S["side_dma"], 48)
                if kind == "p":
                    n = SEQ - kb * P
                    if kb == KB - 1:
                        pool.tensor_copy(s[:, :, 0:n], b[:, :, 0:n]).then_inc(S["s_sum"], 1)
                    elif kb > 0:
                        pool.tensor_tensor(b[:, :, P:n], b[:, :, P:n], s[:, :, 0:n - P], ALU.add
                                           ).then_inc(S["pool_c"], 1)
                        cnt[0] += 1
                        pool.wait_ge(S["pool_c"], cnt[0])
                        pool.tensor_copy(s[:, :, 0:n], b[:, :, 0:n]).then_inc(S["s_sum"], 1)
                    else:
                        pool.memset(s[:, 0, :], 0.0).then_inc(S["s_sum"], 1)
                else:
                    n = P if kb < KB else DEC
                    pool.tensor_tensor(s[0:n, 0, :], s[0:n, 0, :], b[0:n, 0, :], ALU.add).then_inc(S["s_sum"], 1)

            cnt = [2]

            def lru_weights():
                pool.wait_ge(S["s_sum"], NATT)
                pool.wait_ge(S["conv_c"], XT + WT)
                pool.wait_ge(S["o_out"], PAIRS + 1)
                pool.memset(lru_w, 0.0).then_inc(S["lruw_z"], 1)
                pool.wait_ge(S["lruw_z"], 1)
                for g, name in enumerate(("lru_w_a", "lru_w_x")):
                    for b in range(HEADS):
                        r0 = (b % 2) * HD
                        pool.dma_start(lru_w[r0:r0 + HD, g, b // 2, r0:r0 + HD], a[name][0, b]
                                       ).then_inc(S["lruw_in"], 16)
                pool.dma_start(ss_in, a["state_ssm_h"][0, 0].rearrange("(j q) p n -> (q p) j n", q=2)
                               ).then_inc(S["lruw_in"], 16)

            def lru(c):
                r, i, la, m, gl = lt
                g = gb[:, c, :]
                if c > 0:
                    pool.wait_ge(S["ob_r"], c)
                else:
                    pool.wait_ge(S["gb_zero"], 1)
                pool.tensor_tensor(gl, g, g, ALU.mult).then_inc(S["lru_pool"], 1)
                pool.wait_ge(S["lru_pool"], 4 * c + 1)
                pool.tensor_scalar(gl, gl, GELU_A, 1.0, ALU.mult, ALU.add).then_inc(S["lru_pool"], 1)
                pool.wait_ge(S["lru_pool"], 4 * c + 2)
                pool.tensor_tensor(gl, gl, g, ALU.mult).then_inc(S["lru_pool"], 1)
                pool.wait_ge(S["lru_ac"], 2 * c + 1)
                pool.tensor_tensor(m, la, la, ALU.mult).then_inc(S["lru_pool"], 1)

            def decays(c):
                n = TT[c][1]
                td = at(td_flat, HEADS, n)[0:n]
                if c == NT - 1:
                    pool.wait_ge(S["so_out"], 16)
                if c == 0:
                    pool.wait_ge(S["dt_r"], 1)
                    pool.wait_ge(S["ob_r"], WT)
                pool.tensor_tensor(td, bc(u_incl[0:n, 0:n].unsqueeze(1), n, HEADS, n),
                                   bc(dA[0:n, c, :].unsqueeze(2), n, HEADS, n), ALU.mult).then_inc(S["td_r"], 1)

            def ssd_decay(c):
                n = TT[c][1]
                e = at(e_flat, HEADS, n)[0:n]
                if c == 0 or c == NT - 1:
                    decays(c)
                pool.wait_ge(S["d_r"], c + 1)
                pool.tensor_tensor(e, e, bc(ssd_mask[0:n, 0:n].unsqueeze(1), n, HEADS, n), ALU.add
                                   ).then_inc(S["em_r"], 1)
                if c == 0:
                    pool.wait_ge(S["turn_r"], 2 * NT)
                if c > 0:
                    pool.wait_ge(S["mix_ps"], c)
                xs3 = xs_tok[0:n, c, :].rearrange("p (e d) -> p e d", e=HEADS)
                pool.tensor_tensor(xdt[0:n], xs3, bc(dt_sb[0:n, c, :].unsqueeze(2), n, HEADS, HD), ALU.mult
                                   ).then_inc(S["xdt_r"], 1)

            def ssd_exp(c):
                n = TT[c][1]
                e = at(e_flat, HEADS, n)[0:n]
                pool.wait_ge(S["xdt_r"], c + 1)
                pool.wait_ge(S["e_r"], c + 1)
                pool.tensor_tensor(xdd[0:n], xdt[0:n], bc(e[:, :, n - 1:n], n, HEADS, HD), ALU.mult
                                   ).then_inc(S["xdd_r"], 1)

            def ssd_mix(c):
                n = TT[c][1]
                state = hT if c < NT - 1 else hS
                pool.wait_ge(S["mix_ps"], c + 1)
                if c > 0:
                    pool.wait_ge(S["ea_r"], c + 1)
                    s3 = state.rearrange("p (e d) -> p e d", e=HEADS)
                    pool.tensor_tensor(s3, s3, bc(cd.unsqueeze(2), P, HEADS, HD), ALU.mult).then_inc(S["hcd_r"], 1)
                xs3 = xs_tok[0:n, c, :].rearrange("p (e d) -> p e d", e=HEADS)
                pool.tensor_tensor(xs3, xs3, bc(rowc[0:n, 16:24].unsqueeze(2), n, HEADS, HD), ALU.mult
                                   ).then_inc(S["y2_r"], 1)
                pool.wait_ge(S["y2_r"], 2 * c + 1)
                pool.wait_ge(S["y0_r"], c + 1)
                pool.tensor_tensor(y_sb[0:n, :], y_sb[0:n, :], xs_tok[0:n, c, :], ALU.add).then_inc(S["y2_r"], 1)
                pool.wait_ge(S["y2_r"], 2 * c + 2)
                pool.wait_ge(S["y1_r"], c + 1)
                pool.tensor_tensor(y_sb[0:n, :], y_sb[0:n, :], tz[0:n, :], ALU.mult).then_inc(S["yg_r"], 1)
                if c + 1 < NT - 1:
                    decays(c + 1)

            def item(n):
                it = ITEMS[n]
                if it[0] == "b" and it[5] > 0:
                    _, c, hh = it[:3]
                    k = (n - MIX1) // 2
                    wait_drained(pool, n)
                    v = merged[:, c, hh * HALF:(hh + 1) * HALF]
                    pool.tensor_tensor(v, v, gtmp[k % 2], ALU.add).then_inc(S["gm_r"], 1)

            def ffn_norm(t):
                n = TT[t][1]
                if t == 0:
                    pool.wait_ge(S["gm_r"], 4 * KD)
                    pool.wait_ge(S["so_out"], 32)
                    pool.dma_start(g_ffn, a["g_ffn"][0:1, :].partition_broadcast(P)).then_inc(S["gains_in"], 16)
                    pool.wait_ge(S["gains_in"], 16)
                pool.wait_ge(S["u2_a"], t + 1)
                pool.tensor_tensor(u2[t % 2][0:n, :], u2[t % 2][0:n, :], g_ffn[0:n, :], ALU.mult
                                   ).then_inc(S["u2_r"], 1)

            steps = {f.__name__: f for f in (att_after, lru, ssd_decay, ssd_exp, ssd_mix, ffn_norm)}
            for n in range(NITEM + 1):
                if n == MIX1:
                    lru_weights()
                for name, i in JOBS.get(n, []):
                    if name in steps:
                        steps[name](i)
                if n < NITEM:
                    item(n)
            pool.wait_ge(S["lg_ps"], NT)
            pool.dma_start(g_fin, a["g_final"].rearrange("(o d) -> o d", o=1).partition_broadcast(P)
                           ).then_inc(S["gains_in"], 16)
            pool.wait_ge(S["rows_r"], 1)
            pool.wait_ge(S["tab_moved"], 16)
            for s in range(2):
                for t, (o0, n) in enumerate(TT):
                    c = s * NT + t
                    pool.indirect_dma_start(out=tabd, out_offset=bass.IndirectOffsetOnAxis(
                        ap=tab_row[0:n, c:c + 1], axis=0), in_=tok_id[0:n, t:t + 1], in_offset=None
                                            ).then_inc(S["tab_out"], 16)
            pool.wait_ge(S["tab_out"], 16 * 2 * NT)
            pool.dma_start(tab, tabd.rearrange("(p c) o -> p (c o)", p=P)).then_inc(S["tab_moved"], 16)
            pool.wait_ge(S["tab_moved"], 32)
            for s in range(2):
                pool.wait_ge(u2_out[s], 16 * ((NT + 1 - s) // 2))

            def expert_pair(i, before=True):
                if before:
                    pool.wait_ge(S["xg_in"], i * 16)
                    pool.wait_ge(S["xt2_ps"], i)
                pool.tensor_copy(idx_now, tab[:, bass.ds(i, 1)]).then_inc(S["idx_r"], 1)
                pool.wait_ge(S["idx_r"], i + 1)
                pool.sem_inc(S["idx_seen"], 1)
                pool.indirect_dma_start(out=xg, out_offset=None, in_=u2d, in_offset=bass.IndirectOffsetOnAxis(
                    ap=idx_now, axis=0)).then_inc(S["xg_in"], 16)

            expert_pair(0, before=False)
            with pool.Fori(1, EPAIRS) as i:
                expert_pair(i)
            pool.wait_ge(S["over_r"], 1)
            total = pool.value_load(over_total[0:1, 0:1], min_val=0, max_val=OVB)
            for j in range(OPAIRS):
                with pool.If(total > j):
                    expert_pair(EPAIRS + j)
            pool.wait_ge(S["experts_done"], 1)
            for t, (o0, n) in enumerate(TT):
                if t >= 2:
                    pool.wait_ge(S["ssq_r"], 2 * NT + t - 1)
                for s in range(2):
                    c = s * NT + t
                    pool.indirect_dma_start(out=y_back[t % 2][s][0:n, :], out_offset=None, in_=yd,
                                            in_offset=bass.IndirectOffsetOnAxis(ap=y_row[0:n, c:c + 1], axis=0)
                                            ).then_inc(back_in[t % 2], 16)


OUTS = [("y_p", (1, SEQ, D)), ("y_s", (1, DEC, D)),
        ("k_p", (1, 1, SEQ, HEADS, HD)), ("v_p", (1, 1, SEQ, HEADS, HD)),
        ("lru_conv_p", (1, 1, GAP, W)), ("lru_h_p", (1, 1, W)), ("ssm_conv_p", (1, 1, GAP, XBC)),
        ("ssm_h_p", (1, 1, HEADS, HD, STATE)),
        ("k_s", (1, 1, DEC, HEADS, HD)), ("v_s", (1, 1, DEC, HEADS, HD)),
        ("lru_conv_s", (1, 1, GAP, W)), ("lru_h_s", (1, 1, W)), ("ssm_conv_s", (1, 1, GAP, XBC)),
        ("ssm_h_s", (1, 1, HEADS, HD, STATE))]


def kernel(**inputs):
    import numpy as np
    from concourse import bacc
    from concourse.bass_utils import run_bass_kernel_spmd

    nc = bacc.Bacc("TRN2", target_bir_lowering=False, num_devices=1)
    arrays, a, o = {}, {}, {}
    for name, x in inputs.items():
        arrays["in_" + name] = np.ascontiguousarray(x)
        a[name] = nc.dram_tensor("in_" + name, arrays["in_" + name].shape, F32, kind="ExternalInput").ap()
    for name, shape in OUTS:
        o[name] = nc.dram_tensor("out_" + name, shape, F32, kind="ExternalOutput").ap()
    trunk_and_experts(nc, a, o)
    r = run_bass_kernel_spmd(nc, [arrays], core_ids=[0])
    return tuple(r.results[0]["out_" + name] for name, _ in OUTS)
```

```python
from contextlib import ExitStack

import concourse.bass as bass
from concourse import mybir

F32 = mybir.dt.float32
F32R = mybir.dt.float32r
I32 = mybir.dt.int32
U32 = mybir.dt.uint32
ALU = mybir.AluOpType
ACT = mybir.ActivationFunctionType
AXX = mybir.AxisListType.X

P = 128
D = 1024
SEQ = 512
DEC = 64
PAST = 512
T = SEQ + DEC
HALF = T // 2
KD = D // P
TT = [(t * P, P) for t in range(SEQ // P)] + [(SEQ, DEC)]
NT = len(TT)
HEADS = 8
HD = 64
PAIRS = HEADS // 2
KB = SEQ // P
W = 512
WT = W // P
STATE = 128
GROUPS = 2
XBC = W + 2 * GROUPS * STATE
XT = XBC // P
CW = 4
GAP = CW - 1
TW = SEQ + GAP + DEC + 1
SAMP = SEQ + GAP
XP = TW + GAP
EPS = 1e-6
NEG = -1.0e30
BIG = 3.0e38
GELU_C = 0.7978845608028654
GELU_A = 0.044715

NG = 4
EPG = 8
NE = NG * EPG
DE = D // 2
BLK = 64
NA = T * 2
OVB = NA // (BLK + 1) + 1
OVB += OVB % 2
EPAIRS = NE // 2
OPAIRS = OVB // 2
NPC = EPAIRS + OPAIRS

PAR_ROWS = [("g_mix", 8), ("b_gate", 24), ("lru_conv_w", 16), ("lru_conv_b", 4), ("ssm_conv_w", 32),
            ("ssm_conv_b", 8), ("lru_b_a", 4), ("lru_b_x", 4), ("lru_lambda", 4), ("ssm_norm_g", 4),
            ("state_lru_h", 4)]
PAR = {}
_n = 0
for _name, _k in PAR_ROWS:
    PAR[_name] = _n
    _n += _k
NPAR = _n
NST = 36
TAILS = 80
SMALL = 1312
ARENA = 53200
ROUND = 12582912.0

UNITS = [("in", P * i) for i in range(12)] + [("in", 3072 + P * i) for i in range(8)]
UNITS += [("in", 1536 + P * i) for i in range(8)] + [("in", 2560 + P * i) for i in range(4)]
GATE0 = len(UNITS)
for _b in range(3):
    for _c in range(KD):
        UNITS += [("gate", _b * D + _c * P)]
        if _c % 2 == 0:
            UNITS += [("branch", _b, _c // 2)]
        if (_b, _c) == (2, 1):
            UNITS += [("out", P * i) for i in range(4)]
OUTU = len(UNITS)
UNITS += [("out", P * i) for i in range(4, 8)]
UIX = {u: i for i, u in enumerate(UNITS)}
NSLOT = 4

ITEMS = []
for _h in range(2):
    ITEMS += [("q", c, _h, c, 0) for c in range(WT)]
for _c in range(WT):
    ITEMS += [("k", _c, h, 4 + _c, 0) for h in range(2)]
for _u in range(2):
    ITEMS += [("v", _u, t, 8 + 2 * _u, 0) for t in range(NT)]
ITEMS += [("dt", 0, h, None, 0) for h in range(2)]
MIX0 = len(ITEMS)
for _c in range(XT):
    ITEMS += [("x", _c, h, 12 + _c, 0) for h in range(2)]
for _c in range(WT):
    ITEMS += [("r", _c, h, 20 + _c, 0) for h in range(2)]
for _c in range(WT):
    ITEMS += [("gb", _c, h, 24 + _c, 0) for h in range(2)]
for _u in range(2):
    ITEMS += [("z", _u, t, 28 + 2 * _u, 0) for t in range(NT)]
MIX1 = len(ITEMS)
for _b in range(3):
    for _c in range(KD):
        for _h in range(2):
            ITEMS += [("g", _c, _h, UIX[("gate", _b * D + _c * P)], 0, _b),
                      ("b", _c, _h, UIX[("branch", _b, _c // 2)], _c % 2, _b)]
OUT0 = len(ITEMS)
for _t in range(NT):
    ITEMS += [("o", _t, q, UIX[("out", 256 * q)], 0) for q in range(4)]
DVE_KINDS = ("k", "b", "o")
IDX = {}
for _i, _it in enumerate(ITEMS):
    IDX[(_it[0],) + _it[1:3] + _it[5:]] = _i
FIRST_OF, LAST_OF = {}, {}
for _i, _it in enumerate(ITEMS):
    for _u in ((_it[3], _it[3] + 1) if _it[0] in "vzo" else (_it[3],)):
        FIRST_OF.setdefault(_u, _i)
        LAST_OF[_u] = _i
OUT_EARLY = UIX[("out", 0)]
SLOT, BEFORE, ARRIVAL = {}, {}, {}
_in_slot = [None] * NSLOT
_arrived = [0] * NSLOT
for _u in range(len(UNITS)):
    _free = [-1 if w is None else LAST_OF[w] for w in _in_slot]
    if OUT_EARLY <= _u < OUT_EARLY + 4:
        SLOT[_u], BEFORE[_u], ARRIVAL[_u] = NSLOT + _u - OUT_EARLY, None, 4
        continue
    if _u in (8, 10, 28, 30, OUTU, OUTU + 2):
        _s = min((0, 2), key=lambda s: max(_free[s], _free[s + 1]))
    elif _u in (9, 11, 29, 31, OUTU + 1, OUTU + 3):
        _s = SLOT[_u - 1] + 1
    else:
        _s = min(range(NSLOT), key=lambda s: _free[s])
    BEFORE[_u] = _in_slot[_s]
    SLOT[_u] = _s
    _in_slot[_s] = _u
    _arrived[_s] += 1
    ARRIVAL[_u] = _arrived[_s]
AHEAD = 3
SPLIT_AT = {u: max(0, FIRST_OF[u] - AHEAD) for u, v in enumerate(UNITS) if v[0] != "branch" or v[1] > 0}
for _i in range(4):
    SPLIT_AT[OUT_EARLY + _i] = OUT0 - 20 + 4 * _i
    SPLIT_AT[OUTU + _i] = OUT0 + 1 + _i // 2
SPLITS = sorted(SPLIT_AT, key=lambda u: (SPLIT_AT[u], u))
SPLIT_NO = {u: n for n, u in enumerate(SPLITS)}
DRAINED = []
_cnt = [0, 0]
for _it in ITEMS:
    _e = 1 if _it[0] in DVE_KINDS else 0
    _cnt[_e] += 1
    DRAINED.append((_e, _cnt[_e]))

ATT = [("p", hp, kb) for hp in range(PAIRS) for kb in reversed(range(KB))]
ATT += [("d", 0, kb) for kb in reversed(range(PAST // P + 1))]
NATT = len(ATT)


def att_at(u):
    return (7 * u) // 4


JOBS = {}


def job(item, *what):
    JOBS.setdefault(item, []).append((what[0], what[1:]))


for _u in SPLITS:
    job(SPLIT_AT[_u], "split", _u)
job(4, "params", 0)
_v0 = IDX[("v", 0, 0)]
for _i in range(4):
    job(_v0 + 1 + _i, "past_keys", _i)
for _i in range(NT):
    job(_v0 + 5 + _i, "keys_out", _i)
job(MIX0 + 1, "dt_turn", 0)
for _s in range(MIX1 - MIX0):
    for _u in range(NATT):
        if att_at(_u) + 3 == _s:
            job(MIX0 + _s, "att_values", _u)
    for _u in range(NATT):
        if att_at(_u) + 2 == _s:
            job(MIX0 + _s, "att_after", _u)
    for _u in range(NATT):
        if att_at(_u) == _s:
            job(MIX0 + _s, "att_scores", _u)
for _c in range(XT):
    job(IDX[("x", _c, 1)] + 1, "conv", _c)
for _c in range(WT):
    job(IDX[("r", _c, 1)] + 1, "conv", XT + _c)
for _u in range(NATT):
    job(MIX0 + att_at(_u), "att_soft", _u)


def mix3(s):
    return MIX1 + 2 * s


job(mix3(1), "state_in", 0)
for _i in range(XT):
    job(mix3(_i // 4), "silu", _i)
for _t in range(NT):
    job(mix3(2 + _t // 2), "ssm_turn", _t)
LRU0, SSD0 = 4, 22
for _c in range(WT):
    job(MIX1 + LRU0 + 4 * _c, "lru", _c)
    job(MIX1 + LRU0 + 4 * _c + 2, "lru_scan", _c)
for _c in range(NT):
    _s = MIX1 + SSD0 + 8 * _c
    job(_s, "ssd_decay", _c)
    job(_s + 2, "ssd_exp", _c)
    job(_s + 3, "ssd_mix", _c)
    job(_s + 5, "ssd_norm", _c)
    job(_s + 8, "ssd_turn", _c)
for _i, _s in enumerate((26, 28)):
    job(MIX1 + _s, "mix_split", 1, _i)
for _t, _s in enumerate((34, 40, 48, 56, 63)):
    job(MIX1 + _s, "mix_split", 2, _t)
for _c in range(KD):
    for _h in range(2):
        job(min(IDX[("b", _c, _h, 2)] + 2, OUT0), "merged_split", _c, _h)
job(MIX1 + SSD0 + 4, "tails_turn", 0)
job(MIX1 + SSD0 + 8 * 3 + 7, "state_out", 0)
job(MIX1 + SSD0 + 8 * 4 + 7, "state_out", 1)
for _t in range(NT):
    job(OUT0 + 4 * (_t + 1), "ffn_norm", _t)
    job(OUT0 + 4 * (_t + 1) + 2, "ffn_turn", _t)
NEARLY = 3
NMIX = 2 + NT
job(OUT0 + 4 * NEARLY + 5, "early", 0)
NITEM = len(ITEMS)
for _i, _j in [(k, v) for k, v in JOBS.items() if k > NITEM]:
    JOBS.setdefault(NITEM, []).extend(_j)
    del JOBS[_i]


def trunk_and_experts(nc, a, o):
    ctx = ExitStack()
    with ctx:
        def sb(name, shape, dt=F32):
            return ctx.enter_context(nc.sbuf_tensor(name, shape, dt))

        def ps(name, shape):
            return ctx.enter_context(nc.psum_tensor(name, shape, F32))

        def sem(name):
            return ctx.enter_context(nc.semaphore(name))

        arena_at = -(-nc.sbuf_base // 32) * 32
        arena = sb("arena", [P, ARENA])
        cut = [0]

        def take(n):
            cut[0] += n
            assert cut[0] <= ARENA, cut[0]
            return cut[0] - n

        def at(off, *dims):
            n = 1
            for d in dims:
                n *= d
            v = arena[:, off:off + n]
            if len(dims) == 2:
                v = v.rearrange("p (a b) -> p a b", a=dims[0])
            if len(dims) == 3:
                v = v.rearrange("p (a b c) -> p a b c", a=dims[0], b=dims[1])
            return v

        def region(name, off, n, dt=F32R):
            return nc.alloc_sbuf_tensor_at(name, [P, n], dt, offset=arena_at + 4 * off)[:, :]

        ident, u_incl, u_strict, neg_l, neg_ones, ones, att_mask, ssd_mask = (
            at(take(P), P) for _ in range(8))
        cpar = at(take(NPAR), NPAR)
        cst = at(take(NST), NST)
        rowc = at(take(60), 60)
        tails = at(take(TAILS), TAILS)
        small = take(SMALL)
        gains_mix = region("gains_mix", take(KD), KD, F32)
        w_dt_off = take(KD * 8)
        w_dt = at(w_dt_off, KD, 8)
        h_off = take(NT * D)
        h = at(h_off, NT, D)
        merged_off = take(KD * T)
        ring_off = take(NSLOT * 2048)
        ring = region("ring", ring_off, NSLOT * 2048, F32)
        ring4 = [at(ring_off + 2048 * s, WT, 256) for s in range(NSLOT)]
        raw = [ring[:, 2048 * s:2048 * s + 1024].rearrange("p (k n) -> p k n", k=KD) for s in range(NSLOT)]
        raw4 = [ring[:, 2048 * s:2048 * s + 1024].rearrange("p (k n) -> p k n", k=WT) for s in range(NSLOT)]
        ring_flat = region("ring_r", ring_off, NSLOT * 2048)
        ring_r = ring_flat.rearrange("p (s k n) -> p s k n", s=2 * NSLOT, k=KD)
        ring_r4 = ring_flat.rearrange("p (s k n) -> p s k n", s=2 * NSLOT, k=WT)
        rest_r = [ring_r[:, 2 * s] for s in range(NSLOT)]
        high_r = [ring_r[:, 2 * s + 1] for s in range(NSLOT)]
        front = cut[0]

        early_off = front + 2 * KD * T + WT * T
        early = region("early", early_off, NSLOT * 2048, F32)
        early_r = region("early_r", early_off, NSLOT * 2048).rearrange("p (s k n) -> p s k n", s=2 * NSLOT, k=KD)
        for s in range(NSLOT):
            raw.append(early[:, 2048 * s:2048 * s + 1024].rearrange("p (k n) -> p k n", k=KD))
            rest_r.append(early_r[:, 2 * s])
            high_r.append(early_r[:, 2 * s + 1])

        def pair_r(s, part, k):
            v = ring_r if s < NSLOT else early_r
            s %= NSLOT
            return v[:, 2 * s + part:2 * s + part + 3:2, k, :]

        def two_tiles(name, off, dt):
            return [region(f"{name}{j}", off + 2 * T * j, 2 * T, dt).rearrange("p (k t) -> p k t", k=2)
                    for j in range(KD // 2)]

        merged = two_tiles("merged", merged_off, F32)
        merged_rest = two_tiles("merged_rest", merged_off, F32R)
        merged_high = two_tiles("merged_high", early_off + NSLOT * 2048, F32R)
        uh_off = take(KD * T)
        u_high_r = region("u_high_r", uh_off, KD * T).rearrange("p (k t) -> p k t", k=KD)
        u_rest = region("u_rest", h_off, KD * T, F32).rearrange("p (k t) -> p k t", k=KD)
        u_rest_r = region("u_rest_r", h_off, KD * T).rearrange("p (k t) -> p k t", k=KD)
        q2_off = take(2 * PAIRS * T)
        q2 = at(q2_off, 2, PAIRS, T)
        oAT = at(q2_off, PAIRS, T)
        xconv_off = take(XT * TW)
        xconv = at(xconv_off, XT, TW)
        xc_off = take(WT * TW)
        xc = at(xc_off, WT, TW)
        gb_off = take(WT * TW)
        gb = at(gb_off, WT, TW)
        z2_off = take(NT * W)
        z2 = at(z2_off, NT, W)
        x0 = at(xc_off, NT, D)
        tmp = cut[0]
        kT = at(take(PAIRS * T), PAIRS, T)
        kpT = at(take(PAIRS * PAST), PAIRS, PAST)
        att_a = [at(take(1024), 2, 512) for _ in range(2)]
        att_b = [at(take(1024), 2, 512) for _ in range(2)]
        att_s = at(take(1024), 2, 512)
        xp_off = [take(584) for _ in range(2)]
        xp = [at(x, 584) for x in xp_off]
        v_sb = at(merged_off, NT, W)
        vp_sb = at(merged_off + NT * W, KB, W)
        kp_raw = at(xconv_off, KB, W)
        st_a = at(xconv_off + 2048, P)
        st_b = at(xconv_off + 2048 + P, P)
        junk = at(xconv_off + 2048 + 2 * P, D)
        ko = [at(z2_off + 512 + 512 * i, W) for i in range(2)]
        dtT = at(z2_off + 1536, T)
        assert xc_off + NT * D <= z2_off + 512
        cut[0] = tmp
        xs_tok = at(take(NT * W), NT, W)
        b_tok = at(take(NT * 256), NT, 256)
        xdt_off = take(W)
        xdt = at(xdt_off, HEADS, HD)
        ss_in = at(xdt_off, WT, P)
        xdd_off = take(W)
        xdd = at(xdd_off, HEADS, HD)
        y_off_sb = at(take(W), W)
        y_sb = at(take(W), W)
        th = [at(xdd_off + TW * i, TW) for i in range(2)]
        lt_off = take(5 * TW)
        lt = [at(lt_off + TW * i, TW) for i in range(5)]
        lru_w = at(take(8 * P), 2, WT, P)
        gsb = [at(take(HALF), HALF) for _ in range(2)]
        gtmp = [at(take(HALF), HALF) for _ in range(2)]
        hS = at(take(W), W)
        e_flat = lt_off
        m_flat = lt_off + 1024
        td_flat = lt_off + 2048
        hT = at(xc_off, W)
        tz = at(xc_off + W, W)
        h_out = at(lt_off + 3072, WT, P)
        tail_row = at(xc_off + 2 * W, P)
        def mixed(name, off, dt):
            return region(name, off, WT * T, dt).rearrange("p (k t) -> p k t", k=WT)

        out_mix = [None, mixed("lru_out", q2_off + PAIRS * T, F32), mixed("ssm_out", xconv_off, F32)]
        out_rest = [None, mixed("lru_rest", q2_off + PAIRS * T, F32R), mixed("ssm_rest", xconv_off, F32R)]
        out_high = [None, mixed("lru_high", gb_off, F32R), mixed("ssm_high", q2_off, F32R)]

        wexp_off = front
        w_u = at(wexp_off + 8192, 2 * KD, DE)
        w_d = at(wexp_off + 16384, 2 * (DE // P), D)
        cut[0] = front + 24576
        u2_off = take(2 * D)
        u2 = [at(u2_off + D * i, D) for i in range(2)]
        u2T_off = take(2 * D)
        u2T = [at(u2T_off + D * i, KD, P) for i in range(2)]
        place_hot = at(merged_off + D, 2 * NT, P)
        col_hot = at(merged_off + D + 2 * NT * P, 2 * NT, NPC)
        g_fin = at(u2T_off, D)
        over_cmp = at(u2T_off + D, OVB, NE)
        iota_p = at(u2T_off + D + OVB * NE, P).bitcast(I32)
        iota_pf = at(u2T_off + D + OVB * NE + P, P)
        g_ffn = at(take(D), D)
        lg = at(take(NT * 36), NT, 36)
        v_top = [at(take(NT), NT) for _ in range(2)]
        masked_off = take(2 * NT * NE)
        e_masked = at(masked_off, NT, NE)
        e_cand = at(masked_off + NT * NE, NT, NE)
        picked = at(masked_off, 2, NT, NE)
        hot_off = take(2 * NT * NE)
        e_hot = [at(hot_off + NT * NE * s, NT, NE) for s in range(2)]
        both_hot = at(hot_off, 2, NT, NE)
        hot_sum = at(take(NT * NE), NT, NE)
        g_cand = at(take(NT * NG), NT, NG)
        g_hot = at(take(NT * NG), NT, NG)
        g_max, g_key, e_key, p_sel = (at(take(NT), NT) for _ in range(4))
        for_exp = at(take(NT * NG + NT), NT * NG + NT)
        tile_base = at(take((NT + 1) * NE), NT + 1, NE)
        n_over, over_incl, over_start = (at(take(NE), NE) for _ in range(3))
        rank, first, expert, blk_no, place, col, side, is_over, div = (at(take(2 * NT), 2, NT) for _ in range(9))
        eid = at(take(OVB), OVB)
        cut[0] = merged_off
        xg = at(take(D), D)
        xT = at(take(D), KD, P)
        hidT = at(take(DE), DE // P, P)
        gate_t = at(take(DE), DE)
        hid = at(take(DE), DE)
        y_out_sb = at(take(D), D)
        w_g = [at(wexp_off, 2 * KD, DE), at(take(2 * KD * DE), 2 * KD, DE)]
        assert cut[0] <= front
        y_back = [[at(wexp_off + D * (2 * i + s), D) for s in range(2)] for i in range(2)]

        cs = [small]

        def tiny(*dims):
            n = 1
            for d in dims:
                n *= d
            cs[0] += n
            assert cs[0] <= small + SMALL
            return at(cs[0] - n, *dims)

        w_dt_h = tiny(KD * 8)
        ssq = tiny(8)
        rstd = tiny(8)
        sp_x, sp_e, sp_u, sp_l, sp_m, sp_p = (tiny(44) for _ in range(6))
        dt_sb = sp_x[:, 0:40].rearrange("p (t h) -> p t h", t=NT)
        a_exp = tiny(8)
        dA = tiny(NT, 8)
        ls4 = tiny(WT)
        ls4n = tiny(WT)
        acs = tiny(8)
        ea = tiny(8)
        cd = tiny(8)
        ssy = tiny(2)
        rsy = tiny(2)
        ss2 = tiny(8)
        rs2 = tiny(8)

        w_r = tiny(KD, 36)
        w_dt_hr = region("w_dt_high_r", small, KD * 8).rearrange("p (k n) -> p k n", k=KD)
        w_dt_rr = region("w_dt_rest_r", w_dt_off, KD * 8).rearrange("p (k n) -> p k n", k=KD)
        w_sel = tiny(2, NT)
        ss3 = tiny(8)
        rs3 = tiny(8)
        rev = tiny(NE)
        iota_f = tiny(NE)
        tok_id = tiny(NT).bitcast(I32)
        iota_i = tiny(NE).bitcast(I32)
        tok_f = tiny(NT)
        tab = tiny(NPC).bitcast(I32)
        idx_now = tiny(1).bitcast(I32)
        y_row = tiny(2 * NT).bitcast(I32)
        over_total = tiny(1).bitcast(I32)
        over_expert = tiny(OVB).bitcast(I32)
        assert cs[0] <= small + SMALL

        pj = ps("pj", [P, 2, 512])
        za = ps("za", [P, 2, 512])
        zb = ps("zb", [P, 2, 512])
        zz = [za, zb]
        oa = ps("oa", [P, 512])
        ms = ps("ms", [P, 512])

        u2d = nc.dram_tensor("u2d", (T, D), F32, kind="Internal").ap()
        yd = nc.dram_tensor("yd", ((NE + OVB) * BLK, D), F32, kind="Internal").ap()

        names = """
            route_ps route_in routed mix_high mix_rest vp_in consts gmix_in ut_u ut_h high_r rest_r wdt_r
            gb_zero par_in bc_in kp_in par_up ssq_r var_r std_r xn_r pe_par xt_ps ut_r pj_full pj_act pj_dve
            kp_ps kp_r ko_ps ko_r dt_ps dt_raw dt_r z_r nab_r ln_e l_r sp_r zw_r s_sum w_r_ o_r o_out q_zero
            masked conv_c silu_t silu_r turn_ps turn_r lruw_in lruw_z lru_ps lru_tr lru_ac lru_gt lru_m2
            lru_mu lru_h ob_r hs_ps hs_r td_r dec_ps acs_r d_r ea_r em_r e_r m_r xdt_r xdd_r tz_r mix_ps
            hcd_r h_r y0_r y1_r y2_r yg_r ssy_r vy_r sy_r yn_r yt_ps oc_r so_ps so_r so_out v_out tl_out
            tl_ps tl_r gm_r gains_in u2_r u2t_ps u2t_r lg_ps lg_r ids_r fexp_in fexp_r idx_r idx_seen xg_in
            xt2_ps xt2_a xt2_d wu_in wd_in gate_done up_done gate_th gate_mul hid_r hidt_ps hidt_r down_a
            down_b y_a y_b y_out experts_done hy_r fin_r fin_out dve_c pool_c sp_dve sp_act lru_pool side_dma""".split()
        S = {n: sem(n) for n in names}
        x_in = [sem(f"x_in{t}") for t in range(NT)]
        wg_in = [sem(f"wg_in{s}") for s in range(2)]
        back_in = [sem(f"back_in{s}") for s in range(2)]
        ko_out = [sem(f"ko_out{s}") for s in range(2)]
        u2_out = [sem(f"u2_out{s}") for s in range(2)]
        unit_in = [sem(f"unit_in{s}") for s in range(NSLOT)]
        unit_in += [sem("out_in")] * NSLOT

        def drained(n):
            e, v = DRAINED[n]
            return S["pj_act"] if e == 0 else S["pj_dve"], v

        def wait_drained(eng, n):
            s, v = drained(n)
            eng.wait_ge(s, v)

        def rows(ap, lo, n):
            return ap.rearrange("l (r p) -> (l r) p", p=P)[lo:lo + n, :]

        def att_view(buf, u):
            kind, hp, kb = ATT[u]
            if kind == "p":
                return buf[:, :, 0:SEQ - kb * P]
            return buf[0:P if kb < KB else DEC, 0, :]

        def mix_part(br, i):
            if br == 1:
                return slice(2 * i, 2 * i + 2), slice(0, T)
            return slice(0, WT), slice(TT[i][0], TT[i][0] + TT[i][1])

        def tw_cols(t):
            o0, n = TT[t]
            lo = o0 if t < NT - 1 else SAMP
            return lo, n

        block = ctx.enter_context(nc.Block())

        @block.sync
        def _(sp):
            def reload_x(t):
                o0, n = TT[t]
                src = a["x_prompt"][0, o0:o0 + n, :] if t < NT - 1 else a["x_sample"][0]
                sp.dma_start(h[0:n, t, :], src).then_inc(x_in[t], 16)

            for t, (o0, n) in enumerate(TT):
                src = a["x_prompt"][0, o0:o0 + n, :] if t < NT - 1 else a["x_sample"][0]
                sp.dma_start(x0[0:n, t, :], src).then_inc(x_in[t], 16)
            for u, unit in enumerate(UNITS):
                if u == 4:
                    sp.dma_start(kp_raw, a["cache_sb_k"][0, 0].rearrange("(b p) h d -> p b (h d)", p=P)
                                 ).then_inc(S["kp_in"], 16)
                if u == 8:
                    sp.dma_start(vp_sb, a["cache_sb_v"][0, 0].rearrange("(b p) h d -> p b (h d)", p=P)
                                 ).then_inc(S["vp_in"], 16)
                if BEFORE[u] is not None:
                    sp.wait_ge(S["pj_full"], LAST_OF[BEFORE[u]] + 1)
                if u == OUT_EARLY:
                    sp.wait_ge(S["mix_rest"], 2 + NT)
                    sp.wait_ge(S["pj_full"], MIX1 + 8 * KD)
                    sp.wait_ge(S["so_out"], 32)
                    sp.wait_ge(S["tl_out"], 16 * 6)
                if u == OUTU + 2:
                    sp.wait_ge(S["pj_full"], IDX[("g", KD - 1, 1, 2)] + 1)
                    reload_x(0)
                if unit[0] == "branch":
                    src = a["w_branch_out"][0, unit[1] * W:(unit[1] + 1) * W, 256 * unit[2]:256 * unit[2] + 256]
                    dst = (raw4 if unit[1] else ring4)[SLOT[u]]
                else:
                    w = a[{"in": "w_in", "gate": "w_gate", "out": "w_out"}[unit[0]]]
                    src = w[0, :, unit[1]:unit[1] + P]
                    dst = raw[SLOT[u]]
                sp.dma_start(dst, src.rearrange("(k p) n -> p k n", p=P)).then_inc(unit_in[SLOT[u]], 16)
            for t in range(1, NT):
                reload_x(t)
            def load(kind, i, first, second, turn=0):
                name, dst, used, before, arrived = {
                    "gate": ("w_expert_gate", w_g[turn], "gate_done", 2, wg_in[turn]),
                    "up": ("w_expert_up", w_u, "up_done", 1, S["wu_in"]),
                    "down": ("w_expert_down", w_d, "down_b", 1, S["wd_in"])}[kind]
                if i is not None:
                    sp.wait_ge(S[used], i - before + 1)
                k = (DE if kind == "down" else D) // P
                for j, w in enumerate((first, second)):
                    sp.dma_start(dst[:, k * j:k * (j + 1), :], expert_w(name, w)).then_inc(arrived, 16)

            def expert_w(name, e):
                rows_e = D if name != "w_expert_down" else DE
                v = a[name][0].rearrange("e (k p) f -> p (e k) f", p=P)
                k = rows_e // P
                return v[:, bass.ds(e * k, k), :]

            def store_y(i):
                sp.wait_ge(S["y_a"], i + 1)
                sp.wait_ge(S["y_b"], i + 1)
                sp.dma_start(yd[bass.ds(i * P, P), :], y_out_sb).then_inc(S["y_out"], 16)

            sp.wait_ge(S["gm_r"], 4 * KD)
            sp.wait_ge(S["so_out"], 32)
            sp.wait_ge(S["tl_out"], 16 * 6)
            load("gate", None, 0, EPAIRS)
            sp.wait_ge(S["pj_full"], NITEM)
            for s in range(2):
                sp.wait_ge(u2_out[s], 16 * ((NT + 1 - s) // 2))
            load("up", None, 0, EPAIRS)
            load("down", None, 0, EPAIRS)
            sp.wait_ge(S["xg_in"], 16)
            load("gate", None, 1, 1 + EPAIRS, 1)
            with sp.Fori(0, EPAIRS // 2 - 1) as ii:
                for turn in range(2):
                    i = 2 * ii + turn
                    load("gate", i + 2, i + 2, i + 2 + EPAIRS, turn)
                    load("up", i + 1, i + 1, i + 1 + EPAIRS)
                    load("down", i + 1, i + 1, i + 1 + EPAIRS)
                    store_y(i)
            last = EPAIRS - 1
            load("up", last, last, last + EPAIRS)
            load("down", last, last, last + EPAIRS)
            store_y(last - 1)
            store_y(last)
            sp.wait_ge(S["y_out"], 16 * EPAIRS)
            sp.wait_ge(S["routed"], 2)
            total = sp.value_load(over_total[0:1, 0:1], min_val=0, max_val=OVB)
            for j in range(OPAIRS):
                with sp.If(total > j):
                    ids = [sp.value_load(over_expert[0:1, c:c + 1], min_val=0, max_val=NE - 1)
                           for c in (j, j + OPAIRS)]
                    load("gate", EPAIRS + j, *ids, turn=(EPAIRS + j) % 2)
                    load("up", EPAIRS + j, *ids)
                    load("down", EPAIRS + j, *ids)
                    store_y(EPAIRS + j)
                    sp.wait_ge(S["y_out"], 16 * (EPAIRS + j + 1))
            sp.sem_inc(S["experts_done"], 1)
            sp.wait_ge(S["fin_out"], 16 * NT)
            for name, n in (("v_out", 2), ("tl_out", 6), ("so_out", 2)):
                sp.wait_ge(S[name], 16 * n)
            for s in range(2):
                sp.wait_ge(ko_out[s], 16 * ((NT + 1 - s) // 2))
                sp.wait_ge(u2_out[s], 16 * ((NT + 1 - s) // 2))

        @block.tensor
        def _(pe):
            def gain_turn():
                pe.wait_ge(S["gmix_in"], 16)
                pe.transpose(ms[:, 0:KD], st_a[0:KD, :], ident[0:KD, 0:KD]).then_inc(S["pe_par"], 1)

            def params(_):
                pe.wait_ge(S["consts"], 7)
                pe.wait_ge(S["par_in"], 16 * (len(PAR_ROWS) + 2))
                pe.wait_ge(S["par_up"], 1)
                pe.transpose(ms[:, 0:NPAR], st_a[0:NPAR, :], ident[0:NPAR, 0:NPAR])
                pe.transpose(oa[:, 0:NST], st_b[0:NST, :], ident[0:NST, 0:NST]).then_inc(S["pe_par"], 1)

            def x_turn(t):
                n = TT[t][1]
                z = zz[t % 2]
                if t == 0:
                    pe.wait_ge(S["consts"], 1)
                pe.wait_ge(S["xn_r"], t + 1)
                if t >= 2:
                    pe.wait_ge(S["ut_u"], t - 1)
                for k in range(KD):
                    m = pe.transpose(z[:, k // 4, (k % 4) * P:(k % 4) * P + n], x0[0:n, t, k * P:(k + 1) * P],
                                     ident[0:n, 0:n])
                m.then_inc(S["xt_ps"], 1)

            def product(out, left, right, k, last=KD):
                pe.matmul(out, left[0], right[0], start=k == 0, stop=False)
                pe.matmul(out, left[0], right[1], start=False, stop=False)
                return pe.matmul(out, left[1], right[0], start=False, stop=k == last - 1)

            def item(n):
                it = ITEMS[n]
                kind, c, hh, u, ct = it[:5]
                if n >= 2:
                    wait_drained(pe, n - 2)
                if kind == "q" and c == 0:
                    pe.wait_ge(S["ut_r"], NT if hh else -(-HALF // P))
                s = SLOT.get(u)
                if u in SPLIT_NO:
                    pe.wait_ge(S["rest_r"], SPLIT_NO[u + 1 if kind in "vzo" else u] + 1)
                elif u is not None:
                    pe.wait_ge(unit_in[s], 16 * ARRIVAL[u])
                cols = slice(hh * HALF, (hh + 1) * HALF)
                bank = pj[:, n % 2, :]
                if kind == "b":
                    br = it[5]
                    if hh == 0 and c == 0:
                        pe.wait_ge(*[(S["o_out"], PAIRS + 1), (S["mix_rest"], 2), (S["mix_rest"], 2 + NT)][br])
                    m_cols = slice(ct * P, (ct + 1) * P)
                    for k in range(WT):
                        if br == 0:
                            m = pe.matmul(bank[:, 0:HALF], ring4[s][:, k, m_cols], oAT[:, k, cols],
                                          start=k == 0, stop=k == WT - 1)
                        else:
                            m = product(bank[:, 0:HALF], (ring_r4[:, 2 * s + 1, k, m_cols], ring_r4[:, 2 * s, k, m_cols]),
                                        (out_high[br][:, k, cols], out_rest[br][:, k, cols]), k, WT)
                elif kind == "o":
                    o0, rows_n = TT[c]
                    if n == OUT0:
                        pe.wait_ge(S["mix_rest"], NMIX + 2 * KD)
                    out = bank[0:rows_n, 0:256].rearrange("p (a b) -> p a b", a=2)
                    for k in range(KD):
                        mh, mr = (x[k // 2][:, k % 2, o0:o0 + rows_n] for x in (merged_high, merged_rest))
                        m = product(out, (mh, mr), (pair_r(s, 1, k), pair_r(s, 0, k)), k)
                elif kind in "vz":
                    o0, rows_n = TT[hh]
                    out = bank[0:rows_n, 0:256].rearrange("p (a b) -> p a b", a=2)
                    for k in range(KD):
                        uh, ur = (x[:, k, o0:o0 + rows_n] for x in (u_high_r, u_rest_r))
                        m = product(out, (uh, ur), (pair_r(s, 1, k), pair_r(s, 0, k)), k)
                elif kind == "dt":
                    if hh == 0:
                        pe.wait_ge(S["wdt_r"], 2)
                    for k in range(KD):
                        m = product(bank[0:8, 0:HALF], (w_dt_hr[:, k, :], w_dt_rr[:, k, :]),
                                    (u_high_r[:, k, cols], u_rest_r[:, k, cols]), k)
                else:
                    for k in range(KD):
                        m = product(bank[:, 0:HALF], (high_r[s][:, k, :], rest_r[s][:, k, :]),
                                    (u_high_r[:, k, cols], u_rest_r[:, k, cols]), k)
                m.then_inc(S["pj_full"], 1)

            def past_keys(i):
                if i == 0:
                    pe.wait_ge(S["kp_in"], 16)
                    pe.wait_ge(S["ut_r"], NT)
                z = zz[i // 2]
                for b in range(KB):
                    m = pe.transpose(z[:, i % 2, b * P:(b + 1) * P], kp_raw[:, b, i * P:(i + 1) * P], ident)
                m.then_inc(S["kp_ps"], 1)

            def keys_out(t):
                o0, n = TT[t]
                z = [oa, ms][t % 2]
                if t == 0:
                    pe.wait_ge(S["par_up"], 3)
                    wait_drained(pe, IDX[("k", WT - 1, 1)])
                if t >= 2:
                    pe.wait_ge(S["ko_r"], t - 1)
                for c in range(WT):
                    m = pe.transpose(z[0:n, c * P:(c + 1) * P], kT[:, c, o0:o0 + n], ident)
                m.then_inc(S["ko_ps"], 1)

            def dt_turn(_):
                wait_drained(pe, IDX[("dt", 0, 1)])
                pe.wait_ge(S["ko_r"], NT)
                for t, (o0, n) in enumerate(TT):
                    m = pe.transpose(ms[0:n, t * 8:t * 8 + 8], dtT[0:8, o0:o0 + n], ident[0:8, 0:8])
                m.then_inc(S["dt_ps"], 1)

            def att_scores(u):
                kind, hp, kb = ATT[u]
                z = zz[u % 2]
                if u == 0:
                    wait_drained(pe, IDX[("q", WT - 1, 1)])
                    wait_drained(pe, IDX[("k", WT - 1, 1)])
                    pe.wait_ge(S["q_zero"], 1)
                    pe.wait_ge(S["kp_r"], 4)
                if u >= 2:
                    pe.wait_ge(S["w_r_"], u - 1)
                if kind == "p":
                    q0 = kb * P
                    for e in range(2):
                        m = pe.matmul(z[:, e, 0:SEQ - q0], kT[:, hp, q0:q0 + P], q2[:, e, hp, q0:SEQ],
                                      start=True, stop=False, skip_group_check=True)
                else:
                    n = P if kb < KB else DEC
                    for c in range(PAIRS):
                        key = kpT[:, c, kb * P:(kb + 1) * P] if kb < KB else kT[:, c, SEQ:T]
                        m = pe.matmul(z[0:n, 0, c * P:(c + 1) * P], key, q2[:, :, c, SEQ:T],
                                      start=c == 0, stop=False, skip_group_check=True)
                m.then_inc(S["z_r"], 1)

            def att_after(u):
                kind, hp, kb = ATT[u]
                z = zz[u % 2]
                pe.wait_ge(S["sp_r"], u + 1)
                first = kb == (KB - 1 if kind == "p" else KB)
                if not first or kind == "d":
                    pe.wait_ge(S["s_sum"], u)
                b = att_b[u % 2]
                sums = att_s
                if kind == "p":
                    n = SEQ - kb * P
                    for e in range(2):
                        if not first:
                            pe.matmul(z[:, e, P:n], neg_ones, sums[:, e, 0:n - P],
                                      start=False, stop=False, skip_group_check=True)
                        m = pe.matmul(z[:, e, 0:n], neg_l, b[:, e, 0:n],
                                      start=False, stop=True, skip_group_check=True)
                else:
                    n = P if kb < KB else DEC
                    if not first:
                        pe.matmul(z[:, 0, :], neg_ones, sums[:, 0, :], start=False, stop=False,
                                  skip_group_check=True)
                    m = pe.matmul(z[0:n, 0, :], neg_l[0:n, 0:n], b[0:n, 0, :], start=False, stop=True,
                                  skip_group_check=True)
                m.then_inc(S["zw_r"], 1)

            def att_values(u):
                kind, hp, kb = ATT[u]
                w = att_a[u % 2]
                if u == 0:
                    wait_drained(pe, IDX[("v", 1, NT - 1)])
                    pe.wait_ge(S["vp_in"], 16)
                    pe.wait_ge(S["ko_r"], NT)
                pe.wait_ge(S["w_r_"], u + 1)
                if kind == "p":
                    q0 = kb * P
                    if kb == KB - 1 and hp > 0:
                        pe.wait_ge(S["o_out"], hp)
                    for e in range(2):
                        c0 = (2 * hp + e) * HD
                        m = pe.matmul(oa[e * HD:(e + 1) * HD, q0:SEQ], v_sb[:, kb, c0:c0 + HD],
                                      w[:, e, 0:SEQ - q0], start=kb == KB - 1, stop=kb == 0,
                                      skip_group_check=True)
                else:
                    if kb == KB:
                        pe.wait_ge(S["o_out"], PAIRS)
                    n = P if kb < KB else DEC
                    for c in range(PAIRS):
                        for e in range(2):
                            c0 = (2 * c + e) * HD
                            v = vp_sb[:, kb, c0:c0 + HD] if kb < KB else v_sb[0:n, kb, c0:c0 + HD]
                            w0 = c * P + e * HD
                            m = pe.matmul(oa[e * HD:(e + 1) * HD, c * HD:(c + 1) * HD], v,
                                          w[0:n, 0, w0:w0 + HD], start=kb == KB and c == 0, stop=kb == 0,
                                          skip_group_check=True)
                m.then_inc(S["o_r"], 1)

            def state_in(_):
                pe.wait_ge(S["lruw_in"], 16 * 5)
                pe.wait_ge(S["dt_raw"], 1)
                for j in range(WT):
                    m = pe.transpose(ms[:, j * P:(j + 1) * P], ss_in[:, j, :], ident)
                m.then_inc(S["hs_ps"], 1)

            def ssm_turn(t):
                lo, n = tw_cols(t)
                if t == 0:
                    pe.wait_ge(S["silu_r"], XT)
                    pe.wait_ge(S["hs_r"], 1)
                    pe.wait_ge(S["o_out"], PAIRS + 1)
                else:
                    pe.wait_ge(S["turn_r"], 2 * t)
                for j in range(6):
                    z = ms if j < WT else oa
                    m = pe.transpose(z[0:n, (j % WT) * P:(j % WT + 1) * P], xconv[:, j, lo:lo + n], ident)
                m.then_inc(S["turn_ps"], 1)

            def lru(c):
                if c == 0:
                    pe.wait_ge(S["lruw_in"], 16 * 5)
                    pe.wait_ge(S["conv_c"], XT + WT)
                else:
                    pe.wait_ge(S["lru_tr"], 2 * c)
                for g in range(2):
                    for hh in range(2):
                        m = pe.matmul(zz[g][:, hh, 0:TW // 2], lru_w[:, g, c, :],
                                      xc[:, c, hh * (TW // 2):(hh + 1) * (TW // 2)], start=True, stop=True)
                m.then_inc(S["lru_ps"], 1)

            def ssd_decay(c):
                o0, n = TT[c]
                pe.wait_ge(S["td_r"], c + 1)
                if c == 0:
                    pe.wait_ge(S["lru_tr"], 2 * WT)
                else:
                    pe.wait_ge(S["m_r"], c)
                    pe.wait_ge(S["ea_r"], c)
                td = at(td_flat, HEADS, n)
                if n == P:
                    for b in range(2):
                        pe.matmul(za[:, b, :], ones[0:n, :], td[0:n, b * 4:(b + 1) * 4, :], start=True, stop=True)
                else:
                    pe.matmul(za[:, 0, :], ones[0:n, :], td[0:n, :, :], start=True, stop=True)
                pe.matmul(zb[0:n, 0, 256:264], u_incl[0:n, 0:n], dA[0:n, c, :], start=True, stop=True)
                lo, _ = tw_cols(c)
                for g in range(GROUPS):
                    m = pe.matmul(zb[0:n, 0, g * n:(g + 1) * n], xconv[:, 4 + g, lo:lo + n],
                                  xconv[:, 6 + g, lo:lo + n], start=True, stop=True)
                m.then_inc(S["dec_ps"], 1)

            def ssd_mix(c):
                o0, n = TT[c]
                lo, _ = tw_cols(c)
                pe.wait_ge(S["m_r"], c + 1)
                pe.wait_ge(S["xdd_r"], c + 1)
                if c == 0:
                    pe.wait_ge(S["turn_r"], 2 * NT)
                else:
                    pe.wait_ge(S["h_r"], c)
                    pe.wait_ge(S["oc_r"], c)
                    if c == NT - 1:
                        pe.wait_ge(S["so_r"], 1)
                m_sb = at(m_flat, HEADS, n)
                for hd in range(HEADS):
                    pe.matmul(zb[0:n, 1, hd * HD:(hd + 1) * HD], m_sb[0:n, hd, :], xdt[0:n, hd, :],
                              start=True, stop=True)
                if c > 0:
                    state = hT if c < NT - 1 else hS
                    for g in range(GROUPS):
                        pe.matmul(oa[0:n, g * 256:(g + 1) * 256], xconv[:, 6 + g, lo:lo + n],
                                  state[:, g * 256:(g + 1) * 256], start=True, stop=True)
                for g in range(GROUPS):
                    m = pe.matmul(ms[:, g * 256:(g + 1) * 256], b_tok[0:n, c, g * P:(g + 1) * P],
                                  xdd[0:n, 4 * g:4 * g + 4, :], start=True, stop=True)
                m.then_inc(S["mix_ps"], 1)

            def ssd_turn(c):
                o0, n = TT[c]
                pe.wait_ge(S["yn_r"], c + 1)
                if c == 0:
                    pe.wait_ge(S["tl_r"], 1)
                for j in range(WT):
                    m = pe.transpose(oa[:, j * P:j * P + n], y_sb[0:n, j * P:(j + 1) * P], ident[0:n, 0:n])
                m.then_inc(S["yt_ps"], 1)

            def tails_turn(_):
                pe.wait_ge(S["lru_h"], 2 * WT)
                pe.wait_ge(S["turn_r"], 2 * NT)
                pe.transpose(oa[0:TAILS, 0:P], tails, ident).then_inc(S["tl_ps"], 1)

            def state_out(i):
                pe.wait_ge(S["h_r"], NT - 1 + i)
                state = [hT, hS][i]
                for j in range(WT):
                    m = pe.transpose(ms[:, j * P:(j + 1) * P], state[:, j * P:(j + 1) * P], ident)
                m.then_inc(S["so_ps"], 1)

            def ffn_turn(t):
                o0, n = TT[t]
                z = zz[t % 2]
                pe.wait_ge(S["u2_r"], t + 1)
                if t >= 2:
                    pe.wait_ge(S["u2t_r"], t - 1)
                for k in range(KD):
                    m = pe.transpose(z[:, k // 4, (k % 4) * P:(k % 4) * P + n], u2[t % 2][0:n, k * P:(k + 1) * P],
                                     ident[0:n, 0:n])
                m.then_inc(S["u2t_ps"], 1)
                if t == 0:
                    pe.wait_ge(S["side_dma"], 48)
                    pe.wait_ge(S["so_r"], 2)
                pe.wait_ge(S["u2t_r"], t + 1)
                for k in range(KD):
                    m = pe.matmul(ms[0:n, t * 36:(t + 1) * 36], u2T[t % 2][:, k, 0:n], w_r[:, k, :],
                                  start=k == 0, stop=k == KD - 1)
                m.then_inc(S["lg_ps"], 1)

            def expert_pair(i, turn, before=True):
                pe.wait_ge(S["xg_in"], (i + 1) * 16)
                if before:
                    pe.wait_ge(S["hidt_r"], i)
                for k in range(KD):
                    z = oa if k < KD // 2 else ms
                    m = pe.transpose(z[:, (k % 4) * P:(k % 4 + 1) * P], xg[:, k * P:(k + 1) * P], ident)
                m.then_inc(S["xt2_ps"], 1)
                pe.wait_ge(S["xt2_a"], i + 1)
                pe.wait_ge(S["xt2_d"], i + 1)
                par, n_turn = turn
                for b, (w, done) in enumerate(((w_g[par], "gate_done"), (w_u, "up_done"))):
                    if b == 0:
                        pe.wait_ge(wg_in[par], (n_turn + 1) * 32)
                    else:
                        pe.wait_ge(S["wu_in"], (i + 1) * 32)
                    for k in range(KD):
                        for j in range(2):
                            m = pe.matmul(za[j * BLK:(j + 1) * BLK, b, :], xT[:, k, j * BLK:(j + 1) * BLK],
                                          w[:, j * KD + k, :], start=k == 0, stop=k == KD - 1)
                    m.then_inc(S[done], 1)
                pe.wait_ge(S["hid_r"], i + 1)
                for k in range(DE // P):
                    m = pe.transpose(oa[:, k * P:(k + 1) * P], hid[:, k * P:(k + 1) * P], ident)
                m.then_inc(S["hidt_ps"], 1)
                pe.wait_ge(S["hidt_r"], i + 1)
                pe.wait_ge(S["wd_in"], (i + 1) * 32)
                for q, (done, free) in enumerate((("down_a", "y_a"), ("down_b", "y_b"))):
                    if before:
                        pe.wait_ge(S[free], i)
                    for k in range(DE // P):
                        for j in range(2):
                            m = pe.matmul(zb[j * BLK:(j + 1) * BLK, q, :], hidT[:, k, j * BLK:(j + 1) * BLK],
                                          w_d[:, j * (DE // P) + k, q * 512:(q + 1) * 512],
                                          start=k == 0, stop=k == DE // P - 1)
                    m.then_inc(S[done], 1)

            def ranks():
                pe.wait_ge(S["route_in"], 1)
                pe.matmul(ms[:, 0:NT * NE], u_strict, hot_sum, start=True, stop=False)
                pe.matmul(ms[:, 0:NT * NE], ones, tile_base[:, 0:NT, :], start=False, stop=True)
                pe.matmul(ms[:, NT * NE:(NT + 1) * NE], ones, tile_base[:, NT, :], start=True, stop=True
                          ).then_inc(S["route_ps"], 1)

            def table():
                pe.wait_ge(S["route_in"], 2)
                for c in range(2 * NT):
                    m = pe.matmul(ms[:, 0:NPC], place_hot[:, c, :], col_hot[:, c, :], start=c == 0,
                                  stop=c == 2 * NT - 1)
                m.then_inc(S["route_ps"], 1)

            steps = {f.__name__: f for f in (past_keys, keys_out, dt_turn, att_scores, att_after, att_values,
                                             state_in, ssm_turn, lru, ssd_decay, ssd_mix, ssd_turn, tails_turn,
                                             state_out, ffn_turn, params)}
            for t in range(NT):
                x_turn(t)
                if t == 0:
                    gain_turn()
            for n in range(NITEM + 1):
                for name, args in JOBS.get(n, []):
                    if name in steps:
                        steps[name](*args)
                if n < NITEM:
                    item(n)
            ranks()
            table()
            expert_pair(0, (0, 0), before=False)
            expert_pair(1, (1, 0))
            with pe.Fori(1, EPAIRS // 2) as ii:
                expert_pair(2 * ii, (0, ii))
                expert_pair(2 * ii + 1, (1, ii))
            pe.wait_ge(S["routed"], 2)
            total = pe.value_load(over_total[0:1, 0:1], min_val=0, max_val=OVB)
            for j in range(OPAIRS):
                with pe.If(total > j):
                    expert_pair(EPAIRS + j, ((EPAIRS + j) % 2, (EPAIRS + j) // 2))

        @block.scalar
        def _(act):
            act.dma_start(st_a[0:KD, :], a["g_mix"][0].rearrange("(r p) -> r p", p=P)).then_inc(S["gmix_in"], 16)

            def x_norm(t):
                n = TT[t][1]
                act.wait_ge(x_in[t], 16)
                act.activation(junk[0:n, :], x0[0:n, t, :], ACT.Square, accum_out=ssq[0:n, t:t + 1]
                               ).then_inc(S["ssq_r"], 1)
                act.wait_ge(S["var_r"], t + 1)
                act.activation(rstd[0:n, t:t + 1], ssq[0:n, t:t + 1], ACT.Sqrt).then_inc(S["std_r"], 1)

            def gain_up():
                act.wait_ge(S["pe_par"], 1)
                act.activation(gains_mix, ms[:, 0:KD], ACT.Copy).then_inc(S["par_up"], 1)

            def u_split(t):
                o0, n = TT[t]
                act.wait_ge(S["ut_u"], t + 1)
                act.activation(u_high_r[:, :, o0:o0 + n], u_rest[:, :, o0:o0 + n], ACT.Copy).then_inc(S["ut_h"], 1)

            def split(u):
                s = SLOT[u]
                act.wait_ge(unit_in[s], 16 * ARRIVAL[u])
                act.activation(high_r[s], raw[s], ACT.Copy).then_inc(S["high_r"], 1)

            def merged_split(c, hh):
                v = slice(hh * HALF, (hh + 1) * HALF)
                act.wait_ge(S["gm_r"], 2 * KD + 2 * c + hh + 1)
                act.activation(merged_high[c // 2][:, c % 2, v], merged[c // 2][:, c % 2, v], ACT.Copy
                               ).then_inc(S["mix_high"], 1)

            def mix_split(br, i):
                k, cols = mix_part(br, i)
                act.wait_ge(*((S["ob_r"], WT) if br == 1 else (S["oc_r"], i + 1)))
                if br == 2 and i == 0:
                    act.wait_ge(S["pj_full"], MIX1 + 4 * KD)
                act.activation(out_high[br][:, k, cols], out_mix[br][:, k, cols], ACT.Copy).then_inc(S["mix_high"], 1)

            def params(_):
                act.wait_ge(S["par_in"], 16 * (len(PAR_ROWS) + 2))
                act.activation(w_dt_hr, w_dt, ACT.Copy).then_inc(S["wdt_r"], 1)
                act.wait_ge(S["pe_par"], 2)
                act.wait_ge(S["ut_u"], NT)
                act.activation(cpar, ms[:, 0:NPAR], ACT.Copy).then_inc(S["par_up"], 1)
                act.activation(cst, oa[:, 0:NST], ACT.Copy).then_inc(S["par_up"], 1)

            def item(n):
                it = ITEMS[n]
                kind, c, hh = it[:3]
                if kind in DVE_KINDS:
                    return
                act.wait_ge(S["pj_full"], n + 1)
                bank = pj[:, n % 2, :]
                lo = hh * HALF
                if kind == "q":
                    if n == 0:
                        act.wait_ge(S["q_zero"], 1)
                    act.activation(q2[0:HD, 0, c, lo:lo + HALF], bank[0:HD, 0:HALF], ACT.Copy, scale=HD ** -0.5)
                    m = act.activation(q2[HD:P, 1, c, lo:lo + HALF], bank[HD:P, 0:HALF], ACT.Copy,
                                       scale=HD ** -0.5)
                elif kind in "vz":
                    t, r = hh, TT[hh][1]
                    if n == IDX[("z", 0, 0)]:
                        act.wait_ge(ko_out[0], 16 * 3)
                        act.wait_ge(ko_out[1], 16 * 2)
                        act.wait_ge(S["dt_ps"], 1)
                    dst = v_sb if kind == "v" else z2
                    m = act.activation(dst[0:r, t, 256 * c:256 * (c + 1)], bank[0:r, 0:256], ACT.Copy,
                                       scale=1.0 if kind == "v" else 0.5)
                elif kind == "dt":
                    if hh == 0:
                        act.wait_ge(S["xt_ps"], NT)
                    m = act.activation(dtT[0:8, lo:lo + HALF], bank[0:8, 0:HALF], ACT.Copy)
                elif kind in ("x", "r"):
                    j = c + (XT if kind == "r" else 0)
                    dst = xp[j % 2]
                    if j < 2 and hh == 0:
                        act.wait_ge(S["masked"], 1)
                    if j >= 2 and hh == 0:
                        act.wait_ge(S["conv_c"], j - 1)
                    if hh == 0:
                        m = act.activation(dst[:, GAP:GAP + HALF], bank[:, 0:HALF], ACT.Copy)
                    else:
                        act.activation(dst[:, GAP + HALF:GAP + SEQ], bank[:, 0:SEQ - HALF], ACT.Copy)
                        m = act.activation(dst[:, SAMP + GAP:SAMP + GAP + DEC], bank[:, SEQ - HALF:HALF], ACT.Copy)
                elif kind == "gb":
                    if hh == 0:
                        m = act.activation(gb[:, c, 0:HALF], bank[:, 0:HALF], ACT.Copy)
                    else:
                        act.activation(gb[:, c, HALF:SEQ], bank[:, 0:SEQ - HALF], ACT.Copy)
                        m = act.activation(gb[:, c, SAMP:SAMP + DEC], bank[:, SEQ - HALF:HALF], ACT.Copy)
                elif kind == "g":
                    br = it[5]
                    k = (n - MIX1) // 2
                    if k == 0:
                        act.wait_ge(S["conv_c"], XT + WT)
                        act.wait_ge(S["s_sum"], NATT)
                    if k >= 2:
                        wait_drained(act, n - 3)
                    j = PAR["b_gate"] + br * KD + c
                    m = act.activation(gsb[k % 2], bank[:, 0:HALF], ACT.Tanh, scale=0.5, bias=cpar[:, j:j + 1])
                m.then_inc(S["pj_act"], 1)
                if n == IDX[("v", 1, NT - 1)]:
                    act.wait_ge(*drained(n))
                    act.dma_start(o["v_p"][0, 0].rearrange("(t p) h d -> p t (h d)", p=P),
                                  v_sb[:, 0:NT - 1, :]).then_inc(S["v_out"], 16)
                    act.dma_start(o["v_s"][0, 0].rearrange("s h d -> s (h d)"),
                                  v_sb[0:DEC, NT - 1, :]).then_inc(S["v_out"], 16)

            def keys_out(t):
                o0, n = TT[t]
                act.wait_ge(S["ko_ps"], t + 1)
                if t == 0:
                    act.wait_ge(S["xt_ps"], NT)
                if t >= 2:
                    act.wait_ge(ko_out[t % 2], 16 * (t // 2))
                act.activation(ko[t % 2][0:n, :], [oa, ms][t % 2][0:n, :], ACT.Copy).then_inc(S["ko_r"], 1)
                act.wait_ge(S["ko_r"], t + 1)
                dst = o["k_p"][0, 0, o0:o0 + n] if t < NT - 1 else o["k_s"][0, 0]
                act.dma_start(dst.rearrange("s h d -> s (h d)"), ko[t % 2][0:n, :]).then_inc(ko_out[t % 2], 16)

            def dt_turn(_):
                act.wait_ge(S["sp_dve"], 1)
                act.activation(sp_e, sp_e, ACT.Exp).then_inc(S["sp_act"], 1)
                act.activation(a_exp, rowc[:, 8:16], ACT.Exp).then_inc(S["sp_act"], 1)
                act.wait_ge(S["sp_dve"], 2)
                act.activation(sp_l, sp_u, ACT.Ln).then_inc(S["sp_act"], 1)

            def att_scores(u):
                b = att_view(att_a[u % 2], u)
                act.wait_ge(S["nab_r"], u + 1)
                act.activation(b, b, ACT.Exp).then_inc(S["ln_e"], 1)
                act.wait_ge(S["ln_e"], u + 1)
                act.activation(b, b, ACT.Ln, bias=1.0).then_inc(S["l_r"], 1)

            def att_after(u):
                act.wait_ge(S["zw_r"], u + 1)
                act.activation(att_view(att_a[u % 2], u), att_view(zz[u % 2], u), ACT.Exp).then_inc(S["w_r_"], 1)

            def att_values(u):
                kind, hp, kb = ATT[u]
                if kb == 0:
                    act.wait_ge(S["o_r"], u + 1)
                    if kind == "p":
                        act.activation(oAT[:, hp, 0:SEQ], oa[:, :], ACT.Copy).then_inc(S["o_out"], 1)
                    else:
                        act.activation(oAT[:, :, SEQ:T], oa[:, 0:PAIRS * HD].rearrange("p (c q) -> p c q", c=PAIRS),
                                       ACT.Copy).then_inc(S["o_out"], 1)

            def silu(i):
                if i == 0:
                    act.wait_ge(S["o_r"], NATT)
                    act.wait_ge(S["s_sum"], NATT)
                if i >= 2:
                    act.wait_ge(S["silu_r"], i - 1)
                act.wait_ge(S["conv_c"], i + 1)
                act.activation(th[i % 2], xconv[:, i, :], ACT.Tanh).then_inc(S["silu_t"], 1)

            def state_in(_):
                act.wait_ge(S["hs_ps"], 1)
                act.activation(hS, ms[:, :], ACT.Copy).then_inc(S["hs_r"], 1)

            def ssm_turn(t):
                n = TT[t][1]
                act.wait_ge(S["turn_ps"], t + 1)
                act.activation(b_tok[0:n, t, :], oa[0:n, 0:256], ACT.Copy).then_inc(S["turn_r"], 1)

            def both(z):
                return z[:, :, 0:TW // 2]

            def lru(c):
                r, i, la, m, gl = [x.rearrange("p (a b) -> p a b", a=2) for x in lt]
                act.wait_ge(S["lru_ps"], c + 1)
                if c > 0:
                    act.wait_ge(S["ob_r"], c)
                ba = PAR["lru_b_a"] + c
                bx = PAR["lru_b_x"] + c
                act.activation(r, both(za), ACT.Tanh, scale=0.5, bias=cpar[:, ba:ba + 1]).then_inc(S["lru_tr"], 1)
                act.activation(i, both(zb), ACT.Tanh, scale=0.5, bias=cpar[:, bx:bx + 1]).then_inc(S["lru_tr"], 1)
                act.wait_ge(S["lru_tr"], 2 * c + 2)
                act.activation(la, r, ACT.Exp, scale=ls4[:, c:c + 1], bias=ls4[:, c:c + 1]
                               ).then_inc(S["lru_ac"], 1)
                act.activation(r, r, ACT.Tanh, scale=ls4n[:, c:c + 1], bias=ls4n[:, c:c + 1]
                               ).then_inc(S["lru_ac"], 1)
                act.wait_ge(S["lru_pool"], 4 * c + 3)
                act.activation(gl, gl, ACT.Tanh, scale=GELU_C).then_inc(S["lru_gt"], 1)

            def lru_scan(c):
                r, _, _, m, _ = [x.rearrange("p (a b) -> p a b", a=2) for x in lt]
                act.wait_ge(S["lru_m2"], c + 1)
                act.activation(r, m, ACT.Sqrt).then_inc(S["lru_mu"], 1)

            def ssd_decay(c):
                n = TT[c][1]
                act.wait_ge(S["acs_r"], c + 1)
                if c == 0:
                    act.wait_ge(S["ob_r"], WT)
                act.activation(ea[0:n, :], acs[0:n, :], ACT.Exp)
                act.wait_ge(S["d_r"], c + 1)
                if c > 1:
                    act.wait_ge(S["hcd_r"], c - 1)
                last = za[:, :, :].rearrange("p a (b l) -> p (a b) l", l=P)[:, :, P - 1] if n == P else \
                    za[:, 0, :].rearrange("p (b l) -> p b l", l=n)[:, :, n - 1]
                act.activation(cd, last, ACT.Exp).then_inc(S["ea_r"], 1)

            def ssd_exp(c):
                n = TT[c][1]
                act.wait_ge(S["em_r"], c + 1)
                e = at(e_flat, HEADS, n)[0:n]
                act.activation(e, e, ACT.Exp).then_inc(S["e_r"], 1)
                if c > 0:
                    act.wait_ge(S["yg_r"], c)
                act.activation(tz[0:n, :], z2[0:n, c, :], ACT.Tanh).then_inc(S["tz_r"], 1)

            def ssd_norm(c):
                n = TT[c][1]
                act.wait_ge(S["yg_r"], c + 1)
                for g in range(GROUPS):
                    m = act.activation(y_off_sb[0:n, g * 256:(g + 1) * 256], y_sb[0:n, g * 256:(g + 1) * 256],
                                       ACT.Square, accum_out=ssy[0:n, g:g + 1])
                m.then_inc(S["ssy_r"], 1)
                act.wait_ge(S["vy_r"], c + 1)
                act.activation(rsy[0:n, :], ssy[0:n, :], ACT.Sqrt).then_inc(S["sy_r"], 1)

            def tails_turn(_):
                act.wait_ge(S["tl_ps"], 1)
                act.wait_ge(S["ob_r"], WT)
                act.activation(tail_row[0:TAILS, :], oa[0:TAILS, 0:P], ACT.Copy).then_inc(S["tl_r"], 1)
                act.wait_ge(S["tl_r"], 1)
                for q, tag in enumerate("ps"):
                    r0 = q * 36
                    act.dma_start(o["lru_conv_" + tag][0, 0].rearrange("k (r p) -> (k r) p", p=P),
                                  tail_row[r0:r0 + 12, :]).then_inc(S["tl_out"], 16)
                    act.dma_start(o["ssm_conv_" + tag][0, 0].rearrange("k (r p) -> (k r) p", p=P),
                                  tail_row[r0 + 12:r0 + 36, :]).then_inc(S["tl_out"], 16)
                    act.dma_start(o["lru_h_" + tag][0, 0].rearrange("(r p) -> r p", p=P),
                                  tail_row[72 + 4 * q:76 + 4 * q, :]).then_inc(S["tl_out"], 16)

            def state_out(i):
                act.wait_ge(S["so_ps"], i + 1)
                if i == 1:
                    act.wait_ge(S["so_out"], 16)
                act.activation(h_out, ms[:, :].rearrange("p (j n) -> p j n", j=WT), ACT.Copy).then_inc(S["so_r"], 1)
                act.wait_ge(S["so_r"], i + 1)
                act.dma_start(o["ssm_h_" + "ps"[i]][0, 0].rearrange("(j q) p n -> (q p) j n", q=2), h_out
                              ).then_inc(S["so_out"], 16)

            def ffn_norm(t):
                n = TT[t][1]
                wait_drained(act, IDX[("o", t, 3)])
                if t >= 2:
                    act.wait_ge(S["u2t_ps"], t - 1)
                    act.wait_ge(u2_out[t % 2], 16 * (t // 2))
                act.activation(u2[t % 2][0:n, :], h[0:n, t, :], ACT.Square, accum_out=ss2[0:n, t:t + 1]
                               ).then_inc(S["ssq_r"], 1)
                act.wait_ge(S["var_r"], NT + t + 1)
                act.activation(rs2[0:n, t:t + 1], ss2[0:n, t:t + 1], ACT.Sqrt).then_inc(S["std_r"], 1)

            def ffn_turn(t):
                o0, n = TT[t]
                act.wait_ge(S["u2_r"], t + 1)
                act.dma_start(u2d[o0:o0 + n, :], u2[t % 2][0:n, :]).then_inc(u2_out[t % 2], 16)
                act.wait_ge(S["u2t_ps"], t + 1)
                if t >= 2:
                    act.wait_ge(S["lg_ps"], t - 1)
                act.activation(u2T[t % 2][:, :, 0:n], zz[t % 2][:, :, :].rearrange("p a (b l) -> p (a b) l", l=P)
                               [:, :, 0:n], ACT.Copy).then_inc(S["u2t_r"], 1)

            def routing():
                act.wait_ge(S["fexp_in"], 1)
                act.activation(for_exp, for_exp, ACT.Exp).then_inc(S["fexp_r"], 1)

            def expert_pair(i, turn, before=True):
                act.wait_ge(S["xt2_ps"], i + 1)
                act.activation(xT[:, 0:KD // 2, :], oa[:, :].rearrange("p (k l) -> p k l", k=4), ACT.Copy
                               ).then_inc(S["xt2_a"], 1)
                act.wait_ge(S["gate_done"], i + 1)
                act.activation(gate_t, za[:, 0, :], ACT.Tanh, scale=0.5).then_inc(S["gate_th"], 1)
                act.wait_ge(S["down_a"], i + 1)
                if before:
                    act.wait_ge(S["y_out"], i * 16)
                act.activation(y_out_sb[:, 0:512], zb[:, 0, :], ACT.Copy).then_inc(S["y_a"], 1)

            def final(t):
                o0, n = TT[t]
                act.wait_ge(S["hy_r"], t + 1)
                act.activation(y_back[t % 2][0][0:n, :], h[0:n, t, :], ACT.Square, accum_out=ss3[0:n, t:t + 1]
                               ).then_inc(S["ssq_r"], 1)
                act.wait_ge(S["var_r"], 2 * NT + t + 1)
                act.activation(rs3[0:n, t:t + 1], ss3[0:n, t:t + 1], ACT.Sqrt).then_inc(S["std_r"], 1)
                act.wait_ge(S["fin_r"], t + 1)
                dst = o["y_p"][0, o0:o0 + n, :] if t < NT - 1 else o["y_s"][0]
                act.dma_start(dst, h[0:n, t, :]).then_inc(S["fin_out"], 16)

            steps = {f.__name__: f for f in (keys_out, dt_turn, att_scores, att_after, att_values, silu, state_in,
                                             ssm_turn, lru, lru_scan, ssd_decay, ssd_exp, ssd_norm, tails_turn,
                                             state_out, ffn_norm, ffn_turn, split, mix_split, merged_split, params)}
            for t in range(NT):
                x_norm(t)
                if t == 1:
                    gain_up()
                if t > 1:
                    u_split(t - 2)
            u_split(NT - 2)
            u_split(NT - 1)
            for n in range(NITEM + 1):
                for name, args in JOBS.get(n, []):
                    if name in steps:
                        steps[name](*args)
                if n < NITEM:
                    item(n)
            routing()
            expert_pair(0, (0, 0), before=False)
            expert_pair(1, (1, 0))
            with act.Fori(1, EPAIRS // 2) as ii:
                expert_pair(2 * ii, (0, ii))
                expert_pair(2 * ii + 1, (1, ii))
            act.wait_ge(S["routed"], 2)
            total = act.value_load(over_total[0:1, 0:1], min_val=0, max_val=OVB)
            for j in range(OPAIRS):
                with act.If(total > j):
                    expert_pair(EPAIRS + j, ((EPAIRS + j) % 2, (EPAIRS + j) // 2))
            for t in range(NT):
                final(t)

        def bc(v, *shape):
            return v.to_broadcast(list(shape))

        @block.vector
        def _(dve):
            links = [0]

            def link(ins):
                links[0] += 1
                ins.then_inc(S["dve_c"], 1)
                dve.wait_ge(S["dve_c"], links[0])

            def x_norm(t):
                n = TT[t][1]
                dve.wait_ge(S["ssq_r"], t + 1)
                dve.tensor_scalar(ssq[0:n, t:t + 1], ssq[0:n, t:t + 1], 1.0 / D, EPS, ALU.mult, ALU.add
                                  ).then_inc(S["var_r"], 1)
                dve.wait_ge(S["std_r"], t + 1)
                link(dve.reciprocal(rstd[0:n, t:t + 1], rstd[0:n, t:t + 1]))
                dve.tensor_scalar(x0[0:n, t, :], x0[0:n, t, :], rstd[0:n, t:t + 1], None, ALU.mult
                                  ).then_inc(S["xn_r"], 1)

            def x_turn(t):
                o0, n = TT[t]
                z = zz[t % 2]
                dve.wait_ge(S["xt_ps"], t + 1)
                if t == 0:
                    dve.wait_ge(S["par_up"], 1)
                for b in range(2):
                    m = dve.tensor_tensor(u_rest[:, 4 * b:4 * b + 4, o0:o0 + n],
                                          z[:, b, :].rearrange("p (k l) -> p k l", k=4)[:, :, 0:n],
                                          bc(gains_mix[:, 4 * b:4 * b + 4].unsqueeze(2), P, 4, n), ALU.mult)
                m.then_inc(S["ut_u"], 1)

            def u_split(t):
                o0, n = TT[t]
                dve.wait_ge(S["ut_h"], t + 1)
                v = slice(o0, o0 + n)
                dve.tensor_tensor(u_rest_r[:, :, v], u_rest[:, :, v], u_high_r[:, :, v], ALU.subtract
                                  ).then_inc(S["ut_r"], 1)

            def split(u):
                s = SLOT[u]
                dve.wait_ge(S["high_r"], SPLIT_NO[u] + 1)
                dve.tensor_tensor(rest_r[s], raw[s], high_r[s], ALU.subtract).then_inc(S["rest_r"], 1)

            def merged_split(c, hh):
                v = slice(hh * HALF, (hh + 1) * HALF)
                dve.wait_ge(S["mix_high"], NMIX + 2 * c + hh + 1)
                dve.tensor_tensor(merged_rest[c // 2][:, c % 2, v], merged[c // 2][:, c % 2, v],
                                  merged_high[c // 2][:, c % 2, v], ALU.subtract).then_inc(S["mix_rest"], 1)

            def mix_split(br, i):
                k, cols = mix_part(br, i)
                dve.wait_ge(S["mix_high"], (i if br == 1 else i + 2) + 1)
                dve.tensor_tensor(out_rest[br][:, k, cols], out_mix[br][:, k, cols], out_high[br][:, k, cols],
                                  ALU.subtract).then_inc(S["mix_rest"], 1)

            def params(_):
                par_half()
                dve.wait_ge(S["wdt_r"], 1)
                dve.tensor_tensor(w_dt_rr, w_dt, w_dt_hr, ALU.subtract
                                  ).then_inc(S["wdt_r"], 1)

            def par_half():
                dve.wait_ge(S["par_up"], 3)
                for name, k in (("b_gate", 24), ("ssm_conv_w", 40), ("lru_b_a", 8)):
                    v = cpar[:, PAR[name]:PAR[name] + k]
                    m = dve.tensor_scalar(v, v, 0.5, None, ALU.mult)
                lam = cpar[:, PAR["lru_lambda"]:PAR["lru_lambda"] + 4]
                dve.tensor_scalar(sp_x[:, 40:44], lam, -1.0, None, ALU.mult)

            def item(n):
                it = ITEMS[n]
                kind, c, hh = it[:3]
                if kind not in DVE_KINDS:
                    return
                dve.wait_ge(S["pj_full"], n + 1)
                bank = pj[:, n % 2, :]
                lo = hh * HALF
                if kind == "k":
                    m = dve.tensor_copy(kT[:, c, lo:lo + HALF], bank[:, 0:HALF])
                elif kind == "b":
                    br = it[5]
                    k = (n - MIX1) // 2
                    wait_drained(dve, n - 1)
                    dst = merged[c // 2][:, c % 2, lo:lo + HALF] if br == 0 else gtmp[k % 2]
                    if k == 0:
                        dve.wait_ge(S["v_out"], 32)
                    if br > 0:
                        kk = k - 2 * KD
                        if kk >= 2:
                            dve.wait_ge(S["gm_r"], kk - 1)
                    m = dve.scalar_tensor_tensor(out=dst, in0=gsb[k % 2], scalar=1.0, in1=bank[:, 0:HALF],
                                                 op0=ALU.add, op1=ALU.mult)
                elif kind == "o":
                    t, q = c, hh
                    r = TT[t][1]
                    if q == 0:
                        dve.wait_ge(x_in[t], 32)
                    v = h[0:r, t, 256 * q:256 * (q + 1)]
                    m = dve.scalar_tensor_tensor(out=v, in0=bank[0:r, 0:256], scalar=0.5, in1=v,
                                                 op0=ALU.mult, op1=ALU.add)
                m.then_inc(S["pj_dve"], 1)

            def past_keys(i):
                dve.wait_ge(S["kp_ps"], i + 1)
                dve.tensor_copy(kpT[:, i, :], zz[i // 2][:, i % 2, :]).then_inc(S["kp_r"], 1)

            def dt_turn(_):
                dve.wait_ge(S["dt_ps"], 1)
                dve.wait_ge(S["bc_in"], 16 * 5)
                link(dve.memset(sp_x[:, 0:40], 0.0))
                link(dve.tensor_tensor(dt_sb[:, 0:4, :], ms[:, 0:32].rearrange("p (t e) -> p t e", t=4),
                                       bc(rowc[:, 0:8].unsqueeze(1), P, 4, 8), ALU.add))
                dve.tensor_tensor(dt_sb[0:DEC, 4, :], ms[0:DEC, 32:40], rowc[0:DEC, 0:8], ALU.add
                                  ).then_inc(S["dt_raw"], 1)
                dve.wait_ge(S["dt_raw"], 1)
                link(dve.tensor_scalar(sp_p, sp_x, 0.0, None, ALU.max))
                dve.scalar_tensor_tensor(out=sp_e, in0=sp_p, scalar=-2.0, in1=sp_x, op0=ALU.mult, op1=ALU.add
                                         ).then_inc(S["sp_dve"], 1)
                dve.wait_ge(S["sp_act"], 2)
                dve.tensor_scalar(sp_u, sp_e, 1.0, None, ALU.add).then_inc(S["sp_dve"], 1)
                dve.wait_ge(S["sp_dve"], 2)
                dve.wait_ge(S["sp_act"], 3)
                link(dve.tensor_scalar(sp_u, sp_u, -1.0, None, ALU.add))
                link(dve.tensor_scalar(sp_m, sp_u, 0.0, None, ALU.is_equal))
                link(dve.tensor_tensor(sp_l, sp_l, sp_m, ALU.add))
                link(dve.tensor_tensor(sp_u, sp_u, sp_m, ALU.add))
                link(dve.reciprocal(sp_u, sp_u))
                link(dve.tensor_tensor(sp_l, sp_l, sp_e, ALU.mult))
                link(dve.tensor_tensor(sp_l, sp_l, sp_u, ALU.mult))
                link(dve.tensor_tensor(sp_x, sp_l, sp_p, ALU.add))
                dve.tensor_scalar(ls4, sp_x[:, 40:44], -4.0, None, ALU.mult)
                dve.tensor_scalar(ls4n, sp_x[:, 40:44], 4.0, None, ALU.mult)
                dve.scalar_tensor_tensor(out=dA, in0=dt_sb, scalar=-1.0, in1=bc(a_exp.unsqueeze(1), P, NT, 8),
                                         op0=ALU.mult, op1=ALU.mult).then_inc(S["dt_r"], 1)

            def att_scores(u):
                kind, hp, kb = ATT[u]
                z = zz[u % 2]
                dve.wait_ge(S["z_r"], u + 1)
                if kind == "p":
                    dve.tensor_tensor(z[:, :, 0:P], z[:, :, 0:P], bc(att_mask.unsqueeze(1), P, 2, P), ALU.add
                                      ).then_inc(S["masked"], 1)
                    dve.wait_ge(S["masked"], u + 2)
                elif kb == KB:
                    v = z[0:DEC, 0, :].rearrange("p (c q) -> p c q", c=HEADS)
                    dve.tensor_tensor(v, v, bc(att_mask[0:DEC, 0:DEC].unsqueeze(1), DEC, HEADS, DEC), ALU.add
                                      ).then_inc(S["masked"], 1)
                    dve.wait_ge(S["masked"], u + 2)
                if u >= 2:
                    dve.wait_ge(S["o_r"], u - 1)
                    dve.wait_ge(S["s_sum"], u - 1)
                link(dve.tensor_scalar(att_view(att_b[u % 2], u), att_view(z, u), 0.0, None, ALU.max))
                dve.scalar_tensor_tensor(out=att_view(att_a[u % 2], u), in0=att_view(att_b[u % 2], u),
                                         scalar=-2.0, in1=att_view(z, u), op0=ALU.mult, op1=ALU.add
                                         ).then_inc(S["nab_r"], 1)

            def att_soft(u):
                b, ln = att_view(att_b[u % 2], u), att_view(att_a[u % 2], u)
                dve.wait_ge(S["l_r"], u + 1)
                dve.tensor_tensor(b, b, ln, ALU.add).then_inc(S["sp_r"], 1)

            def conv(j):
                src = xp[j % 2]
                ssm = j < XT
                c = j if ssm else j - XT
                kind = "x" if ssm else "r"
                nt = XT if ssm else WT
                base = 12 if ssm else 0
                wait_drained(dve, IDX[(kind, c, 1)])
                link(dve.tensor_copy(src[:, SAMP:SAMP + GAP],
                                     cst[:, base:base + GAP * nt].rearrange("p (k c) -> p k c", k=GAP)[:, :, c]))
                for q, lo in enumerate((SEQ, SAMP + DEC)):
                    v = tails[:, q * 36 + base:q * 36 + base + GAP * nt].rearrange("p (k c) -> p k c", k=GAP)
                    dve.tensor_copy(v[:, :, c], src[:, lo:lo + GAP])
                dst = (xconv if ssm else xc)[:, c, :]
                w0 = PAR["ssm_conv_w" if ssm else "lru_conv_w"] + c
                b0 = PAR["ssm_conv_b" if ssm else "lru_conv_b"] + c
                if j == 0:
                    dve.wait_ge(S["kp_ps"], 4)
                link(dve.tensor_scalar(dst, src[:, 0:TW], cpar[:, w0:w0 + 1], cpar[:, b0:b0 + 1],
                                       ALU.mult, ALU.add))
                for k in range(1, CW):
                    w = w0 + k * nt
                    m = dve.scalar_tensor_tensor(out=dst, in0=src[:, k:k + TW], scalar=cpar[:, w:w + 1], in1=dst,
                                                 op0=ALU.mult, op1=ALU.add)
                    if k < CW - 1:
                        link(m)
                m.then_inc(S["conv_c"], 1)

            def silu(i):
                dve.wait_ge(S["silu_t"], i + 1)
                dve.scalar_tensor_tensor(out=xconv[:, i, :], in0=th[i % 2], scalar=1.0, in1=xconv[:, i, :],
                                         op0=ALU.add, op1=ALU.mult).then_inc(S["silu_r"], 1)

            def ssm_turn(t):
                n = TT[t][1]
                if t == 0:
                    dve.wait_ge(S["s_sum"], NATT)
                dve.wait_ge(S["turn_ps"], t + 1)
                dve.tensor_copy(xs_tok[0:n, t, :], ms[0:n, :]).then_inc(S["turn_r"], 1)

            def lru(c):
                r, i, la, m, gl = lt
                dve.wait_ge(S["lru_tr"], 2 * c + 2)
                dve.scalar_tensor_tensor(out=i, in0=i, scalar=1.0, in1=xc[:, c, :], op0=ALU.add, op1=ALU.mult)
                dve.wait_ge(S["lru_pool"], 4 * c + 4)
                dve.wait_ge(S["lru_ac"], 2 * c + 2)
                dve.scalar_tensor_tensor(out=m, in0=m, scalar=1.0, in1=r, op0=ALU.add, op1=ALU.mult
                                         ).then_inc(S["lru_m2"], 1)

            def lru_scan(c):
                r, i, la, m, gl = lt
                dve.wait_ge(S["lru_mu"], c + 1)
                link(dve.scalar_tensor_tensor(out=i, in0=r, scalar=0.5, in1=i, op0=ALU.mult, op1=ALU.mult))
                h0 = PAR["state_lru_h"] + c
                dve.tensor_tensor_scan(m[:, 0:SEQ], la[:, 0:SEQ], i[:, 0:SEQ], 0.0, ALU.mult, ALU.add)
                link(dve.tensor_tensor_scan(m[:, SAMP:SAMP + DEC], la[:, SAMP:SAMP + DEC], i[:, SAMP:SAMP + DEC],
                                            cpar[:, h0:h0 + 1], ALU.mult, ALU.add))
                for q, last in enumerate((SEQ - 1, SAMP + DEC - 1)):
                    col = 72 + 4 * q + c
                    dve.tensor_copy(tails[:, col:col + 1], m[:, last:last + 1]).then_inc(S["lru_h"], 1)
                dve.wait_ge(S["lru_gt"], c + 1)
                link(dve.scalar_tensor_tensor(out=gl, in0=gl, scalar=1.0, in1=gb[:, c, :],
                                              op0=ALU.add, op1=ALU.mult))
                dve.scalar_tensor_tensor(out=out_mix[1][:, c, 0:SEQ], in0=gl[:, 0:SEQ], scalar=0.5, in1=m[:, 0:SEQ],
                                         op0=ALU.mult, op1=ALU.mult)
                dve.scalar_tensor_tensor(out=out_mix[1][:, c, SEQ:T], in0=gl[:, SAMP:SAMP + DEC], scalar=0.5,
                                         in1=m[:, SAMP:SAMP + DEC], op0=ALU.mult, op1=ALU.mult
                                         ).then_inc(S["ob_r"], 1)

            def ssd_decay(c):
                n = TT[c][1]
                e = at(e_flat, HEADS, n)[0:n]
                dve.wait_ge(S["dec_ps"], c + 1)
                dve.tensor_copy(acs[0:n, :], zb[0:n, 0, 256:264]).then_inc(S["acs_r"], 1)
                dve.wait_ge(S["acs_r"], c + 1)
                if c > 0:
                    dve.wait_ge(S["xdd_r"], c)
                src = za[0:n, :, :].rearrange("p a (b l) -> p (a b) l", l=P) if n == P else \
                    za[0:n, 0, :].rearrange("p (b l) -> p b l", l=n)
                dve.tensor_tensor(e, src, bc(acs[0:n, :].unsqueeze(2), n, HEADS, n), ALU.subtract
                                  ).then_inc(S["d_r"], 1)

            def ssd_exp(c):
                n = TT[c][1]
                e = at(e_flat, HEADS, n)[0:n]
                mm = at(m_flat, HEADS, n)[0:n]
                dve.wait_ge(S["e_r"], c + 1)
                if c > 0:
                    dve.wait_ge(S["mix_ps"], c)
                for g in range(GROUPS):
                    k = dve.tensor_tensor(mm[:, 4 * g:4 * g + 4, :], e[:, 4 * g:4 * g + 4, :],
                                          bc(zb[0:n, 0, g * n:(g + 1) * n].unsqueeze(1), n, 4, n), ALU.mult)
                k.then_inc(S["m_r"], 1)

            def ssd_mix(c):
                n = TT[c][1]
                y3 = y_sb[0:n, :].rearrange("p (e d) -> p e d", e=HEADS)
                t3 = y_off_sb[0:n, :].rearrange("p (e d) -> p e d", e=HEADS)
                dve.wait_ge(S["mix_ps"], c + 1)
                dve.wait_ge(S["ea_r"], c + 1)
                state = hT if c < NT - 1 else hS
                if c > 0:
                    dve.wait_ge(S["yt_ps"], c)
                    link(dve.tensor_tensor(t3, oa[0:n, :].rearrange("p (e d) -> p e d", e=HEADS),
                                           bc(ea[0:n, :].unsqueeze(2), n, HEADS, HD), ALU.mult))
                    dve.tensor_tensor(y_sb[0:n, :], zb[0:n, 1, :], y_off_sb[0:n, :], ALU.add
                                      ).then_inc(S["y0_r"], 1)
                    dve.wait_ge(S["hcd_r"], c)
                    dve.tensor_tensor(state, ms[:, :], state, ALU.add).then_inc(S["h_r"], 1)
                else:
                    dve.tensor_copy(y_sb[0:n, :], zb[0:n, 1, :]).then_inc(S["y0_r"], 1)
                    dve.tensor_copy(state, ms[:, :]).then_inc(S["h_r"], 1)
                dve.wait_ge(S["tz_r"], c + 1)
                dve.scalar_tensor_tensor(out=tz[0:n, :], in0=tz[0:n, :], scalar=1.0, in1=z2[0:n, c, :],
                                         op0=ALU.add, op1=ALU.mult).then_inc(S["y1_r"], 1)

            def ssd_norm(c):
                n = TT[c][1]
                dve.wait_ge(S["ssy_r"], c + 1)
                dve.tensor_scalar(ssy[0:n, :], ssy[0:n, :], 1.0 / 256, EPS, ALU.mult, ALU.add
                                  ).then_inc(S["vy_r"], 1)
                dve.wait_ge(S["sy_r"], c + 1)
                link(dve.reciprocal(rsy[0:n, :], rsy[0:n, :]))
                for g in range(GROUPS):
                    v = y_sb[0:n, g * 256:(g + 1) * 256]
                    k = dve.tensor_scalar(v, v, rsy[0:n, g:g + 1], None, ALU.mult)
                k.then_inc(S["yn_r"], 1)

            def ssd_turn(c):
                o0, n = TT[c]
                dve.wait_ge(S["yt_ps"], c + 1)
                g = PAR["ssm_norm_g"]
                dve.tensor_tensor(out_mix[2][:, :, o0:o0 + n], oa[:, :].rearrange("p (j l) -> p j l", j=WT)[:, :, 0:n],
                                  bc(cpar[:, g:g + 4].unsqueeze(2), P, WT, n), ALU.mult).then_inc(S["oc_r"], 1)

            def ffn_norm(t):
                n = TT[t][1]
                dve.wait_ge(S["ssq_r"], NT + t + 1)
                dve.tensor_scalar(ss2[0:n, t:t + 1], ss2[0:n, t:t + 1], 1.0 / D, EPS, ALU.mult, ALU.add
                                  ).then_inc(S["var_r"], 1)
                dve.wait_ge(S["std_r"], NT + t + 1)
                link(dve.reciprocal(rs2[0:n, t:t + 1], rs2[0:n, t:t + 1]))
                if t == 0:
                    dve.wait_ge(S["gains_in"], 16)
                dve.scalar_tensor_tensor(out=u2[t % 2][0:n, :], in0=h[0:n, t, :], scalar=rs2[0:n, t:t + 1],
                                         in1=g_ffn[0:n, :], op0=ALU.mult, op1=ALU.mult).then_inc(S["u2_r"], 1)

            def ffn_turn(t):
                n = TT[t][1]
                if t == 0:
                    link(dve.memset(lg, 0.0))
                dve.wait_ge(S["lg_ps"], t + 1)
                dve.tensor_tensor(lg[0:n, t, :], ms[0:n, t * 36:(t + 1) * 36], rowc[0:n, 24:60], ALU.add
                                  ).then_inc(S["lg_r"], 1)

            def per(v, k):
                return bc(v.unsqueeze(2), P, NT, k)

            def across(v, k=NT):
                return bc(v.unsqueeze(1), P, k, v.shape[-1])

            def one_hot(ts, dst, values, top, cand, key, keys):
                nt, k = ts.stop - ts.start, values.shape[-1]
                dst, values, cand = (v[:, ts] for v in (dst, values, cand))
                top, key = top[:, ts], key[:, ts]

                def wide(v):
                    return bc(v.unsqueeze(2), P, nt, k)

                link(dve.tensor_reduce(top, values, AXX, ALU.max))
                link(dve.tensor_tensor(cand, values, wide(top), ALU.is_equal))
                link(dve.tensor_tensor(cand, cand, across(keys, nt), ALU.mult))
                link(dve.tensor_reduce(key, cand, AXX, ALU.max))
                link(dve.tensor_tensor(dst, across(keys, nt), wide(key), ALU.is_equal))

            def choose(ts):
                g_lg, e_lg = lg[:, :, 0:NG], lg[:, :, NG:NG + NE]
                dve.wait_ge(S["lg_r"], ts.stop)
                if ts.start == 0:
                    dve.wait_ge(S["ids_r"], 1)
                    dve.tensor_copy(iota_f, iota_i)
                    dve.tensor_copy(tok_f, tok_id)
                    link(dve.tensor_scalar(rev, iota_i, -1.0, float(NE), ALU.mult, ALU.add))
                    link(dve.memset(tok_f[DEC:P, NT - 1:NT], 0.0))
                one_hot(ts, g_hot, g_lg, g_max, g_cand, g_key, rev[:, 0:NG])
                link(dve.tensor_scalar(g_cand[:, ts], g_hot[:, ts], BIG, -BIG, ALU.mult, ALU.add))
                for t in range(ts.start, ts.stop):
                    m = dve.tensor_tensor(e_masked[:, t, :].rearrange("p (g e) -> p g e", g=NG),
                                          e_lg[:, t, :].rearrange("p (g e) -> p g e", g=NG),
                                          bc(g_cand[:, t, :].unsqueeze(2), P, NG, EPG), ALU.add)
                link(m)
                one_hot(ts, e_hot[0], e_masked, v_top[0], e_cand, e_key, rev)
                link(dve.scalar_tensor_tensor(out=e_masked[:, ts], in0=e_hot[0][:, ts], scalar=-BIG,
                                              in1=e_masked[:, ts], op0=ALU.mult, op1=ALU.add))
                one_hot(ts, e_hot[1], e_masked, v_top[1], e_cand, e_key, rev)

                if ts.stop == NT:
                    for s in range(2):
                        m = dve.memset(e_hot[s][DEC:P, NT - 1, :], 0.0)
                    link(m)
                else:
                    link(dve.memset(tile_base[:, 0, :], 0.0))
                link(dve.tensor_tensor(hot_sum[:, ts], e_hot[0][:, ts], e_hot[1][:, ts], ALU.add))
                for t in range(ts.start, ts.stop):
                    m = dve.tensor_tensor(tile_base[:, t + 1, :], tile_base[:, t, :], hot_sum[:, t, :], ALU.add)
                    if t < NT - 1:
                        link(m)
                if ts.stop == NT:
                    m.then_inc(S["route_in"], 1)

            def early(_):
                choose(slice(0, NEARLY))

            def floor_div(dst, src, d):
                link(dve.tensor_scalar(dst, src, 1.0 / d, 0.5 / d - 0.5, ALU.mult, ALU.add))
                link(dve.tensor_scalar(dst, dst, ROUND, None, ALU.add))
                link(dve.tensor_scalar(dst, dst, ROUND, None, ALU.subtract))

            def routing():
                g_lg = lg[:, :, 0:NG]
                choose(slice(NEARLY, NT))
                dve.wait_ge(S["ids_r"], 2)
                dve.tensor_copy(iota_pf, iota_p)
                dve.tensor_tensor(for_exp[:, 0:NT * NG].rearrange("p (t g) -> p t g", t=NT), g_lg, per(g_max, NG),
                                  ALU.subtract)
                dve.tensor_tensor(for_exp[:, NT * NG:], v_top[1], v_top[0], ALU.subtract).then_inc(S["fexp_in"], 1)
                def pick(dst, v):
                    link(dve.tensor_tensor(picked, both_hot, bc(v, P, 2, NT, NE), ALU.mult))
                    link(dve.tensor_reduce(dst, picked, AXX, ALU.add))

                def each(v):
                    return v.unsqueeze(1).unsqueeze(1)

                pick(expert, each(iota_f))
                link(dve.tensor_scalar(side, expert, float(EPAIRS), None, ALU.is_ge))
                link(dve.scalar_tensor_tensor(out=col, in0=side, scalar=-float(EPAIRS), in1=expert,
                                              op0=ALU.mult, op1=ALU.add))
                dve.wait_ge(S["route_ps"], 1)
                pick(rank, ms[:, 0:NT * NE].rearrange("p (t e) -> p t e", t=NT).unsqueeze(1))
                link(dve.tensor_scalar(n_over, ms[:, NT * NE:(NT + 1) * NE], -1.0, None, ALU.add))
                floor_div(n_over, n_over, BLK)
                link(dve.tensor_scalar(n_over, n_over, 0.0, None, ALU.max))
                link(dve.tensor_tensor_scan(over_incl, ones[:, 0:NE], n_over, 0.0, ALU.mult, ALU.add))
                link(dve.tensor_tensor(over_start, over_incl, n_over, ALU.subtract))
                pick(first, each(over_start))
                floor_div(div, rank, BLK)
                link(dve.scalar_tensor_tensor(out=place, in0=div, scalar=-float(BLK), in1=rank,
                                              op0=ALU.mult, op1=ALU.add))
                link(dve.tensor_scalar(is_over, div, 0.0, None, ALU.is_gt))
                link(dve.scalar_tensor_tensor(out=first, in0=first, scalar=-1.0, in1=div, op0=ALU.add, op1=ALU.add))
                link(dve.tensor_scalar(div, first, float(OPAIRS), None, ALU.is_ge))
                link(dve.scalar_tensor_tensor(out=first, in0=div, scalar=-float(OPAIRS), in1=first,
                                              op0=ALU.mult, op1=ALU.add))
                link(dve.tensor_scalar(first, first, float(EPAIRS), None, ALU.add))
                for own, over in ((side, div), (col, first)):
                    link(dve.tensor_tensor(over, over, own, ALU.subtract))
                    link(dve.tensor_tensor(over, over, is_over, ALU.mult))
                    link(dve.tensor_tensor(own, own, over, ALU.add))
                link(dve.scalar_tensor_tensor(out=place, in0=side, scalar=float(BLK), in1=place,
                                              op0=ALU.mult, op1=ALU.add))
                flat = [v.rearrange("p s t -> p (s t)") for v in (place, col)]
                k2 = 2 * NT
                dve.tensor_tensor(place_hot, bc(iota_pf.unsqueeze(1), P, k2, P), bc(flat[0].unsqueeze(2), P, k2, P),
                                  ALU.is_equal)
                link(dve.tensor_tensor(col_hot, bc(iota_f[:, 0:NPC].unsqueeze(1), P, k2, NPC),
                                       bc(flat[1].unsqueeze(2), P, k2, NPC), ALU.is_equal))
                c4 = col_hot.rearrange("p (s t) c -> p s t c", s=2)
                for s_ in range(2):
                    m = dve.tensor_tensor(c4[:, s_], c4[:, s_], per(tok_f, NPC), ALU.mult)
                m.then_inc(S["route_in"], 1)
                dve.scalar_tensor_tensor(out=y_row, in0=flat[1], scalar=float(2 * BLK), in1=flat[0],
                                         op0=ALU.mult, op1=ALU.add)
                dve.wait_ge(S["route_ps"], 2)
                dve.tensor_copy(tab, ms[:, 0:NPC]).then_inc(S["routed"], 1)
                link(dve.tensor_tensor(over_cmp, bc(over_incl.unsqueeze(1), P, OVB, NE),
                                       bc(iota_f[:, 0:OVB].unsqueeze(2), P, OVB, NE), ALU.is_le))
                link(dve.tensor_reduce(eid, over_cmp, AXX, ALU.add))
                dve.tensor_scalar(over_expert, eid, float(NE - 1), None, ALU.min)
                dve.tensor_copy(over_total, over_incl[:, NE - 1:NE]).then_inc(S["routed"], 1)
                dve.wait_ge(S["fexp_r"], 1)
                link(dve.tensor_reduce(p_sel, for_exp[:, 0:NT * NG].rearrange("p (t g) -> p t g", t=NT), AXX,
                                       ALU.add))
                link(dve.tensor_scalar(w_sel[:, 0, :], for_exp[:, NT * NG:], 1.0, None, ALU.add))
                link(dve.tensor_tensor(w_sel[:, 0, :], w_sel[:, 0, :], p_sel, ALU.mult))
                link(dve.reciprocal(w_sel[:, 0, :], w_sel[:, 0, :]))
                link(dve.tensor_tensor(w_sel[:, 1, :], w_sel[:, 0, :], for_exp[:, NT * NG:], ALU.mult))

            def expert_pair(i, turn, before=True):
                dve.wait_ge(S["xt2_ps"], i + 1)
                dve.tensor_copy(xT[:, KD // 2:KD, :], ms[:, :].rearrange("p (k l) -> p k l", k=4)
                                ).then_inc(S["xt2_d"], 1)
                dve.wait_ge(S["gate_th"], i + 1)
                dve.scalar_tensor_tensor(out=gate_t, in0=gate_t, scalar=1.0, in1=za[:, 0, :],
                                         op0=ALU.add, op1=ALU.mult).then_inc(S["gate_mul"], 1)
                dve.wait_ge(S["gate_mul"], i + 1)
                dve.wait_ge(S["up_done"], i + 1)
                dve.scalar_tensor_tensor(out=hid, in0=gate_t, scalar=0.5, in1=za[:, 1, :],
                                         op0=ALU.mult, op1=ALU.mult).then_inc(S["hid_r"], 1)
                dve.wait_ge(S["hidt_ps"], i + 1)
                dve.tensor_copy(hidT, oa[:, :].rearrange("p (k l) -> p k l", k=4)).then_inc(S["hidt_r"], 1)
                dve.wait_ge(S["down_b"], i + 1)
                if before:
                    dve.wait_ge(S["y_out"], i * 16)
                dve.tensor_copy(y_out_sb[:, 512:D], zb[:, 1, :]).then_inc(S["y_b"], 1)

            def final(t):
                n = TT[t][1]
                hv = h[0:n, t, :]
                dve.wait_ge(back_in[t % 2], 32 * (t // 2 + 1))
                link(dve.scalar_tensor_tensor(out=hv, in0=y_back[t % 2][0][0:n, :], scalar=w_sel[0:n, 0, t:t + 1],
                                              in1=hv, op0=ALU.mult, op1=ALU.add))
                dve.scalar_tensor_tensor(out=hv, in0=y_back[t % 2][1][0:n, :], scalar=w_sel[0:n, 1, t:t + 1],
                                         in1=hv, op0=ALU.mult, op1=ALU.add).then_inc(S["hy_r"], 1)

            def final_norm(t):
                n = TT[t][1]
                hv = h[0:n, t, :]
                dve.wait_ge(S["ssq_r"], 2 * NT + t + 1)
                dve.tensor_scalar(ss3[0:n, t:t + 1], ss3[0:n, t:t + 1], 1.0 / D, EPS, ALU.mult, ALU.add
                                  ).then_inc(S["var_r"], 1)
                dve.wait_ge(S["std_r"], 2 * NT + t + 1)
                dve.wait_ge(S["gains_in"], 32)
                link(dve.reciprocal(rs3[0:n, t:t + 1], rs3[0:n, t:t + 1]))
                dve.scalar_tensor_tensor(out=hv, in0=hv, scalar=rs3[0:n, t:t + 1], in1=g_fin[0:n, :],
                                         op0=ALU.mult, op1=ALU.mult).then_inc(S["fin_r"], 1)

            steps = {f.__name__: f for f in (past_keys, dt_turn, att_scores, att_soft, conv, silu, ssm_turn, lru,
                                             lru_scan, ssd_decay, ssd_exp, ssd_mix, ssd_norm, ssd_turn, ffn_norm, ffn_turn,
                                             split, mix_split, merged_split, params, early)}
            x_norm(0)
            x_norm(1)
            x_turn(0)
            for t in range(1, NT):
                if t + 1 < NT:
                    x_norm(t + 1)
                x_turn(t)
                u_split(t - 1)
            u_split(NT - 1)
            for n in range(NITEM + 1):
                for name, args in JOBS.get(n, []):
                    if name in steps:
                        steps[name](*args)
                if n < NITEM:
                    item(n)
            routing()
            expert_pair(0, (0, 0), before=False)
            expert_pair(1, (1, 0))
            with dve.Fori(1, EPAIRS // 2) as ii:
                expert_pair(2 * ii, (0, ii))
                expert_pair(2 * ii + 1, (1, ii))
            dve.wait_ge(S["routed"], 2)
            total = dve.value_load(over_total[0:1, 0:1], min_val=0, max_val=OVB)
            for j in range(OPAIRS):
                with dve.If(total > j):
                    expert_pair(EPAIRS + j, ((EPAIRS + j) % 2, (EPAIRS + j) // 2))
            for t in range(NT):
                final(t)
                if t > 0:
                    final_norm(t - 1)
            final_norm(NT - 1)

        @block.gpsimd
        def _(pool):
            pool.memset(att_s, 0.0).then_inc(S["pool_c"], 1)
            pool.wait_ge(S["pool_c"], 1)
            zeros = att_s[:, 0, 0:P]

            def mask(dst, src, op, fill, step, ch):
                pool.affine_select(out=dst, in_=src, pattern=[[step, P]], compare_op=op, fill=fill, base=0,
                                   channel_multiplier=ch).then_inc(S["consts"], 1)

            mask(ident, zeros, ALU.not_equal, 1.0, -1, 1)
            pool.memset(q2, 0.0).then_inc(S["q_zero"], 1)
            lo = 0
            for name, k in PAR_ROWS:
                if name == "g_mix":
                    lo += k
                    continue
                src = a[name][0]
                if len(src.shape) == 1:
                    src = src.rearrange("(r p) -> r p", p=P)
                elif len(src.shape) == 2:
                    src = src.rearrange("k (r p) -> (k r) p", p=P)
                pool.dma_start(st_a[lo:lo + k, :], src).then_inc(S["par_in"], 16)
                lo += k
            pool.dma_start(st_b[0:12, :], a["state_lru_conv"][0, 0].rearrange("k (r p) -> (k r) p", p=P)
                          ).then_inc(S["par_in"], 16)
            pool.dma_start(st_b[12:36, :], a["state_ssm_conv"][0, 0].rearrange("k (r p) -> (k r) p", p=P)
                          ).then_inc(S["par_in"], 16)
            for lo, n, name in ((0, 8, "ssm_dt_bias"), (8, 8, "ssm_a_log"), (16, 8, "ssm_d"),
                                (24, 4, "b_router_group"), (28, 32, "b_router_expert")):
                pool.dma_start(rowc[:, lo:lo + n], a[name][0:1, :].partition_broadcast(P)
                              ).then_inc(S["bc_in"], 16)
            pool.dma_start(w_dt, a["w_in"][0, :, 4096:4104].rearrange("(k p) n -> p k n", p=P)
                           ).then_inc(S["par_in"], 16)
            pool.memset(ones, 1.0)
            pool.memset(neg_ones, -1.0).then_inc(S["pool_c"], 1)
            pool.wait_ge(S["pool_c"], 2)
            mask(u_incl, ones, ALU.is_ge, 0.0, 1, -1)
            mask(u_strict, ones, ALU.is_gt, 0.0, 1, -1)
            mask(neg_l, neg_ones, ALU.is_ge, 0.0, -1, 1)
            mask(att_mask, zeros, ALU.is_gt, NEG, 1, -1)
            mask(ssd_mask, zeros, ALU.is_ge, NEG, 1, -1)
            pool.memset(xp[0], 0.0)
            pool.memset(xp[1], 0.0).then_inc(S["consts"], 1)
            pool.wait_ge(S["consts"], 7)
            pool.sem_inc(S["masked"], 1)
            pool.iota(iota_i, [[1, NE]], base=0, channel_multiplier=0)
            pool.iota(tok_id, [[P, NT]], base=0, channel_multiplier=1).then_inc(S["ids_r"], 1)
            pool.dma_start(yd[NE * BLK:(NE + OVB) * BLK, :].rearrange("(c p) d -> p c d", p=P),
                           att_s[:, :, :].rearrange("p a b -> p (a b)").unsqueeze(1).to_broadcast([P, OPAIRS, D])
                           ).then_inc(S["side_dma"], 16)
            for lo, k, name in ((0, NG, "w_router_group"), (NG, NE, "w_router_expert")):
                pool.dma_start(w_r[:, :, lo:lo + k], a[name][0].rearrange("(k p) n -> p k n", p=P)
                               ).then_inc(S["side_dma"], 16)

            pool.wait_ge(S["xt_ps"], NT)
            pool.memset(gb[:, :, SEQ:TW], 0.0).then_inc(S["gb_zero"], 1)

            def att_after(u):
                kind, hp, kb = ATT[u]
                s, b = att_s, att_b[u % 2]
                pool.wait_ge(S["zw_r"], u + 1)
                if u == 0:
                    pool.wait_ge(S["side_dma"], 48)
                else:
                    pool.wait_ge(S["s_sum"], u)
                if kind == "p":
                    n = SEQ - kb * P
                    if kb == KB - 1:
                        pool.tensor_copy(s[:, :, 0:n], b[:, :, 0:n]).then_inc(S["s_sum"], 1)
                    elif kb > 0:
                        pool.tensor_tensor(b[:, :, P:n], b[:, :, P:n], s[:, :, 0:n - P], ALU.add
                                           ).then_inc(S["pool_c"], 1)
                        cnt[0] += 1
                        pool.wait_ge(S["pool_c"], cnt[0])
                        pool.tensor_copy(s[:, :, 0:n], b[:, :, 0:n]).then_inc(S["s_sum"], 1)
                    else:
                        pool.memset(s[:, 0, :], 0.0).then_inc(S["s_sum"], 1)
                else:
                    n = P if kb < KB else DEC
                    pool.tensor_tensor(s[0:n, 0, :], s[0:n, 0, :], b[0:n, 0, :], ALU.add).then_inc(S["s_sum"], 1)

            cnt = [2]

            def lru_weights():
                pool.wait_ge(S["s_sum"], NATT)
                pool.wait_ge(S["conv_c"], XT + WT)
                pool.wait_ge(S["o_out"], PAIRS + 1)
                pool.memset(lru_w, 0.0).then_inc(S["lruw_z"], 1)
                pool.wait_ge(S["lruw_z"], 1)
                for g, name in enumerate(("lru_w_a", "lru_w_x")):
                    blocks = a[name][0].rearrange("(c q) i j -> q i c j", q=2)
                    for q in range(2):
                        half = slice(q * HD, (q + 1) * HD)
                        pool.dma_start(lru_w[half, g, :, half], blocks[q]).then_inc(S["lruw_in"], 16)
                pool.dma_start(ss_in, a["state_ssm_h"][0, 0].rearrange("(j q) p n -> (q p) j n", q=2)
                               ).then_inc(S["lruw_in"], 16)

            def lru(c):
                r, i, la, m, gl = lt
                g = gb[:, c, :]
                if c > 0:
                    pool.wait_ge(S["ob_r"], c)
                else:
                    pool.wait_ge(S["gb_zero"], 1)
                pool.tensor_tensor(gl, g, g, ALU.mult).then_inc(S["lru_pool"], 1)
                pool.wait_ge(S["lru_pool"], 4 * c + 1)
                pool.tensor_scalar(gl, gl, GELU_A, 1.0, ALU.mult, ALU.add).then_inc(S["lru_pool"], 1)
                pool.wait_ge(S["lru_pool"], 4 * c + 2)
                pool.tensor_tensor(gl, gl, g, ALU.mult).then_inc(S["lru_pool"], 1)
                pool.wait_ge(S["lru_ac"], 2 * c + 1)
                pool.tensor_tensor(m, la, la, ALU.mult).then_inc(S["lru_pool"], 1)

            def decays(c):
                n = TT[c][1]
                td = at(td_flat, HEADS, n)[0:n]
                if c == 0:
                    pool.wait_ge(S["dt_r"], 1)
                    pool.wait_ge(S["ob_r"], WT)
                pool.tensor_tensor(td, bc(u_incl[0:n, 0:n].unsqueeze(1), n, HEADS, n),
                                   bc(dA[0:n, c, :].unsqueeze(2), n, HEADS, n), ALU.mult).then_inc(S["td_r"], 1)

            def ssd_decay(c):
                n = TT[c][1]
                e = at(e_flat, HEADS, n)[0:n]
                if c == 0:
                    decays(c)
                pool.wait_ge(S["d_r"], c + 1)
                pool.tensor_tensor(e, e, bc(ssd_mask[0:n, 0:n].unsqueeze(1), n, HEADS, n), ALU.add
                                   ).then_inc(S["em_r"], 1)
                if c == 0:
                    pool.wait_ge(S["turn_r"], 2 * NT)
                if c > 0:
                    pool.wait_ge(S["mix_ps"], c)
                xs3 = xs_tok[0:n, c, :].rearrange("p (e d) -> p e d", e=HEADS)
                pool.tensor_tensor(xdt[0:n], xs3, bc(dt_sb[0:n, c, :].unsqueeze(2), n, HEADS, HD), ALU.mult
                                   ).then_inc(S["xdt_r"], 1)

            def ssd_exp(c):
                n = TT[c][1]
                e = at(e_flat, HEADS, n)[0:n]
                pool.wait_ge(S["xdt_r"], c + 1)
                pool.wait_ge(S["e_r"], c + 1)
                pool.tensor_tensor(xdd[0:n], xdt[0:n], bc(e[:, :, n - 1:n], n, HEADS, HD), ALU.mult
                                   ).then_inc(S["xdd_r"], 1)

            def ssd_mix(c):
                n = TT[c][1]
                state = hT if c < NT - 1 else hS
                pool.wait_ge(S["mix_ps"], c + 1)
                if c > 0:
                    pool.wait_ge(S["ea_r"], c + 1)
                    s3 = state.rearrange("p (e d) -> p e d", e=HEADS)
                    pool.tensor_tensor(s3, s3, bc(cd.unsqueeze(2), P, HEADS, HD), ALU.mult).then_inc(S["hcd_r"], 1)
                xs3 = xs_tok[0:n, c, :].rearrange("p (e d) -> p e d", e=HEADS)
                pool.tensor_tensor(xs3, xs3, bc(rowc[0:n, 16:24].unsqueeze(2), n, HEADS, HD), ALU.mult
                                   ).then_inc(S["y2_r"], 1)
                pool.wait_ge(S["y2_r"], 2 * c + 1)
                pool.wait_ge(S["y0_r"], c + 1)
                pool.tensor_tensor(y_sb[0:n, :], y_sb[0:n, :], xs_tok[0:n, c, :], ALU.add).then_inc(S["y2_r"], 1)
                pool.wait_ge(S["y2_r"], 2 * c + 2)
                pool.wait_ge(S["y1_r"], c + 1)
                pool.tensor_tensor(y_sb[0:n, :], y_sb[0:n, :], tz[0:n, :], ALU.mult).then_inc(S["yg_r"], 1)
                if c + 1 < NT:
                    decays(c + 1)

            def item(n):
                it = ITEMS[n]
                if it[0] == "b" and it[5] > 0:
                    _, c, hh = it[:3]
                    k = (n - MIX1) // 2
                    wait_drained(pool, n)
                    v = merged[c // 2][:, c % 2, hh * HALF:(hh + 1) * HALF]
                    pool.tensor_tensor(v, v, gtmp[k % 2], ALU.add).then_inc(S["gm_r"], 1)

            def ffn_norm(t):
                n = TT[t][1]
                if t == 0:
                    pool.wait_ge(S["gm_r"], 4 * KD)
                    pool.wait_ge(S["so_out"], 32)
                    pool.dma_start(g_ffn, a["g_ffn"][0:1, :].partition_broadcast(P)).then_inc(S["gains_in"], 16)

            steps = {f.__name__: f for f in (att_after, lru, ssd_decay, ssd_exp, ssd_mix, ffn_norm)}
            for n in range(NITEM + 1):
                if n == MIX1:
                    lru_weights()
                for name, args in JOBS.get(n, []):
                    if name in steps:
                        steps[name](*args)
                if n < NITEM:
                    item(n)
            pool.wait_ge(S["lg_ps"], NT)
            pool.dma_start(g_fin, a["g_final"].rearrange("(o d) -> o d", o=1).partition_broadcast(P)
                           ).then_inc(S["gains_in"], 16)
            pool.iota(iota_p, [[1, P]], base=0, channel_multiplier=0).then_inc(S["ids_r"], 1)
            pool.wait_ge(S["routed"], 1)
            for s in range(2):
                pool.wait_ge(u2_out[s], 16 * ((NT + 1 - s) // 2))

            def expert_pair(i, turn, before=True):
                if before:
                    pool.wait_ge(S["xg_in"], i * 16)
                    pool.wait_ge(S["xt2_ps"], i)
                pool.tensor_copy(idx_now, tab[:, bass.ds(i, 1)]).then_inc(S["idx_r"], 1)
                pool.wait_ge(S["idx_r"], i + 1)
                pool.sem_inc(S["idx_seen"], 1)
                pool.indirect_dma_start(out=xg, out_offset=None, in_=u2d, in_offset=bass.IndirectOffsetOnAxis(
                    ap=idx_now, axis=0)).then_inc(S["xg_in"], 16)

            expert_pair(0, (0, 0), before=False)
            expert_pair(1, (1, 0))
            with pool.Fori(1, EPAIRS // 2) as ii:
                expert_pair(2 * ii, (0, ii))
                expert_pair(2 * ii + 1, (1, ii))
            pool.wait_ge(S["routed"], 2)
            total = pool.value_load(over_total[0:1, 0:1], min_val=0, max_val=OVB)
            for j in range(OPAIRS):
                with pool.If(total > j):
                    expert_pair(EPAIRS + j, ((EPAIRS + j) % 2, (EPAIRS + j) // 2))
            pool.wait_ge(S["experts_done"], 1)
            for t, (o0, n) in enumerate(TT):
                if t >= 2:
                    pool.wait_ge(S["ssq_r"], 2 * NT + t - 1)
                for s in range(2):
                    c = s * NT + t
                    pool.indirect_dma_start(out=y_back[t % 2][s][0:n, :], out_offset=None, in_=yd,
                                            in_offset=bass.IndirectOffsetOnAxis(ap=y_row[0:n, c:c + 1], axis=0)
                                            ).then_inc(back_in[t % 2], 16)


OUTS = [("y_p", (1, SEQ, D)), ("y_s", (1, DEC, D)),
        ("k_p", (1, 1, SEQ, HEADS, HD)), ("v_p", (1, 1, SEQ, HEADS, HD)),
        ("lru_conv_p", (1, 1, GAP, W)), ("lru_h_p", (1, 1, W)), ("ssm_conv_p", (1, 1, GAP, XBC)),
        ("ssm_h_p", (1, 1, HEADS, HD, STATE)),
        ("k_s", (1, 1, DEC, HEADS, HD)), ("v_s", (1, 1, DEC, HEADS, HD)),
        ("lru_conv_s", (1, 1, GAP, W)), ("lru_h_s", (1, 1, W)), ("ssm_conv_s", (1, 1, GAP, XBC)),
        ("ssm_h_s", (1, 1, HEADS, HD, STATE))]


def kernel(**inputs):
    import numpy as np
    from concourse import bacc
    from concourse.bass_utils import run_bass_kernel_spmd

    nc = bacc.Bacc("TRN2", target_bir_lowering=False, num_devices=1)
    arrays, a, o = {}, {}, {}
    for name, x in inputs.items():
        arrays["in_" + name] = np.ascontiguousarray(x)
        a[name] = nc.dram_tensor("in_" + name, arrays["in_" + name].shape, F32, kind="ExternalInput").ap()
    for name, shape in OUTS:
        o[name] = nc.dram_tensor("out_" + name, shape, F32, kind="ExternalOutput").ap()
    trunk_and_experts(nc, a, o)
    r = run_bass_kernel_spmd(nc, [arrays], core_ids=[0])
    return tuple(r.results[0]["out_" + name] for name, _ in OUTS)
```
